# Optimizing a Trainium2 kernel written in Bass

```python
import jax, jax.numpy as jnp
from jax import lax
import numpy as np

D_MODEL = 1024
BATCH = 1
SEQ = 512
DEPTH = 1

HEAD_DIM = 64
N_HEADS_SB = 8
N_HEADS_DSA = 8
N_HEADS_IDX = 8
D_IDX = 64
TOPK_MAX = 256
D_FF = 2816
Q_BLOCK = 128
N_MOD = 9
RMS_EPS = 1e-6

W_SB = N_HEADS_SB * HEAD_DIM
W_DSA = N_HEADS_DSA * HEAD_DIM
IN_SIZES = (W_SB, W_SB, W_SB,
            W_DSA, HEAD_DIM, HEAD_DIM,
            N_HEADS_IDX * D_IDX, D_IDX,
            N_HEADS_IDX)
D_IN = int(sum(IN_SIZES))
SPLIT_POINTS = tuple(int(v) for v in np.cumsum(IN_SIZES)[:-1])

kernel_name = "hybrid_stickbreaking_dsa_macaron_block"

def rmsnorm(x, g):
    xf = x.astype(jnp.float32)
    y = xf * lax.rsqrt(jnp.mean(xf * xf, axis=-1, keepdims=True) + RMS_EPS)
    return (y * g.astype(jnp.float32)).astype(x.dtype)

def modulate(x, shift, scale):
    return x * (1.0 + scale[:, None, :]) + shift[:, None, :]

def swiglu(x, w1, w3, w2):
    return (jax.nn.silu(x @ w1) * (x @ w3)) @ w2

def to_blocks(a):
    b, s = a.shape[:2]
    return a.reshape((b, s // Q_BLOCK, Q_BLOCK) + a.shape[2:]).swapaxes(0, 1)

def from_blocks(a):
    a = a.swapaxes(0, 1)
    return a.reshape((a.shape[0], a.shape[1] * a.shape[2]) + a.shape[3:])

def stick_breaking_attention(q, k, v):
    S, dh = q.shape[1], q.shape[-1]
    scale = dh ** -0.5
    kpos = jnp.arange(S)
    nb = S // Q_BLOCK

    def block(args):
        q_blk, i = args
        qpos = i * Q_BLOCK + jnp.arange(Q_BLOCK)
        z = jnp.einsum('bqhd,bshd->bhqs', q_blk, k).astype(jnp.float32) * scale
        strict = (kpos[None, :] < qpos[:, None])[None, None]
        log1m = jnp.where(strict, jax.nn.log_sigmoid(-z), 0.0)
        after = lax.cumsum(log1m, axis=3, reverse=True) - log1m
        a = jnp.where(strict, jnp.exp(jax.nn.log_sigmoid(z) + after), 0.0)
        return jnp.einsum('bhqs,bshd->bqhd', a.astype(v.dtype), v)

    out = lax.map(block, (to_blocks(q), jnp.arange(nb)))
    return from_blocks(out)

def dsa_attention(q, k, v, q_idx, k_idx, w_idx):
    B, S, H, dh = q.shape
    topk = min(TOPK_MAX, S // 4)
    scale = dh ** -0.5
    idx_scale = (D_IDX ** -0.5) * (N_HEADS_IDX ** -0.5)
    slopes = jnp.exp2(-8.0 * jnp.arange(1, H + 1, dtype=jnp.float32) / H)
    kpos = jnp.arange(S)
    bidx = jnp.arange(B)[:, None, None]
    nb = S // Q_BLOCK

    def block(args):
        q_blk, qi_blk, wi_blk, i = args
        qpos = i * Q_BLOCK + jnp.arange(Q_BLOCK)
        causal = (kpos[None, :] <= qpos[:, None])[None]
        rel = jax.nn.relu(jnp.einsum('bqhd,bsd->bqhs', qi_blk, k_idx).astype(jnp.float32))
        score = jnp.einsum('bqhs,bqh->bqs', rel, wi_blk.astype(jnp.float32)) * idx_scale
        score = jnp.where(causal, score, -jnp.inf)
        top_val, sel = lax.top_k(score, topk)
        valid = top_val > -jnp.inf
        k_sel = k[bidx, sel]
        v_sel = v[bidx, sel]
        logits = jnp.einsum('bqhd,bqkd->bhqk', q_blk, k_sel).astype(jnp.float32) * scale
        dist = (qpos[None, :, None] - sel).astype(jnp.float32)
        logits = logits - slopes[None, :, None, None] * dist[:, None]
        logits = jnp.where(valid[:, None], logits, -jnp.inf)
        p = jax.nn.softmax(logits, axis=-1)
        return jnp.einsum('bhqk,bqkd->bqhd', p.astype(v.dtype), v_sel)

    out = lax.map(block, (to_blocks(q), to_blocks(q_idx), to_blocks(w_idx), jnp.arange(nb)))
    return from_blocks(out)

def setup_inputs(seed: int = 0) -> dict:
    key = jax.random.key(seed)
    ks = jax.random.split(key, 24)
    f32 = jnp.float32

    def dense(k, shape, fan_in, mult=1.0):
        return jax.random.normal(k, shape, f32) * (mult * fan_in ** -0.5)

    def gain(k, shape):
        return 1.0 + 0.05 * jax.random.normal(k, shape, f32)

    L, D = DEPTH, D_MODEL
    return {
        "x": jax.random.normal(ks[0], (BATCH, SEQ, D), f32),
        "c": jax.random.normal(ks[1], (BATCH, D), f32),
        "w_ada": dense(ks[2], (L, D, N_MOD * D), D, 0.5),
        "b_ada": 0.02 * jax.random.normal(ks[3], (L, N_MOD * D), f32),
        "g_ffn1": gain(ks[4], (L, D)),
        "w1_ffn1": dense(ks[5], (L, D, D_FF), D),
        "w3_ffn1": dense(ks[6], (L, D, D_FF), D),
        "w2_ffn1": dense(ks[7], (L, D_FF, D), D_FF),
        "g_mix": gain(ks[8], (L, D)),
        "w_in": dense(ks[9], (L, D, D_IN), D),
        "g_q_dsa": gain(ks[10], (L, HEAD_DIM)),
        "g_k_dsa": gain(ks[11], (L, HEAD_DIM)),
        "w_proj_sb": dense(ks[12], (L, W_SB, D), W_SB),
        "w_proj_dsa": dense(ks[13], (L, W_DSA, D), W_DSA),
        "w_gate": dense(ks[14], (L, D, 2 * D), D),
        "b_gate": 0.02 * jax.random.normal(ks[15], (L, 2 * D), f32),
        "w_out": dense(ks[16], (L, D, D), D),
        "g_ffn2": gain(ks[17], (L, D)),
        "w1_ffn2": dense(ks[18], (L, D, D_FF), D),
        "w3_ffn2": dense(ks[19], (L, D, D_FF), D),
        "w2_ffn2": dense(ks[20], (L, D_FF, D), D_FF),
    }

def reference(x, c, w_ada, b_ada, g_ffn1, w1_ffn1, w3_ffn1, w2_ffn1, g_mix, w_in,
              g_q_dsa, g_k_dsa, w_proj_sb, w_proj_dsa, w_gate, b_gate, w_out,
              g_ffn2, w1_ffn2, w3_ffn2, w2_ffn2):
    B, S, D = x.shape
    sc = jax.nn.silu(c)
    h = x
    for l in range(DEPTH):
        mod = sc @ w_ada[l] + b_ada[l]
        sh1, sc1, gt1, sh2, sc2, gt2, sh3, sc3, gt3 = jnp.split(mod, N_MOD, axis=-1)

        n1 = modulate(rmsnorm(h, g_ffn1[l]), sh1, sc1)
        h = h + 0.5 * gt1[:, None, :] * swiglu(n1, w1_ffn1[l], w3_ffn1[l], w2_ffn1[l])

        n = modulate(rmsnorm(h, g_mix[l]), sh2, sc2)
        proj = n @ w_in[l]
        q_sb, k_sb, v_sb, q_d, k_d, v_d, q_i, k_i, w_i = jnp.split(proj, SPLIT_POINTS, axis=-1)

        heads = lambda t, nh: t.reshape(B, S, nh, -1)
        y_sb = stick_breaking_attention(heads(q_sb, N_HEADS_SB), heads(k_sb, N_HEADS_SB),
                                        heads(v_sb, N_HEADS_SB))
        q_d = rmsnorm(heads(q_d, N_HEADS_DSA), g_q_dsa[l])
        k_d = rmsnorm(k_d, g_k_dsa[l])
        y_d = dsa_attention(q_d, k_d, v_d, heads(q_i, N_HEADS_IDX), k_i, w_i)

        y_sb = y_sb.reshape(B, S, W_SB) @ w_proj_sb[l]
        y_d = y_d.reshape(B, S, W_DSA) @ w_proj_dsa[l]
        gates = jax.nn.sigmoid(n @ w_gate[l] + b_gate[l])
        g_sb, g_d = jnp.split(gates, 2, axis=-1)
        mixed = (g_sb * y_sb + g_d * y_d) @ w_out[l]
        h = h + gt2[:, None, :] * mixed

        n3 = modulate(rmsnorm(h, g_ffn2[l]), sh3, sc3)
        h = h + 0.5 * gt3[:, None, :] * swiglu(n3, w1_ffn2[l], w3_ffn2[l], w2_ffn2[l])
    return h


_drawn_inputs = setup_inputs


def setup_inputs(seed=0):
    import zlib

    import numpy as np

    out = dict(_drawn_inputs(seed))
    spreads = {}
    factors = {'g_ffn1': 5.166,
     'g_mix': 2.901,
     'g_q_dsa': 8.0,
     'g_k_dsa': 8.0,
     'b_gate': 34.906,
     'g_ffn2': 7.79}
    for name, (base, spread) in spreads.items():
        noise = np.random.default_rng([zlib.crc32(name.encode()), seed]).standard_normal(out[name].shape)
        drawn = base * np.exp(spread * noise) if base else spread * noise
        out[name] = __import__('jax').numpy.asarray(drawn.astype(out[name].dtype))
    for name, factor in factors.items():
        out[name] = (out[name] * factor).astype(out[name].dtype)
    return out
```

```python
from contextlib import ExitStack

import concourse.bass as bass
from concourse import mybir

F32 = mybir.dt.float32
F32R = mybir.dt.float32r
BF16 = mybir.dt.bfloat16
ACT = mybir.ActivationFunctionType
ALU = mybir.AluOpType
AX = mybir.AxisListType

P = 128
D = 1024
S = 512
KD = D // P
NB = S // P
F = 2816
KF = F // P
HD = 64
NH = 8
TOPK = 128
EPS = 1e-6
UP_PAIRS = KF // 2
FFN_UNITS = 3 * UP_PAIRS
SLOT = 2112
NEG = -(2.0 ** 100)
NOT_CAUSAL = -1e38
TAKEN = -3e38

Q_SB, K_SB, V_SB, Q_D, K_D, V_D, Q_I, K_I, W_I, W_END = 0, 512, 1024, 1536, 2048, 2112, 2176, 2688, 2752, 2760
XC = 2 * HD + HD + HD + NH

U_X = FFN_UNITS
U_QD = U_X + 1
U_QI = U_QD + 2
U_QSB = U_QI + 2
U_KSB = U_QSB + 2
U_VSB = U_KSB + 2
U_GATE = U_VSB + 2
U_PROJ = U_GATE + 8
U_OUT = U_PROJ + 4
U_FFN2 = U_OUT + 4
U_END = U_FFN2 + FFN_UNITS

C_BADA, C_G, C_BGATE, C_C, C_GQ, C_GK, C_END = 0, 72, 96, 112, 120, 121, 122
HEAD_COLS = 2 * D
GROUPS = (9 * D - HEAD_COLS) // 256
LOOP_GROUPS = 2 * UP_PAIRS

B_Z, B_Y, B_F, B_LG, B_PT, B_O = 0, 3, 4, 5, 6, 7
W2_ORDER = [4, 5, 6, 7, 0, 1, 2, 3]
ORDERS = [list(range(KD)), W2_ORDER, list(range(KD)), W2_ORDER]

BLK = {0: 0, 1: 512, 3: 896, 2: 1024}
ZW = 1280
IDX = [(i, h) for i in (1, 2, 3) for h in range(NH)]
S_OFF = {1: 0, 2: 256, 3: 640}
R_OFF = {0: 0, 1: 128, 2: 384, 3: 768}
ROUNDS = TOPK // 8


def tiles_of(u):
    if u < U_X or u >= U_FFN2:
        n = u if u < U_X else u - U_FFN2
        return 2 if n < 2 * UP_PAIRS else KD if n == FFN_UNITS - 1 else 1
    return {U_X: 3, U_QD: 1, U_QD + 1: NB, U_VSB: 1, U_VSB + 1: NB}.get(u, 4 if U_PROJ <= u < U_OUT else 2)


def before(u):
    return 1 + sum(tiles_of(v) for v in range(u))


def tile_at(u, t):
    return before(u) + t + 1


def layer_kernel(nc, x, c, w_ada, b_ada, g_ffn1, w1_ffn1, w3_ffn1, w2_ffn1, g_mix, w_in, g_q_dsa, g_k_dsa,
                 w_proj_sb, w_proj_dsa, w_gate, b_gate, w_out, g_ffn2, w1_ffn2, w3_ffn2, w2_ffn2, out):
    ctx = ExitStack()
    with ctx:
        place = [16640]

        def sb(name, shape, dt=F32, at=None):
            n = 1
            for v in shape[1:]:
                n *= v
            n *= 2 if dt == BF16 else 4
            off = place[0] if at is None else at
            if at is None:
                place[0] += -(-n // 32) * 32
                assert place[0] <= 229344, (name, place[0])
            return nc.alloc_sbuf_tensor_at(name, shape, dt, offset=off)

        def sem(name):
            return ctx.enter_context(nc.semaphore(name))

        h = sb("h", [P, KD, S])
        n_hi = sb("n_hi", [P, KD, S], F32R)
        n_lo = sb("n_lo", [P, KD, S], F32R)
        raw = [sb(f"raw{i}", [P, SLOT]) for i in range(2)]
        w_hi = [sb(f"w_hi{i}", [P, SLOT], F32R) for i in range(2)]
        w_lo = [sb(f"w_lo{i}", [P, SLOT], F32R) for i in range(2)]
        ident = sb("ident", [P, P])
        ident_bf = sb("ident_bf", [P, P], BF16)
        strict_bf = sb("strict_bf", [P, P], BF16)
        neg_tri = sb("neg_tri", [P, P])
        neg_ones = sb("neg_ones", [P, P])
        ones = sb("ones", [P, P])
        rows = sb("rows", [C_END, P])
        cols = sb("cols", [P, C_END])
        mod = sb("mod", [P, 9 * KD])
        nscale = sb("nscale", [P, 3, KD])
        half_gate = sb("half_gate", [P, 2, KD])
        sc = sb("sc", [P, KD])
        eps = sb("eps", [P, 1])
        qscale = sb("qscale", [P, NB])
        wi = sb("wi", [P, NB, NH])
        kr = sb("kr", [P, NB])
        qr = sb("qr", [P, NB * NH])
        best = sb("best", [P, 8])
        negmax = sb("negmax", [P, NB * NH])
        psum_p = sb("psum_p", [P, NB * NH])
        pinv = sb("pinv", [P, NB * NH])
        tmp_at = place[0]
        nt = sb("nt", [P, 2, S])
        sq = sb("sq", [P, S])
        ssq = sb("ssq", [P, S])
        outb = sb("outb", [P, 4, NB, P], at=tmp_at)
        lgb = sb("lgb", [P, 2, S], at=tmp_at)
        pb = sb("pb", [P, 2, S], at=tmp_at + 2 * S * 4)
        arena = place[0]
        mid_hi = sb("mid_hi", [P, KF, S], F32R)
        mid_lo = sb("mid_lo", [P, KF, S], F32R)
        ada_ring = sb("ada_ring", [P, 2, 4 * 256])
        ada_acc = sb("ada_acc", [P, 256])
        ada_rest = sb("ada_rest", [P, GROUPS - LOOP_GROUPS, 256], at=arena + 32768)
        slab = sb("slab", [P, KD, HEAD_COLS], at=arena)
        head_acc = sb("head_acc", [P, HEAD_COLS], at=arena + 65536)
        xin = sb("xin", [P, NB, D], at=arena + 73728)
        gates = sb("gates", [P, 16, S], at=arena)
        qiT = sb("qiT", [P, 4, S], at=arena)
        kiT = sb("kiT", [P, S], at=arena + 8192)
        relu = sb("relu", [P, 2, S], at=arena + 10240)
        qn = sb("qn", [P, 2, S], at=arena + 16384)
        kn = sb("kn", [P, NB, 2, HD], at=arena + 20480)
        dist = sb("dist", [P, S], at=arena + 26112)
        score = sb("score", [P, 1152], at=arena + 28160)
        qsbT = sb("qsbT", [P, 4, S], at=arena + 32768)
        ksbT = sb("ksbT", [P, 4, S], at=arena + 40960)
        ysb_hi = sb("ysb_hi", [P, 4, S], F32R, at=arena + 32768)
        ysb_lo = sb("ysb_lo", [P, 4, S], F32R, at=arena + 40960)
        vsb = sb("vsb", [P, NB, S], at=arena + 49152)
        qdT = sb("qdT", [P, 4, S], at=arena + 57344)
        yd_hi = sb("yd_hi", [P, 4, S], F32R, at=arena + 49152)
        yd_lo = sb("yd_lo", [P, 4, S], F32R, at=arena + 57344)
        kdT = sb("kdT", [P, S], at=arena + 65536)
        vd = sb("vd", [P, NB, HD], at=arena + 67584)
        R = sb("R", [P, ZW], at=arena + 68608)
        sp_a = sb("sp_a", [P, ZW], at=arena + 73728)
        sqt = sb("sqt", [P, S], at=arena + 73728)
        ydT = sb("ydT", [P, 4, S], at=arena + 78848)
        pT = sb("pT", [P, 2, S], at=arena + 87040)
        ydtok = sb("ydtok", [P, S], at=arena + 91136)
        assert arena + 93184 <= place[0] - 1024 - 4096

        ps = ctx.enter_context(nc.psum_tensor("ps", [P, 8, S], F32))
        psf = ps[:, :, :].rearrange("p b n -> p (b n)")

        rows_in, rows_t, cols_done, silu_c = sem("rows_in"), sem("rows_t"), sem("cols_done"), sem("silu_c")
        coef_q = sem("coef_q")
        consts = sem("consts")
        slab_in = [sem(f"slab_in{k}") for k in range(KD)]
        x_in = [sem(f"x_in{j}") for j in range(NB)]
        x_t = sem("x_t")
        head_mac, head_mm = sem("head_mac"), sem("head_mm")
        ada_in = [sem(f"ada_in{r}") for r in range(2)]
        ada_mac = sem("ada_mac")
        ada_mm = sem("ada_mm")
        mod_done = sem("mod_done")
        coef = sem("coef")
        raw_in = [sem(f"raw_in{i}") for i in range(2)]
        hi_done, lo_done = sem("hi_done"), sem("lo_done")
        tiles = sem("tiles")
        silu_done, mul_done = sem("silu_done"), sem("mul_done")
        mid_hi_done, mid_lo_done = sem("mid_hi_done"), sem("mid_lo_done")
        h_done = sem("h_done")
        sq_done, ssq_done = sem("sq_done"), sem("ssq_done")
        sum_done, std_done, rstd_done = sem("sum_done"), sem("std_done"), sem("rstd_done")
        nt_done, nf_done, n_hi_done, n_lo_done = sem("nt_done"), sem("nf_done"), sem("n_hi_done"), sem("n_lo_done")
        ki_done, vw_done = sem("ki_done"), sem("vw_done")
        ksq_done, kss_done, kstd_done, kr_done, kn_done = (sem(f"k{v}_done") for v in ("sq", "ss", "std", "r", "n"))
        kn_t, kdT_done = sem("kn_t"), sem("kdT_done")
        qsq_done, qss_done, qstd_done, qr_done, qn_done = (sem(f"q{v}_done") for v in ("sq", "ss", "std", "r", "n"))
        qn_t, qdT_done = sem("qn_t"), sem("qdT_done")
        qi_done = sem("qi_done")
        idx_mm, relu_done, score_add = sem("idx_mm"), sem("relu_done"), sem("score_add")
        causal = sem("causal")
        top = sem("top")
        r_step, r_done = sem("r_step"), sem("r_done")
        sbp_done = sem("sbp_done")
        vsb_done = sem("vsb_done")
        z_done, ln_step, sp_done, suf_done, a_done, pv_done = (
            sem(v) for v in ("z_done", "ln_step", "sp_done", "suf_done", "a_done", "pv_done"))
        ysb_hi_done, ysb_lo_done = sem("ysb_hi_done"), sem("ysb_lo_done")
        gate_done = sem("gate_done")
        lg_done, ttr_done, p_done, p_t, pT_done, pvd_done = (
            sem(v) for v in ("lg_done", "ttr_done", "p_done", "p_t", "pT_done", "pvd_done"))
        pinv_done, ydn_done, yd_t, ydT_done = sem("pinv_done"), sem("ydn_done"), sem("yd_t"), sem("ydT_done")
        yd_hi_done, yd_lo_done = sem("yd_hi_done"), sem("yd_lo_done")
        sig_done = sem("sig_done")
        gy_done, gz_done, mg_done, mg_hi_done, mg_lo_done = (
            sem(v) for v in ("gy_done", "gz_done", "mg_done", "mg_hi_done", "mg_lo_done"))
        h_t, out_copy = sem("h_t"), sem("out_copy")
        out_in = [sem(f"out_in{i}") for i in range(4)]

        def cols_unit(w, c0, n=256):
            return w[:, c0:c0 + n].rearrange("(k p) n -> p k n", p=P)

        def rows_unit(w, r0, c0, n):
            k = 2048 // n
            return w[r0:r0 + k * P, c0:c0 + n].rearrange("(k p) n -> p k n", p=P)

        ffn_w = [(w1_ffn1[0], w3_ffn1[0], w2_ffn1[0]), (w1_ffn2[0], w3_ffn2[0], w2_ffn2[0])]
        win, wg = w_in[0], w_gate[0]
        out_view = out[0].rearrange("(j p) (m q) -> m p j q", p=P, q=P)

        def middle_unit(u):
            if u < U_QI:
                return rows_unit(win, 4 * P * (u - U_QD), Q_D, 512)
            if u < U_QSB:
                return cols_unit(win, Q_I + 256 * (u - U_QI))
            if u < U_KSB:
                return cols_unit(win, Q_SB + 256 * (u - U_QSB))
            if u < U_VSB:
                return cols_unit(win, K_SB + 256 * (u - U_KSB))
            if u < U_GATE:
                return rows_unit(win, 4 * P * (u - U_VSB), V_SB, 512)
            if u < U_PROJ:
                return cols_unit(wg, 256 * (u - U_GATE))
            if u < U_OUT:
                w = (w_proj_sb, w_proj_dsa)[(u - U_PROJ) % 2][0]
                return rows_unit(w, 0, 512 * ((u - U_PROJ) // 2), 512)
            return cols_unit(w_out[0], 256 * (u - U_OUT))

        def raw_as(u, n):
            return raw[u % 2][:, 0:2048].rearrange("p (k n) -> p k n", n=n)

        def size(u):
            return KD * XC if u == U_X else 2048

        def in_parts(u):
            return 16 * 5 if u == U_X else 16

        def arrived(u):
            extra = in_parts(U_X) - 16 if u % 2 == U_X % 2 and u >= U_X else 0
            return 16 * (u // 2 + 1) + extra

        block = ctx.enter_context(nc.Block())

        @block.sync
        def _(sp):
            def load(u, src, n):
                if u >= 2:
                    sp.wait_ge(lo_done, u - 1)
                sp.dma_start(raw_as(u, n), src).then_inc(raw_in[u % 2], 16)

            for j in range(NB):
                sp.dma_start(xin[:, j, :], x[0, j * P:(j + 1) * P, :]).then_inc(x_in[j], 16)
            for k in range(KD):
                sp.dma_start(slab[:, k, :], w_ada[0, k * P:(k + 1) * P, 0:HEAD_COLS]).then_inc(slab_in[k], 16)

            def ffn(f):
                w1, w3, w2 = ffn_w[f]
                u0 = (0, U_FFN2)[f]
                load(u0, cols_unit(w1, 0), 256)
                load(u0 + 1, cols_unit(w3, 0), 256)
                w1v = w1.rearrange("(k p) (c n) -> c p k n", p=P, n=256)
                w3v = w3.rearrange("(k p) (c n) -> c p k n", p=P, n=256)
                with sp.Fori(1, UP_PAIRS) as i:
                    sp.wait_ge(lo_done, i * 2 + (u0 - 1))
                    sp.dma_start(raw_as(u0, 256), w1v[bass.ds(i, 1)].rearrange("a p k n -> (a p) k n")
                                 ).then_inc(raw_in[u0 % 2], 16)
                    sp.wait_ge(lo_done, i * 2 + u0)
                    sp.dma_start(raw_as(u0 + 1, 256), w3v[bass.ds(i, 1)].rearrange("a p k n -> (a p) k n")
                                 ).then_inc(raw_in[(u0 + 1) % 2], 16)
                w2v = w2.rearrange("(t k p) n -> t p k n", p=P, k=2)
                u1 = u0 + 2 * UP_PAIRS
                load(u1, w2v[0], 1024)
                with sp.Fori(0, (UP_PAIRS - 1) // 2) as i:
                    for r in range(2):
                        sp.wait_ge(lo_done, i * 2 + (u1 + r))
                        sp.dma_start(raw_as(u1 + 1 + r, 1024),
                                     w2v[bass.ds(i * 2 + (1 + r), 1)].rearrange("a p k n -> (a p) k n")
                                     ).then_inc(raw_in[(u1 + 1 + r) % 2], 16)

            ffn(0)
            sp.wait_ge(lo_done, U_X - 1)
            xr = raw[U_X % 2][:, 0:KD * XC].rearrange("p (k n) -> p k n", n=XC)
            for at, c0, c1 in ((0, K_I, K_I + HD), (HD, K_I, K_I + HD), (2 * HD, K_D, K_D + HD),
                               (3 * HD, V_D, V_D + HD), (4 * HD, W_I, W_END)):
                sp.dma_start(xr[:, :, at:at + c1 - c0], cols_unit(win, c0, c1 - c0)).then_inc(raw_in[U_X % 2], 16)
            for u in range(U_QD, U_FFN2):
                load(u, middle_unit(u), 512 if u in range(U_QD, U_QI) or u in range(U_VSB, U_GATE)
                     or u in range(U_PROJ, U_OUT) else 256)
            ffn(1)
            for o, m in enumerate(W2_ORDER):
                sp.wait_ge(out_copy, o + 1)
                sp.dma_start(out_view[m], outb[:, o % 4]).then_inc(out_in[o % 4], 16)
            for i in range(4):
                sp.wait_ge(out_in[i], 16 * KD // 4)

        @block.gpsimd
        def _(pool):
            g = nc.gpsimd
            g.memset(ident[:], 0.0).then_inc(consts, 1)
            pool.wait_ge(consts, 1)
            g.affine_select(out=ident[:], in_=ident[:], compare_op=ALU.not_equal, fill=1.0, base=0,
                            pattern=[[-1, P]], channel_multiplier=1).then_inc(consts, 1)
            g.memset(ones[:], 1.0).then_inc(consts, 1)
            g.memset(neg_ones[:], -1.0).then_inc(consts, 1)
            g.memset(eps[:], EPS).then_inc(consts, 1)
            pool.wait_ge(consts, 5)
            g.tensor_copy(ident_bf[:], ident[:]).then_inc(consts, 1)
            g.affine_select(out=neg_tri[:], in_=neg_ones[:], compare_op=ALU.is_ge, fill=0.0, base=0,
                            pattern=[[-1, P]], channel_multiplier=1).then_inc(consts, 1)
            g.memset(strict_bf[:], 0.0).then_inc(consts, 1)
            pool.wait_ge(consts, 8)
            g.affine_select(out=strict_bf[:], in_=strict_bf[:], compare_op=ALU.is_gt, fill=NEG, base=0,
                            pattern=[[1, P]], channel_multiplier=-1).then_inc(consts, 1)

            ada_v = w_ada[0].rearrange("(r k p) n -> r p k n", p=P, k=4)

            def ada_load(gr, wait):
                for r in range(2):
                    if wait is not None:
                        pool.wait_ge(ada_mac, wait + 4 * r)
                    src = (ada_v[r, :, :, HEAD_COLS + 256 * gr:HEAD_COLS + 256 * gr + 256] if isinstance(gr, int)
                           else ada_v[r, :, :, bass.ds(gr * 256 + HEAD_COLS, 256)])
                    pool.dma_start(ada_ring[:, r, :].rearrange("p (k n) -> p k n", n=256), src).then_inc(ada_in[r], 16)

            ada_load(0, None)
            with pool.Fori(1, LOOP_GROUPS) as i:
                ada_load(i, i * 8 - 4)
            for gr in range(LOOP_GROUPS, GROUPS):
                ada_load(gr, 8 * gr - 4)

            pool.wait_ge(n_lo_done, 2 * KD)
            g.iota(dist[:], pattern=[[1, S]], base=0, channel_multiplier=-1,
                   allow_small_or_imprecise_dtypes=True).then_inc(consts, 1)
            pool.wait_ge(consts, 10)
            g.affine_select(out=R[:, 0:P], in_=dist[:, 0:P], compare_op=ALU.is_ge, fill=NEG, base=0,
                            pattern=[[-1, P]], channel_multiplier=1).then_inc(consts, 1)
            for n, i in enumerate((1, 2, 3)):
                pool.wait_ge(score_add, NH * (n + 1))
                d = score[:, S_OFF[i] + i * P:S_OFF[i] + (i + 1) * P]
                g.affine_select(out=d, in_=d, compare_op=ALU.is_ge, fill=NOT_CAUSAL, base=0,
                                pattern=[[-1, P]], channel_multiplier=1).then_inc(causal, 1)

        @block.scalar
        def _(act):
            a = nc.scalar
            dma_rows = [(C_BADA, 72, b_ada[0].rearrange("(r q) -> r q", q=P)),
                        (C_G, 8, g_ffn1[0].rearrange("(r q) -> r q", q=P)),
                        (C_G + 8, 8, g_mix[0].rearrange("(r q) -> r q", q=P)),
                        (C_G + 16, 8, g_ffn2[0].rearrange("(r q) -> r q", q=P)),
                        (C_BGATE, 16, b_gate[0].rearrange("(r q) -> r q", q=P)),
                        (C_C, 8, c[0].rearrange("(r q) -> r q", q=P))]
            for r0, n, src in dma_rows:
                act.dma_start(rows[r0:r0 + n, :], src).then_inc(rows_in, 16)
            for half in range(2):
                act.dma_start(rows[C_GQ:C_GQ + 1, half * HD:(half + 1) * HD], g_q_dsa).then_inc(rows_in, 16)
                act.dma_start(rows[C_GK:C_GK + 1, half * HD:(half + 1) * HD], g_k_dsa).then_inc(rows_in, 16)

            def hi(u):
                act.wait_ge(raw_in[u % 2], arrived(u))
                if u >= 2:
                    act.wait_ge(tiles, before(u - 1))
                n = size(u)
                a.activation(w_hi[u % 2][:, 0:n], raw[u % 2][:, 0:n], ACT.Copy).then_inc(hi_done, 1)

            def hi_in_loop(i, u, signals):
                act.wait_ge(raw_in[u % 2], i * 16 + arrived(u))
                act.wait_ge(tiles, i * signals + before(u - 1))
                a.activation(w_hi[u % 2][:, 0:2048], raw[u % 2][:, 0:2048], ACT.Copy).then_inc(hi_done, 1)

            def squares(q, o):
                act.wait_ge(h_done, KD * q + o + 1)
                if o >= 2:
                    act.wait_ge(ssq_done, (KD - 1) * q + o - 1)
                a.activation(ssq[:] if o == 0 else sq[:], h[:, ORDERS[q][o], :], ACT.Square).then_inc(sq_done, 1)

            def norm_std(q):
                act.wait_ge(sum_done, q + 1)
                a.activation(ssq[:], ps[:, 4, :], ACT.Sqrt, bias=eps[:], scale=1.0 / D).then_inc(std_done, 1)

            def norm_apply(q):
                act.wait_ge(coef, (1, 3, 5)[q])
                for m in range(KD):
                    act.wait_ge(nt_done, KD * q + m + 1)
                    a.activation(nt[:, m % 2, :], nt[:, m % 2, :], ACT.Identity, bias=mod[:, 24 * q + m:24 * q + m + 1],
                                 scale=nscale[:, q, m:m + 1]).then_inc(nf_done, 1)
                    act.wait_ge(nf_done, KD * q + m + 1)
                    a.activation(n_hi[:, m, :], nt[:, m % 2, :], ACT.Copy).then_inc(n_hi_done, 1)

            def ffn(f):
                u0 = (0, U_FFN2)[f]
                j0 = KF * f
                with act.Fori(0, UP_PAIRS) as i:
                    hi_in_loop(i, u0 + 1, 4)
                    for t in range(2):
                        act.wait_ge(tiles, i * 4 + tile_at(u0, t))
                        act.wait_ge(mid_lo_done, i * 2 + (j0 + t + 1))
                        a.activation(nt[:, t, :], ps[:, t, :], ACT.Silu).then_inc(silu_done, 1)
                        if t == 0:
                            hi_in_loop(i, u0 + 2, 4)
                    for t in range(2):
                        act.wait_ge(mul_done, i * 2 + (j0 + t + 3))
                        a.activation(mid_hi[:, bass.ds(i * 2 + t, 1), :], nt[:, t:t + 1, :], ACT.Copy).then_inc(mid_hi_done, 1)
                with act.Fori(0, (UP_PAIRS - 1) // 2) as i:
                    hi_in_loop(i, u0 + 2 * UP_PAIRS + 1, 2)
                    hi_in_loop(i, u0 + 2 * UP_PAIRS + 2, 2)

            act.wait_ge(consts, 5)
            act.wait_ge(rows_in, 16 * 10)
            act.wait_ge(cols_done, 1)
            a.activation(sc[:], cols[:, C_C:C_C + KD], ACT.Silu).then_inc(silu_c, 1)
            for o in range(KD):
                squares(0, o)
            norm_std(0)
            hi(0)
            norm_apply(0)
            ffn(0)
            hi(U_X)
            for o in range(KD):
                squares(1, o)
            norm_std(1)
            hi(U_QD)
            norm_apply(1)

            act.wait_ge(tiles, tile_at(U_X, 0))
            a.activation(kiT[:], ps[:, 0, :], ACT.Copy).then_inc(ki_done, 1)
            for y in range(2):
                act.wait_ge(tiles, tile_at(U_X, 1 + y))
                src = ps[:, 1 + y, 0:2 * 136].rearrange("p (b n) -> p b n", n=136)[:, :, 0:HD]
                a.activation(sqt[:, y * P:(y + 1) * P].rearrange("p (b n) -> p b n", n=HD), src,
                             ACT.Square).then_inc(ksq_done, 1)
            hi(U_QD + 1)
            act.wait_ge(kss_done, 1)
            a.activation(kr[:], kr[:], ACT.Sqrt, bias=eps[:], scale=1.0 / HD).then_inc(kstd_done, 1)
            hi(U_QI)
            for j in range(NB):
                act.wait_ge(tiles, tile_at(U_QD + 1, j))
                if j == 0:
                    act.wait_ge(kss_done, 1)
                else:
                    act.wait_ge(qss_done, j)
                a.activation(sqt[:], ps[:, 4 + j, :], ACT.Square).then_inc(qsq_done, 1)
            act.wait_ge(qss_done, NB)
            a.activation(qr[:], qr[:], ACT.Sqrt, bias=eps[:], scale=1.0 / HD).then_inc(qstd_done, 1)
            hi(U_QI + 1)
            for t in range(4):
                if t == 2:
                    hi(U_QSB)
                act.wait_ge(tiles, tile_at(U_QI, t))
                a.activation(qiT[:, t, :], ps[:, t % 2, :], ACT.Copy).then_inc(qi_done, 1)
            for s, (i, hd) in enumerate(IDX):
                n = (i + 1) * P
                act.wait_ge(idx_mm, s + 1)
                if s >= 2:
                    act.wait_ge(score_add, s - 1)
                a.activation(relu[:, s % 2, 0:n], ps[:, 4 + s % 4, 0:n], ACT.Relu).then_inc(relu_done, 1)
            for t in range(8):
                if t % 2 == 0:
                    hi(U_QSB + 1 + t // 2)
                act.wait_ge(tiles, tile_at(U_QSB, t))
                dst = (qsbT if t < 4 else ksbT)[:, t % 4, :]
                a.activation(dst, ps[:, t % 4, :], ACT.Copy, scale=HD ** -0.5 if t < 4 else 1.0).then_inc(sbp_done, 1)
            hi(U_VSB + 1)
            hi(U_GATE)
            for j in range(NB):
                act.wait_ge(tiles, tile_at(U_VSB + 1, j))
                a.activation(vsb[:, j, :], ps[:, 4 + j, :], ACT.Copy).then_inc(vsb_done, 1)

            def soft(s):
                i = s // NH
                n = (i + 1) * P
                act.wait_ge(ttr_done, s + 1)
                if s >= 2:
                    act.wait_ge(p_t, s - 1)
                a.activation(pb[:, s % 2, 0:n], lgb[:, s % 2, 0:n], ACT.Exp, bias=negmax[:, s:s + 1], scale=-1.0,
                             accum_out=psum_p[:, s:s + 1]).then_inc(p_done, 1)

            def ydT_copy(i):
                act.wait_ge(yd_t, i + 1)
                a.activation(ydT[:, :, i * P:(i + 1) * P], ps[:, B_F, :].rearrange("p (t q) -> p t q", q=P),
                             ACT.Copy).then_inc(ydT_done, 1)

            for hd in range(NH):
                act.wait_ge(z_done, hd + 1)
                if hd:
                    act.wait_ge(pv_done, hd)
                a.activation(sp_a[:], psf[:, 0:ZW], ACT.Abs).then_inc(ln_step, 1)
                act.wait_ge(ln_step, 3 * hd + 1)
                a.activation(sp_a[:], sp_a[:], ACT.Exp, scale=-1.0).then_inc(ln_step, 1)
                act.wait_ge(ln_step, 3 * hd + 2)
                a.activation(sp_a[:], sp_a[:], ACT.Ln, bias=1.0).then_inc(ln_step, 1)
                soft(4 * hd)
                if hd < NH - 1:
                    hi(U_GATE + 1 + hd)
                soft(4 * hd + 1)
                act.wait_ge(suf_done, hd + 1)
                a.activation(sp_a[:], psf[:, 0:ZW], ACT.Exp).then_inc(a_done, 1)
                if hd in (2, 4, 6):
                    ydT_copy(hd // 2 - 1)
                soft(4 * hd + 2)
                soft(4 * hd + 3)
                if hd % 2:
                    act.wait_ge(pv_done, hd + 1)
                    a.activation(ysb_hi[:, hd // 2, :], ps[:, B_Y, :], ACT.Copy).then_inc(ysb_hi_done, 1)
            hi(U_PROJ)
            ydT_copy(3)
            act.wait_ge(ydT_done, 4)
            a.activation(yd_hi[:], ydT[:], ACT.Copy).then_inc(yd_hi_done, 1)
            hi(U_PROJ + 1)
            act.wait_ge(gate_done, 16)
            for m in list(range(0, 4)) + list(range(8, 12)) + list(range(4, 8)) + list(range(12, 16)):
                a.activation(gates[:, m, :], gates[:, m, :], ACT.Sigmoid).then_inc(sig_done, 1)
            hi(U_PROJ + 2)
            for m in range(KD):
                if m == 4:
                    hi(U_PROJ + 3)
                    hi(U_OUT)
                act.wait_ge(mg_done, m + 1)
                a.activation(n_hi[:, m, :], gates[:, 8 + m, :], ACT.Copy).then_inc(mg_hi_done, 1)
            hi(U_OUT + 1)
            for o in range(KD):
                if o == 2:
                    hi(U_OUT + 2)
                if o == 4:
                    hi(U_OUT + 3)
                if o == 6:
                    hi(U_FFN2)
                squares(2, o)
            norm_std(2)
            norm_apply(2)
            ffn(1)
            for o, m in enumerate(W2_ORDER):
                act.wait_ge(h_t, o + 1)
                if o >= 4:
                    act.wait_ge(out_in[o % 4], 16)
                a.activation(outb[:, o % 4], ps[:, m, :].rearrange("p (j q) -> p j q", q=P), ACT.Copy).then_inc(out_copy, 1)

        @block.vector
        def _(dve):
            v = nc.vector

            def lo(u):
                dve.wait_ge(hi_done, u + 1)
                n = size(u)
                v.tensor_tensor(w_lo[u % 2][:, 0:n], raw[u % 2][:, 0:n], w_hi[u % 2][:, 0:n].bitcast(F32),
                                ALU.subtract).then_inc(lo_done, 1)

            def lo_in_loop(i, u):
                dve.wait_ge(hi_done, i * 2 + (u + 1))
                v.tensor_tensor(w_lo[u % 2][:, 0:2048], raw[u % 2][:, 0:2048], w_hi[u % 2][:, 0:2048].bitcast(F32),
                                ALU.subtract).then_inc(lo_done, 1)

            def add_square(q, o):
                dve.wait_ge(sq_done, KD * q + o + 1)
                if o >= 2:
                    dve.wait_ge(ssq_done, (KD - 1) * q + o - 1)
                v.tensor_tensor(ssq[:], ssq[:], sq[:], ALU.add).then_inc(ssq_done, 1)

            def norm_rstd(q):
                dve.wait_ge(std_done, q + 1)
                v.reciprocal(ssq[:], ssq[:]).then_inc(rstd_done, 1)

            def norm_apply(q):
                dve.wait_ge(rstd_done, q + 1)
                for m in range(KD + 1):
                    if m < KD:
                        if m >= 2:
                            dve.wait_ge(n_lo_done, KD * q + m - 1)
                        v.tensor_tensor(nt[:, m % 2, :], h[:, m, :], ssq[:], ALU.mult).then_inc(nt_done, 1)
                    if m >= 1:
                        dve.wait_ge(n_hi_done, KD * q + m)
                        v.tensor_tensor(n_lo[:, m - 1, :], nt[:, (m - 1) % 2, :], n_hi[:, m - 1, :].bitcast(F32),
                                        ALU.subtract).then_inc(n_lo_done, 1)

            def scale_of(q):
                v.scalar_tensor_tensor(out=nscale[:, q, :], in0=mod[:, 24 * q + 8:24 * q + 16], scalar=1.0,
                                       in1=cols[:, C_G + 8 * q:C_G + 8 * q + 8], op0=ALU.add, op1=ALU.mult).then_inc(coef, 1)

            def ada_group(acc, arrive, mac_at):
                for k in range(KD):
                    if k % 4 == 0:
                        dve.wait_ge(ada_in[k // 4], arrive)
                    w = ada_ring[:, k // 4, 256 * (k % 4):256 * (k % 4) + 256]
                    if k == 0:
                        v.tensor_scalar(acc, w, sc[:, 0:1], None, ALU.mult).then_inc(ada_mac, 1)
                    else:
                        dve.wait_ge(ada_mac, mac_at + k)
                        v.scalar_tensor_tensor(out=acc, in0=w, scalar=sc[:, k:k + 1], in1=acc,
                                               op0=ALU.mult, op1=ALU.add).then_inc(ada_mac, 1)

            def ada_columns(g, at):
                dve.wait_ge(ada_mm, g + 1)
                v.tensor_tensor(mod[:, at], ps[:, 7, 0:2], cols[:, at], ALU.add).then_inc(mod_done, 1)

            def residual(q, o, bank, gate):
                m = ORDERS[q][o]
                dve.wait_ge(tiles, tile_at((U_X - 1, U_OUT, U_END - 1)[q - 1], o))
                v.scalar_tensor_tensor(out=h[:, m, :], in0=ps[:, bank, :], scalar=gate[:, m:m + 1], in1=h[:, m, :],
                                       op0=ALU.mult, op1=ALU.add).then_inc(h_done, 1)

            def ffn(f):
                u0 = (0, U_FFN2)[f]
                j0 = KF * f
                with dve.Fori(0, UP_PAIRS) as i:
                    lo_in_loop(i, u0 + 1)
                    if f == 0:
                        ada_group(ada_acc[:], i * 32 + 16, i * 16)
                        ada_columns(i * 2, bass.ds(i * 4 + 16, 2))
                    lo_in_loop(i, u0 + 2)
                    if f == 0:
                        ada_group(ada_acc[:], i * 32 + 32, i * 16 + 8)
                    for t in range(2):
                        dve.wait_ge(tiles, i * 4 + tile_at(u0 + 1, t))
                        dve.wait_ge(silu_done, i * 2 + (j0 + t + 3))
                        v.tensor_tensor(nt[:, t, :], nt[:, t, :], ps[:, 2 + t, :], ALU.mult).then_inc(mul_done, 1)
                    for t in range(2):
                        dve.wait_ge(mid_hi_done, i * 2 + (j0 + t + 1))
                        v.tensor_tensor(mid_lo[:, bass.ds(i * 2 + t, 1), :], nt[:, t:t + 1, :],
                                        mid_hi[:, bass.ds(i * 2 + t, 1), :].bitcast(F32), ALU.subtract).then_inc(mid_lo_done, 1)
                    if f == 0:
                        ada_columns(i * 2 + 1, bass.ds(i * 4 + 18, 2))
                if f == 0:
                    v.tensor_scalar(half_gate[:, 0, :], mod[:, 16:24], 0.5, None, ALU.mult).then_inc(coef, 1)
                    scale_of(1)
                with dve.Fori(0, (UP_PAIRS - 1) // 2) as i:
                    lo_in_loop(i, u0 + 2 * UP_PAIRS + 1)
                    lo_in_loop(i, u0 + 2 * UP_PAIRS + 2)

            v.memset(best[:, 0:1], 0.0).then_inc(tiles, 1)
            v.memset(best[:, 1:2], 0.0).then_inc(silu_done, 2)
            v.memset(best[:, 2:3], 0.0).then_inc(mul_done, 2)
            v.memset(best[:, 3:4], 0.0).then_inc(mid_lo_done, 2)
            for t in range(NB):
                for half in range(2):
                    ins = v.memset(qscale[half * HD:(half + 1) * HD, t:t + 1], 2.0 ** (2 * t + half + 1) * HD ** -0.5)
            ins.then_inc(coef_q, 1)
            dve.wait_ge(rows_t, 1)
            v.tensor_copy(cols[:], ps[:, 0, 0:C_END]).then_inc(cols_done, 1)
            dve.wait_ge(cols_done, 1)
            dve.wait_ge(coef_q, 1)
            v.tensor_scalar(qscale[:], qscale[:], cols[:, C_GQ:C_GQ + 1], None, ALU.mult).then_inc(coef_q, 1)
            for o in range(KD + 1):
                if o < KD:
                    dve.wait_ge(x_t, o + 1)
                    v.tensor_copy(h[:, o, :], ps[:, 2 + o % 2, :]).then_inc(h_done, 1)
                if o >= 2:
                    add_square(0, o - 1)
            dve.wait_ge(silu_c, 1)
            for k in range(KD):
                dve.wait_ge(slab_in[k], 16)
                if k == 0:
                    v.tensor_scalar(head_acc[:], slab[:, 0, :], sc[:, 0:1], None, ALU.mult).then_inc(head_mac, 1)
                else:
                    dve.wait_ge(head_mac, k)
                    v.scalar_tensor_tensor(out=head_acc[:], in0=slab[:, k, :], scalar=sc[:, k:k + 1], in1=head_acc[:],
                                           op0=ALU.mult, op1=ALU.add).then_inc(head_mac, 1)
            norm_rstd(0)
            dve.wait_ge(head_mm, 1)
            v.tensor_tensor(mod[:, 0:16], ps[:, 1, 0:16], cols[:, 0:16], ALU.add).then_inc(mod_done, 1)
            dve.wait_ge(mod_done, 1)
            scale_of(0)
            lo(0)
            norm_apply(0)
            ffn(0)
            dve.wait_ge(coef, 2)
            lo(U_X)
            for o in range(KD + 1):
                if o < KD:
                    residual(1, o, W2_ORDER[o], half_gate[:, 0, :])
                if o >= 2:
                    add_square(1, o - 1)
            norm_rstd(1)
            norm_apply(1)
            lo(U_QD)

            for gr in range(LOOP_GROUPS, LOOP_GROUPS + 3):
                ada_group(ada_rest[:, gr - LOOP_GROUPS, :], 16 * (gr + 1), 8 * gr)
            for y in range(2):
                dve.wait_ge(tiles, tile_at(U_X, 1 + y))
                dve.wait_ge(ksq_done, 1 + y)
                both = ps[:, 1 + y, 0:2 * 136].rearrange("p (b n) -> p b n", n=136)
                v.tensor_copy(vd[:, 2 * y:2 * y + 2, :], both[:, :, HD:2 * HD]).then_inc(vw_done, 1)
                v.tensor_scalar(wi[:, 2 * y:2 * y + 2, :], both[:, :, 2 * HD:2 * HD + NH],
                                HD ** -0.5 * NH ** -0.5, None, ALU.mult).then_inc(vw_done, 1)
            v.tensor_reduce(kr[:], sqt[:, 0:NB * HD].rearrange("p (b n) -> p b n", n=HD), AX.X, ALU.add).then_inc(kss_done, 1)
            dve.wait_ge(kstd_done, 1)
            v.reciprocal(kr[:], kr[:]).then_inc(kr_done, 1)
            dve.wait_ge(kr_done, 1)
            for y in range(2):
                both = ps[:, 1 + y, 0:2 * 136].rearrange("p (b n) -> p b n", n=136)
                for dup in range(2):
                    v.tensor_tensor(kn[:, 2 * y:2 * y + 2, dup, :], both[:, :, 0:HD],
                                    kr[:, 2 * y:2 * y + 2].unsqueeze(2).to_broadcast([P, 2, HD]), ALU.mult).then_inc(kn_done, 1)
            lo(U_QD + 1)
            for gr in range(LOOP_GROUPS + 3, GROUPS):
                ada_group(ada_rest[:, gr - LOOP_GROUPS, :], 16 * (gr + 1), 8 * gr)
            lo(U_QI)
            for j in range(NB):
                dve.wait_ge(qsq_done, j + 1)
                v.tensor_reduce(qr[:, j * NH:(j + 1) * NH], sqt[:].rearrange("p (b n) -> p b n", n=HD),
                                AX.X, ALU.add).then_inc(qss_done, 1)
            dve.wait_ge(kn_t, 1)
            v.tensor_scalar(kdT[:], ps[:, 3, :], cols[:, C_GK:C_GK + 1], None, ALU.mult).then_inc(kdT_done, 1)
            dve.wait_ge(qstd_done, 1)
            v.reciprocal(qr[:], qr[:]).then_inc(qr_done, 1)
            dve.wait_ge(qr_done, 1)

            def q_norm(j):
                if j >= 2:
                    dve.wait_ge(qn_t, j - 1)
                v.tensor_tensor(qn[:, j % 2, :].rearrange("p (b n) -> p b n", n=HD),
                                ps[:, 4 + j, :].rearrange("p (b n) -> p b n", n=HD),
                                qr[:, j * NH:(j + 1) * NH].unsqueeze(2).to_broadcast([P, NH, HD]), ALU.mult).then_inc(qn_done, 1)

            def q_store(j):
                dve.wait_ge(qn_t, j + 1)
                v.tensor_tensor(qdT[:, :, j * P:(j + 1) * P], ps[:, 2 + j % 2, :].rearrange("p (t q) -> p t q", q=P),
                                qscale[:].unsqueeze(2).to_broadcast([P, NB, P]), ALU.mult).then_inc(qdT_done, 1)

            q_norm(0)
            q_norm(1)
            lo(U_QI + 1)
            dve.wait_ge(ada_mm, LOOP_GROUPS + 1)
            v.tensor_tensor(mod[:, 60:72], ps[:, 3, 0:12], cols[:, 60:72], ALU.add).then_inc(mod_done, 1)
            dve.wait_ge(mod_done, LOOP_GROUPS + 2)
            scale_of(2)
            v.tensor_scalar(half_gate[:, 1, :], mod[:, 64:72], 0.5, None, ALU.mult).then_inc(coef, 1)
            q_store(0)
            q_norm(2)
            q_store(1)
            q_norm(3)
            lo(U_QSB)
            q_store(2)
            q_store(3)
            for s, (i, hd) in enumerate(IDX):
                n = (i + 1) * P
                acc = score[:, S_OFF[i]:S_OFF[i] + n]
                dve.wait_ge(relu_done, s + 1)
                w = wi[:, i, hd:hd + 1]
                if hd == 0:
                    v.tensor_scalar(acc, relu[:, s % 2, 0:n], w, 0.0, ALU.mult, ALU.add).then_inc(score_add, 1)
                else:
                    dve.wait_ge(score_add, s)
                    v.scalar_tensor_tensor(out=acc, in0=relu[:, s % 2, 0:n], scalar=w, in1=acc,
                                           op0=ALU.mult, op1=ALU.add).then_inc(score_add, 1)

            top_count = [0]

            def take(i):
                n = (i + 1) * P
                acc = score[:, S_OFF[i]:S_OFF[i] + n]
                if top_count[0] % (2 * ROUNDS) == 0:
                    dve.wait_ge(causal, i)
                    dve.wait_ge(consts, 11)
                if top_count[0]:
                    dve.wait_ge(top, top_count[0])
                v.max(best[:], acc).then_inc(top, 1)
                dve.wait_ge(top, top_count[0] + 1)
                v.match_replace(acc, best[:], acc, TAKEN).then_inc(top, 1)
                top_count[0] += 2
                if top_count[0] % (2 * ROUNDS) == 0:
                    r = R[:, R_OFF[i]:R_OFF[i] + n]
                    dve.wait_ge(top, top_count[0])
                    v.tensor_scalar(r, acc, (TAKEN + NOT_CAUSAL) / 2, NEG, ALU.is_gt, ALU.mult).then_inc(r_step, 1)
                    dve.wait_ge(r_step, i)
                    v.scalar_tensor_tensor(out=r, in0=dist[:, 0:n], scalar=float(-P * i), in1=r,
                                           op0=ALU.add, op1=ALU.add).then_inc(r_done, 1)

            rounds = [1] * ROUNDS + [2] * ROUNDS + [3] * ROUNDS
            taken = [0]

            def takes(n):
                for i in rounds[taken[0]:taken[0] + n]:
                    take(i)
                taken[0] += n

            for t in range(4):
                lo(U_QSB + 1 + t)
                takes(7)
            lo(U_VSB + 1)
            takes(4)
            lo(U_GATE)

            def logits_max(s):
                i, hd = divmod(s, NH)
                n = (i + 1) * P
                dve.wait_ge(lg_done, s + 1)
                if s == 0:
                    dve.wait_ge(consts, 11)
                if hd == 0 and i:
                    dve.wait_ge(r_done, i)
                if s >= 2:
                    dve.wait_ge(p_done, s - 1)
                v.tensor_tensor_reduce(lgb[:, s % 2, 0:n], ps[:, B_LG, 0:n], R[:, R_OFF[i]:R_OFF[i] + n],
                                       -(2.0 ** -(hd + 1)), 3e38, ALU.add, ALU.min, negmax[:, s:s + 1]).then_inc(ttr_done, 1)

            def pT_copy(s):
                n = (s // NH + 1) * P
                dve.wait_ge(p_t, s + 1)
                if s >= 2:
                    dve.wait_ge(pvd_done, s - 1)
                v.tensor_copy(pT[:, s % 2, 0:n], ps[:, B_PT, 0:n]).then_inc(pT_done, 1)

            def gate_store(m):
                dve.wait_ge(tiles, tile_at(U_GATE, m))
                v.tensor_scalar(gates[:, m, :], ps[:, B_F, :], cols[:, C_BGATE + m:C_BGATE + m + 1], None,
                                ALU.add).then_inc(gate_done, 1)

            def yd_norm(i):
                dve.wait_ge(pvd_done, NH * (i + 1))
                v.reciprocal(pinv[:, NH * i:NH * (i + 1)], psum_p[:, NH * i:NH * (i + 1)]).then_inc(pinv_done, 1)
                dve.wait_ge(pinv_done, i + 1)
                if i:
                    dve.wait_ge(yd_t, i)
                v.tensor_tensor(ydtok[:].rearrange("p (b n) -> p b n", n=HD), ps[:, B_O, :].rearrange("p (b n) -> p b n", n=HD),
                                pinv[:, NH * i:NH * (i + 1)].unsqueeze(2).to_broadcast([P, NH, HD]), ALU.mult).then_inc(ydn_done, 1)

            for hd in range(NH):
                if hd:
                    pT_copy(4 * hd - 1)
                logits_max(4 * hd)
                dve.wait_ge(ln_step, 3 * hd + 3)
                v.scalar_tensor_tensor(out=sp_a[:], in0=psf[:, 0:ZW], scalar=0.0, in1=sp_a[:], op0=ALU.max,
                                       op1=ALU.add).then_inc(sp_done, 1)
                gate_store(2 * hd)
                pT_copy(4 * hd)
                logits_max(4 * hd + 1)
                if hd < NH - 1:
                    lo(U_GATE + 1 + hd)
                if hd in (2, 4, 6):
                    yd_norm(hd // 2 - 1)
                pT_copy(4 * hd + 1)
                logits_max(4 * hd + 2)
                if hd < 4:
                    takes(4)
                gate_store(2 * hd + 1)
                pT_copy(4 * hd + 2)
                logits_max(4 * hd + 3)
                if hd % 2:
                    dve.wait_ge(ysb_hi_done, hd // 2 + 1)
                    v.tensor_tensor(ysb_lo[:, hd // 2, :], ps[:, B_Y, :], ysb_hi[:, hd // 2, :].bitcast(F32),
                                    ALU.subtract).then_inc(ysb_lo_done, 1)
            assert taken[0] == len(rounds)
            lo(U_PROJ)
            pT_copy(31)
            yd_norm(3)
            dve.wait_ge(yd_hi_done, 1)
            v.tensor_tensor(yd_lo[:], ydT[:], yd_hi[:].bitcast(F32), ALU.subtract).then_inc(yd_lo_done, 1)
            lo(U_PROJ + 1)

            def gated_sb(m):
                dve.wait_ge(tiles, tile_at(U_PROJ + 2 * (m // 4), m % 4))
                dve.wait_ge(sig_done, m + 1 if m < 4 else m + 5)
                v.tensor_tensor(gates[:, m, :], gates[:, m, :], ps[:, m % 4, :], ALU.mult).then_inc(gy_done, 1)

            def merged(m):
                dve.wait_ge(tiles, tile_at(U_PROJ + 2 * (m // 4) + 1, m % 4))
                dve.wait_ge(sig_done, m + 5 if m < 4 else m + 9)
                g = gates[:, 8 + m, :]
                v.tensor_tensor(g, g, ps[:, 4 + m % 4, :], ALU.mult).then_inc(gz_done, 1)
                dve.wait_ge(gz_done, m + 1)
                dve.wait_ge(gy_done, m + 1)
                v.tensor_tensor(g, g, gates[:, m, :], ALU.add).then_inc(mg_done, 1)

            def merged_lo(m):
                dve.wait_ge(mg_hi_done, m + 1)
                v.tensor_tensor(n_lo[:, m, :], gates[:, 8 + m, :], n_hi[:, m, :].bitcast(F32), ALU.subtract).then_inc(mg_lo_done, 1)

            for half in range(2):
                for m in range(4 * half, 4 * half + 4):
                    gated_sb(m)
                    if m == 4 * half + 3:
                        lo(U_PROJ + 2 if half == 0 else U_OUT)
                for m in range(4 * half, 4 * half + 4):
                    merged(m)
                    if m > 4 * half:
                        merged_lo(m - 1)
                merged_lo(4 * half + 3)
                lo(U_PROJ + 3 if half == 0 else U_OUT + 1)
            for o in range(KD + 1):
                if o == 2:
                    lo(U_OUT + 2)
                if o == 4:
                    lo(U_OUT + 3)
                if o == 6:
                    lo(U_FFN2)
                if o < KD:
                    residual(2, o, o, mod[:, 40:48])
                if o >= 2:
                    add_square(2, o - 1)
            norm_rstd(2)
            norm_apply(2)
            ffn(1)
            for o in range(KD):
                residual(3, o, W2_ORDER[o], half_gate[:, 1, :])

        @block.tensor
        def _(pe):
            def mm3(dst, whi, wlo, xhi, xlo, first, last):
                pe.matmul(dst, whi, xhi, start=first, stop=False, skip_group_check=True)
                pe.matmul(dst, whi, xlo, start=False, stop=False, skip_group_check=True)
                return pe.matmul(dst, wlo, xhi, start=False, stop=last, skip_group_check=True)

            def column_tile(u, bank, t, act_hi, act_lo, width=256, nk=KD, step=None):
                for k in range(nk):
                    if step is not None:
                        pe.wait_ge(step[0], step[1] + k)
                    w = slice(k * width + t * P, k * width + (t + 1) * P)
                    ins = mm3(ps[:, bank, :], w_hi[u % 2][:, w], w_lo[u % 2][:, w], act_hi[:, k, :], act_lo[:, k, :],
                              k == 0, k == nk - 1)
                return ins

            def token_tile(u, dst, j, w0, n, width, ks, k0, first, last):
                for k in ks:
                    w = slice((k - k0) * width + w0, (k - k0) * width + w0 + n)
                    tok = slice(j * P, (j + 1) * P)
                    f, l = first and k == ks[0], last and k == ks[-1]
                    pe.matmul(dst, n_hi[:, k, tok], w_hi[u % 2][:, w], start=f, stop=False, skip_group_check=True)
                    pe.matmul(dst, n_hi[:, k, tok], w_lo[u % 2][:, w], start=False, stop=False, skip_group_check=True)
                    ins = pe.matmul(dst, n_lo[:, k, tok], w_hi[u % 2][:, w], start=False, stop=l, skip_group_check=True)
                return ins

            def norm_sum(q):
                pe.wait_ge(ssq_done, (KD - 1) * (q + 1))
                if q:
                    pe.wait_ge(h_done, KD * (q + 1))
                pe.matmul(ps[:, 4, :], ones[:], ssq[:], start=True, stop=True).then_inc(sum_done, 1)

            def ffn(f):
                u0 = (0, U_FFN2)[f]
                j0 = KF * f
                pe.wait_ge(n_lo_done, KD * (2 * f + 1))
                with pe.Fori(0, UP_PAIRS) as i:
                    for r in range(2):
                        u = u0 + r
                        pe.wait_ge(lo_done, i * 2 + (u + 1))
                        for t in range(2):
                            pe.wait_ge((silu_done, mul_done)[r], i * 2 + (j0 + t + 1))
                            column_tile(u, 2 * r + t, t, n_hi, n_lo).then_inc(tiles, 1)
                        if f == 0:
                            pe.wait_ge(ada_mac, i * 16 + 8 * (r + 1))
                            pe.wait_ge(mod_done, i * 2 + (r + 1))
                            for t in range(2):
                                ins = pe.matmul(ps[:, 7, t:t + 1], ada_acc[:, t * P:(t + 1) * P], ones[:, 0:1],
                                                start=True, stop=True, skip_group_check=True)
                            ins.then_inc(ada_mm, 1)
                u1 = u0 + 2 * UP_PAIRS

                def down(u, k_at, first=False, last=False):
                    for o, m in enumerate(W2_ORDER):
                        if first and m == 7 and f == 0:
                            pe.wait_ge(mod_done, 1 + LOOP_GROUPS)
                        if first and m == 0:
                            pe.wait_ge(silu_done, j0 + KF + 2)
                        if first and m == 2:
                            pe.wait_ge(mul_done, j0 + KF + 2)
                        for k in range(2):
                            w = slice(k * D + m * P, k * D + (m + 1) * P)
                            ins = mm3(ps[:, m, :], w_hi[u % 2][:, w], w_lo[u % 2][:, w], mid_hi[:, k_at(k), :],
                                      mid_lo[:, k_at(k), :], first and k == 0, last and k == 1)
                        if last or m == W2_ORDER[-1]:
                            ins.then_inc(tiles, 1)
                        if last and f == 1 and o >= 2:
                            out_tile(o - 2)

                def out_tile(o):
                    m = W2_ORDER[o]
                    pe.wait_ge(h_done, KD * 3 + o + 1)
                    for j in range(NB):
                        ins = pe.transpose(ps[:, m, j * P:(j + 1) * P], h[:, m, j * P:(j + 1) * P], ident[:])
                    ins.then_inc(h_t, 1)

                pe.wait_ge(lo_done, u1 + 1)
                pe.wait_ge(mid_lo_done, j0 + 2 + 2)
                down(u1, lambda k: slice(k, k + 1), first=True)
                pe.wait_ge(mid_lo_done, j0 + KF + 2)
                with pe.Fori(0, (UP_PAIRS - 3) // 2) as i:
                    for r in range(2):
                        pe.wait_ge(lo_done, i * 2 + (u1 + 2 + r))
                        down(u1 + 1 + r, lambda k: bass.ds(i * 4 + (2 + 2 * r + k), 1))
                for n in (UP_PAIRS - 2, UP_PAIRS - 1):
                    pe.wait_ge(lo_done, u1 + n + 1)
                    down(u1 + n, lambda k: slice(2 * n + k, 2 * n + k + 1), last=n == UP_PAIRS - 1)
                if f == 0:
                    norm_sum(1)
                else:
                    out_tile(KD - 2)
                    out_tile(KD - 1)

            pe.wait_ge(rows_in, 16 * 10)
            pe.wait_ge(consts, 9)
            pe.transpose(ps[:, 0, 0:C_END], rows[:], ident[0:C_END, 0:C_END]).then_inc(rows_t, 1)
            for j in range(NB):
                pe.wait_ge(x_in[j], 16)
            for m in range(KD):
                if m >= 2:
                    pe.wait_ge(h_done, m - 1)
                for j in range(NB):
                    ins = pe.transpose(ps[:, 2 + m % 2, j * P:(j + 1) * P], xin[:, j, m * P:(m + 1) * P], ident[:])
                ins.then_inc(x_t, 1)
            norm_sum(0)
            pe.wait_ge(head_mac, KD)
            for t in range(16):
                ins = pe.matmul(ps[:, 1, t:t + 1], head_acc[:, t * P:(t + 1) * P], ones[:, 0:1], start=True, stop=True,
                                skip_group_check=True)
            ins.then_inc(head_mm, 1)
            ffn(0)

            u = U_X
            pe.wait_ge(lo_done, u + 1)
            column_tile(u, 0, 0, n_hi, n_lo, width=XC, step=(n_lo_done, KD + 1)).then_inc(tiles, 1)
            for y in range(2):
                for j in (2 * y, 2 * y + 1):
                    ins = token_tile(u, ps[:, 1 + y, (j % 2) * 136:(j % 2) * 136 + 136], j, 2 * HD, 136, XC,
                                     range(KD), 0, True, True)
                ins.then_inc(tiles, 1)
            for half in range(2):
                u = U_QD + half
                pe.wait_ge(lo_done, u + 1)
                for j in range(NB):
                    ins = token_tile(u, ps[:, 4 + j, :], j, 0, 512, 512, range(4 * half, 4 * half + 4), 4 * half,
                                     half == 0, half == 1)
                    if half or j == NB - 1:
                        ins.then_inc(tiles, 1)
            pe.wait_ge(kn_done, NB)
            for j in range(NB):
                ins = pe.transpose(ps[:, 3, j * P:(j + 1) * P], kn[:, j].rearrange("p a n -> p (a n)"), ident[:])
            ins.then_inc(kn_t, 1)

            def q_turn(j):
                pe.wait_ge(qn_done, j + 1)
                if j == 0:
                    pe.wait_ge(mod_done, LOOP_GROUPS + 2)
                if j >= 2:
                    pe.wait_ge(qdT_done, j - 1)
                for t in range(4):
                    ins = pe.transpose(ps[:, 2 + j % 2, t * P:(t + 1) * P], qn[:, j % 2, t * P:(t + 1) * P], ident[:])
                ins.then_inc(qn_t, 1)

            def qi_tile(t):
                u = U_QI + t // 2
                pe.wait_ge(lo_done, u + 1)
                if t == 0:
                    pe.wait_ge(ki_done, 1)
                if t >= 2:
                    pe.wait_ge(qi_done, t - 1)
                column_tile(u, t % 2, t % 2, n_hi, n_lo).then_inc(tiles, 1)

            qi_tile(0)
            qi_tile(1)
            pe.wait_ge(ada_mac, 8 * GROUPS)
            pe.wait_ge(kdT_done, 1)
            for t in range(2 * (GROUPS - LOOP_GROUPS)):
                ins = pe.matmul(ps[:, 3, t:t + 1], ada_rest[:, t // 2, (t % 2) * P:(t % 2 + 1) * P], ones[:, 0:1],
                                start=True, stop=True, skip_group_check=True)
            ins.then_inc(ada_mm, 1)
            q_turn(0)
            q_turn(1)
            qi_tile(2)
            qi_tile(3)
            q_turn(2)
            q_turn(3)

            pe.wait_ge(qi_done, 4)
            for s, (i, hd) in enumerate(IDX):
                n = (i + 1) * P
                half = slice((hd % 2) * HD, (hd % 2 + 1) * HD)
                if s >= 4:
                    pe.wait_ge(relu_done, s - 3)
                pe.matmul(ps[:, 4 + s % 4, 0:n], qiT[half, hd // 2, i * P:n], kiT[half, 0:n],
                          start=True, stop=True).then_inc(idx_mm, 1)
            for t in range(8):
                u = U_QSB + t // 2
                pe.wait_ge(lo_done, u + 1)
                if t == 2:
                    pe.wait_ge(qdT_done, NB)
                if t >= 4:
                    pe.wait_ge(sbp_done, t - 3)
                column_tile(u, t % 4, t % 2, n_hi, n_lo).then_inc(tiles, 1)
            pe.wait_ge(relu_done, len(IDX))
            for half in range(2):
                u = U_VSB + half
                pe.wait_ge(lo_done, u + 1)
                for j in range(NB):
                    ins = token_tile(u, ps[:, 4 + j, :], j, 0, 512, 512, range(4 * half, 4 * half + 4), 4 * half,
                                     half == 0, half == 1)
                    if half or j == NB - 1:
                        ins.then_inc(tiles, 1)

            def logits(s):
                i, hd = divmod(s, NH)
                half = slice((hd % 2) * HD, (hd % 2 + 1) * HD)
                if s:
                    pe.wait_ge(ttr_done, s)
                pe.matmul(ps[:, B_LG, 0:(i + 1) * P], qdT[half, hd // 2, i * P:(i + 1) * P], kdT[half, 0:(i + 1) * P],
                          start=True, stop=True).then_inc(lg_done, 1)

            def turn(s):
                pe.wait_ge(p_done, s + 1)
                if s:
                    pe.wait_ge(pT_done, s)
                for b in range(s // NH + 1):
                    ins = pe.transpose(ps[:, B_PT, b * P:(b + 1) * P], pb[:, s % 2, b * P:(b + 1) * P], ident[:])
                ins.then_inc(p_t, 1)

            def values(s):
                i, hd = divmod(s, NH)
                pe.wait_ge(pT_done, s + 1)
                if hd == 0 and i:
                    pe.wait_ge(ydn_done, i)
                for b in range(i + 1):
                    ins = pe.matmul(ps[:, B_O, hd * HD:(hd + 1) * HD], pT[:, s % 2, b * P:(b + 1) * P], vd[:, b, :],
                                    start=b == 0, stop=b == i, skip_group_check=True)
                ins.then_inc(pvd_done, 1)

            def sparse(s):
                if s >= 2:
                    values(s - 2)
                if 1 <= s <= NB * NH:
                    turn(s - 1)
                if s < NB * NH:
                    logits(s)

            def yd_turn(i, gate_tiles):
                pe.wait_ge(ydn_done, i + 1)
                pe.wait_ge(gate_done, gate_tiles)
                for t in range(4):
                    ins = pe.transpose(ps[:, B_F, t * P:(t + 1) * P], ydtok[:, t * P:(t + 1) * P], ident[:])
                ins.then_inc(yd_t, 1)

            def z_block(b, q0=0):
                return psf[:, BLK[b] + q0 * P:BLK[b] + S - b * P]

            pe.wait_ge(sbp_done, 8)
            pe.wait_ge(vsb_done, NB)
            for hd in range(NH):
                t, half = hd // 2, slice((hd % 2) * HD, (hd % 2 + 1) * HD)
                if hd:
                    pe.wait_ge(a_done, hd)
                for b in (0, 1, 3, 2):
                    pe.matmul(z_block(b), ksbT[half, t, b * P:(b + 1) * P], qsbT[half, t, b * P:S],
                              start=b != 3, stop=False, skip_group_check=True)
                for b in range(NB):
                    ins = pe.matmul(psf[:, BLK[b]:BLK[b] + P], ident_bf[:], strict_bf[:], start=False, stop=False,
                                    skip_group_check=True)
                ins.then_inc(z_done, 1)
                sparse(4 * hd)
                u = U_GATE + hd
                pe.wait_ge(lo_done, u + 1)
                if hd:
                    pe.wait_ge(gate_done, 2 * hd)
                column_tile(u, B_F, 0, n_hi, n_lo).then_inc(tiles, 1)
                sparse(4 * hd + 1)
                pe.wait_ge(sp_done, hd + 1)
                for b in range(NB):
                    for b2 in range(b, NB):
                        ins = pe.matmul(z_block(b, b2 - b), (neg_tri if b2 == b else neg_ones)[:],
                                        sp_a[:, BLK[b2]:BLK[b2] + S - b2 * P], start=False, stop=b2 == NB - 1,
                                        skip_group_check=True)
                ins.then_inc(suf_done, 1)
                if hd in (2, 4, 6):
                    yd_turn(hd // 2 - 1, 2 * hd + 1)
                sparse(4 * hd + 2)
                pe.wait_ge(gate_done, 2 * hd + 1)
                if hd in (2, 4, 6):
                    pe.wait_ge(ydT_done, hd // 2)
                column_tile(u, B_F, 1, n_hi, n_lo).then_inc(tiles, 1)
                sparse(4 * hd + 3)
                pe.wait_ge(a_done, hd + 1)
                if hd and hd % 2 == 0:
                    pe.wait_ge(ysb_lo_done, hd // 2)
                for b in range(NB):
                    ins = pe.matmul(ps[half, B_Y, b * P:S], vsb[:, b, hd * HD:(hd + 1) * HD],
                                    sp_a[:, BLK[b]:BLK[b] + S - b * P], start=b == 0, stop=b == NB - 1,
                                    skip_group_check=True)
                ins.then_inc(pv_done, 1)
            sparse(32)
            sparse(33)
            yd_turn(3, 16)

            for n in range(4):
                u = U_PROJ + n
                if n == 0:
                    pe.wait_ge(ysb_lo_done, 4)
                if n == 1:
                    pe.wait_ge(yd_lo_done, 1)
                pe.wait_ge(lo_done, u + 1)
                for t in range(4):
                    if n >= 2:
                        pe.wait_ge((gy_done, gz_done)[n % 2], t + 1)
                    column_tile(u, 4 * (n % 2) + t, t, *((ysb_hi, ysb_lo), (yd_hi, yd_lo))[n % 2], width=512,
                                nk=4).then_inc(tiles, 1)
            for m in range(KD):
                u = U_OUT + m // 2
                pe.wait_ge(lo_done, u + 1)
                if m == 0:
                    pe.wait_ge(mg_done, KD)
                column_tile(u, m, m % 2, n_hi, n_lo, step=(mg_lo_done, 1) if m == 0 else None).then_inc(tiles, 1)
            norm_sum(2)
            ffn(1)


_INS = ["x", "c", "w_ada", "b_ada", "g_ffn1", "w1_ffn1", "w3_ffn1", "w2_ffn1", "g_mix", "w_in", "g_q_dsa", "g_k_dsa",
        "w_proj_sb", "w_proj_dsa", "w_gate", "b_gate", "w_out", "g_ffn2", "w1_ffn2", "w3_ffn2", "w2_ffn2"]


def kernel(**inputs):
    import numpy as np
    import concourse.bacc as bacc
    from concourse.bass_utils import run_bass_kernel_spmd

    nc = bacc.Bacc("TRN2", target_bir_lowering=False, num_devices=1)
    arrays, args = {}, []
    for name in _INS:
        a = np.ascontiguousarray(inputs[name])
        arrays[f"in_{name}"] = a
        args.append(nc.dram_tensor(f"in_{name}", a.shape, mybir.dt.from_np(a.dtype), kind="ExternalInput").ap())
    args.append(nc.dram_tensor("out", (1, S, D), F32, kind="ExternalOutput").ap())
    layer_kernel(nc, *args)
    r = run_bass_kernel_spmd(nc, [arrays], core_ids=[0])
    return r.results[0]["out"]
```

```python
from contextlib import ExitStack

import concourse.bass as bass
from concourse import mybir

F32 = mybir.dt.float32
F32R = mybir.dt.float32r
BF16 = mybir.dt.bfloat16
ACT = mybir.ActivationFunctionType
ALU = mybir.AluOpType
AX = mybir.AxisListType

P = 128
D = 1024
S = 512
KD = D // P
NB = S // P
F = 2816
KF = F // P
HD = 64
NH = 8
TOPK = 128
EPS = 1e-6
UP_PAIRS = KF // 2
FFN_UNITS = 3 * UP_PAIRS
SLOT = 2112
NEG = -(2.0 ** 100)
NOT_CAUSAL = -1e38
TAKEN = -3e38

Q_SB, K_SB, V_SB, Q_D, K_D, V_D, Q_I, K_I, W_I, W_END = 0, 512, 1024, 1536, 2048, 2112, 2176, 2688, 2752, 2760
XC = HD + HD + HD + NH

U_X = FFN_UNITS
U_QD = U_X + 1
U_QI = U_QD + 2
U_QSB = U_QI + 2
U_KSB = U_QSB + 2
U_VSB = U_KSB + 2
U_GATE = U_VSB + 2
U_PROJ = U_GATE + 8
U_OUT = U_PROJ + 4
U_FFN2 = U_OUT + 4
U_END = U_FFN2 + FFN_UNITS

C_BADA, C_G, C_BGATE, C_C, C_GQ, C_GK, C_END = 0, 72, 96, 112, 120, 121, 122
HEAD_COLS = 2 * D
GROUPS = (9 * D - HEAD_COLS) // 512
LOOP_GROUPS = UP_PAIRS
REST = GROUPS - LOOP_GROUPS
SHIFT_MACS = 7

B_Z, B_Y, B_F, B_LG, B_PT, B_O = 0, 3, 4, 5, 6, 7
X_BANKS = [2, 3, 5, 6]
W2_ORDER = [4, 5, 6, 0, 1, 2, 3, 7]
ORDERS = [list(range(KD)), W2_ORDER, list(range(KD)), W2_ORDER]

BLK = {0: 0, 1: 512, 3: 896, 2: 1024}
ZW = 1280
IDX = [(i, h) for i in (1, 2, 3) for h in range(NH)]
S_OFF = {1: 0, 2: 256, 3: 640}
R_OFF = {0: 0, 1: 128, 2: 384, 3: 768}
ROUNDS = TOPK // 8
HALVES = ((slice(0, HD), slice(HD, P)), (slice(HD, P), slice(0, HD)))


def tiles_of(u):
    if u < U_X or u >= U_FFN2:
        n = u if u < U_X else u - U_FFN2
        return 2 if n < 2 * UP_PAIRS else KD if n == FFN_UNITS - 1 else 1
    return {U_X: 2, U_QD: 1, U_QD + 1: NB, U_VSB: 1, U_VSB + 1: NB}.get(u, 4 if U_PROJ <= u < U_OUT else 2)


def before(u):
    return 1 + sum(tiles_of(v) for v in range(u))


def tile_at(u, t):
    return before(u) + t + 1


def layer_kernel(nc, x, c, w_ada, b_ada, g_ffn1, w1_ffn1, w3_ffn1, w2_ffn1, g_mix, w_in, g_q_dsa, g_k_dsa,
                 w_proj_sb, w_proj_dsa, w_gate, b_gate, w_out, g_ffn2, w1_ffn2, w3_ffn2, w2_ffn2, out):
    ctx = ExitStack()
    with ctx:
        place = [16640]

        def sb(name, shape, dt=F32, at=None):
            n = 1
            for v in shape[1:]:
                n *= v
            n *= 2 if dt == BF16 else 4
            off = place[0] if at is None else at
            if at is None:
                place[0] += -(-n // 32) * 32
                assert place[0] <= 229344, (name, place[0])
            return nc.alloc_sbuf_tensor_at(name, shape, dt, offset=off)

        def sem(name):
            return ctx.enter_context(nc.semaphore(name))

        h = sb("h", [P, KD, S])
        n_hi = sb("n_hi", [P, KD, S], F32R)
        n_at = place[0]
        n_lo = sb("n_lo", [P, KD, S], F32R)
        nx = sb("nx", [P, KD, S], at=n_at)
        raw = [sb(f"raw{i}", [P, SLOT]) for i in range(2)]
        w_hi = [sb(f"w_hi{i}", [P, SLOT], F32R) for i in range(2)]
        w_lo = [sb(f"w_lo{i}", [P, SLOT], F32R) for i in range(2)]
        ident = sb("ident", [P, P])
        ident_bf = sb("ident_bf", [P, P], BF16)
        strict_bf = sb("strict_bf", [P, P], BF16)
        neg_tri = sb("neg_tri", [P, P])
        neg_ones = sb("neg_ones", [P, P])
        neg_tri_r = sb("neg_tri_r", [P, P], F32R, at=place[0] - 1024)
        neg_ones_r = sb("neg_ones_r", [P, P], F32R, at=place[0] - 512)
        ones = sb("ones", [P, P])
        share = sb("share", [P, P])
        rows = sb("rows", [C_END, P])
        cols = sb("cols", [P, C_END])
        mod = sb("mod", [P, 9 * KD])
        nscale = sb("nscale", [P, 3, KD])
        half_gate = sb("half_gate", [P, 2, KD])
        sc = sb("sc", [P, KD])
        eps = sb("eps", [P, 1])
        zeros = sb("zeros", [P, LOOP_GROUPS])
        pick = sb("pick", [P, 2 * REST - 1])
        turns = sb("turns", [P, LOOP_GROUPS])
        now = sb("now", [P, LOOP_GROUPS], F32R)
        slope_inv = sb("slope_inv", [P, NH])
        wi = sb("wi", [P, NB, NH])
        kr = sb("kr", [P, NB])
        qr = sb("qr", [P, NB * NH])
        best = sb("best", [P, 8])
        negmax = sb("negmax", [P, NB * NH])
        psum_p = sb("psum_p", [P, NB * NH])
        pinv = sb("pinv", [P, NB * NH])
        tmp_at = place[0]
        nt = sb("nt", [P, 2, S])
        ssq = sb("ssq", [P, S])
        outb = sb("outb", [P, 4, NB, P], at=tmp_at)
        lgb = sb("lgb", [P, 2, S], at=tmp_at)
        arena = place[0]
        mid_hi = sb("mid_hi", [P, KF, S], F32R)
        mid_lo = sb("mid_lo", [P, KF, S], F32R)
        ada_ring = sb("ada_ring", [P, 2, 2 * 512])
        mod_rows = sb("mod_rows", [LOOP_GROUPS, 512], at=place[0])
        acc_lo = sb("acc_lo", [P, 512], F32R, at=place[0])
        acc_hi = sb("acc_hi", [P, 512], F32R, at=arena - 2048)
        ada_acc = sb("ada_acc", [P, 512])
        ada_rest = sb("ada_rest", [P, REST, 512], at=arena + 49152)
        slab = sb("slab", [P, KD, HEAD_COLS], at=arena)
        head_acc = sb("head_acc", [P, HEAD_COLS], at=arena + 65536)
        xin = sb("xin", [P, NB, D], at=arena + 73728)
        gates = sb("gates", [P, 16, S], at=arena)
        qi2 = [sb(f"qi2_{v}", [P, 4, S], F32R, at=arena + (0, 78848)[v]) for v in range(2)]
        ki_hi = sb("ki_hi", [P, S], F32R, at=arena + 8192)
        ki_lo = sb("ki_lo", [P, S], F32R, at=arena + 14336)
        relu = sb("relu", [P, 2, S], at=arena + 10240)
        qn = sb("qn", [P, 2, S], at=arena + 69120)
        kn = sb("kn", [P, NB, 2, HD], at=arena + 20480)
        ki = sb("ki", [P, NB, 2, HD], at=arena + 22528)
        dist = sb("dist", [P, S], at=arena + 26112)
        score = sb("score", [P, 1152], at=arena + 28160)
        qsbT = sb("qsbT", [P, 4, S], at=arena + 32768)
        ksbT = sb("ksbT", [P, 4, S], at=arena + 40960)
        ysb_hi = sb("ysb_hi", [P, 4, S], F32R, at=arena + 32768)
        ysb_lo = sb("ysb_lo", [P, 4, S], F32R, at=arena + 40960)
        vsb = sb("vsb", [P, NB, S], at=arena + 49152)
        qd2 = [sb(f"qd2_{i}", [P, NH, P], F32R, at=arena + (20480, 16384, 57344, 61440)[i]) for i in range(NB)]
        yd_hi = sb("yd_hi", [P, 4, S], F32R, at=arena + 49152)
        yd_lo = sb("yd_lo", [P, 4, S], F32R, at=arena + 57344)
        kd_hi = sb("kd_hi", [P, S], F32R, at=arena + 65536)
        kd_lo = sb("kd_lo", [P, S], F32R, at=arena + 87040)
        vd = sb("vd", [P, NB, HD], at=arena + 67584)
        R = sb("R", [P, ZW], at=arena + 68608)
        sp_a = sb("sp_a", [P, ZW], at=arena + 73728)
        sp_lo = sb("sp_lo", [P, ZW], F32R, at=arena + 73728)
        sqt = sb("sqt", [P, S], at=arena + 73728)
        ydT = sb("ydT", [P, 4, S], at=arena + 78848)
        pT = sb("pT", [P, 2, S], at=arena + 93184)
        ydtok = sb("ydtok", [P, S], at=arena + 91136)
        assert arena + 93184 <= place[0] - 2048 - 4096
        sp_hi0 = sb("sp_hi0", [P, S], F32R, at=arena - 2048)
        sp_hi1 = sb("sp_hi1", [P, ZW - S], F32R, at=arena + 97280)
        assert arena + 97280 + 4 * (ZW - S) <= place[0]

        ps = ctx.enter_context(nc.psum_tensor("ps", [P, 8, S], F32))
        psf = ps[:, :, :].rearrange("p b n -> p (b n)")

        rows_in, rows_t, cols_done, silu_c = sem("rows_in"), sem("rows_t"), sem("cols_done"), sem("silu_c")
        coef_q = sem("coef_q")
        consts = sem("consts")
        scale_in = [sem(f"scale_in{k}") for k in range(KD)]
        shift_in = [sem(f"shift_in{k}") for k in range(KD)]
        x_in = [sem(f"x_in{j}") for j in range(NB)]
        x_t = sem("x_t")
        head_mac, head_mm = sem("head_mac"), sem("head_mm")
        xg_done = sem("xg_done")
        sq_used = sem("sq_used")
        first_in, first_hi, first_lo = sem("first_in"), sem("first_hi"), sem("first_lo")
        now_done = sem("now_done")
        ada_in = [sem(f"ada_in{r}") for r in range(2)]
        acc_hi_done, acc_lo_done = sem("acc_hi_done"), sem("acc_lo_done")
        ada_mac = sem("ada_mac")
        ada_mm = sem("ada_mm")
        ada_rows, ada_t = sem("ada_rows"), sem("ada_t")
        mod_done = sem("mod_done")
        coef = sem("coef")
        raw_in = [sem(f"raw_in{i}") for i in range(2)]
        hi_done, lo_done = sem("hi_done"), sem("lo_done")
        tiles = sem("tiles")
        silu_done, mul_done = sem("silu_done"), sem("mul_done")
        mid_hi_done, mid_lo_done = sem("mid_hi_done"), sem("mid_lo_done")
        h_done = sem("h_done")
        sq_done, ssq_done = sem("sq_done"), sem("ssq_done")
        sum_done, std_done, rstd_done = sem("sum_done"), sem("std_done"), sem("rstd_done")
        nx_done, n_hi_done, n_lo_done = sem("nx_done"), sem("n_hi_done"), sem("n_lo_done")
        ki_tok, ki_t, ki_done, vw_done = sem("ki_tok"), sem("ki_t"), sem("ki_done"), sem("vw_done")
        ksq_done, kss_done, kstd_done, kr_done, kn_done = (sem(f"k{v}_done") for v in ("sq", "ss", "std", "r", "n"))
        kn_t, kd_hi_done, kd_lo_done = sem("kn_t"), sem("kd_hi_done"), sem("kd_lo_done")
        qsq_done, qss_done, qstd_done, qr_done, qn_done = (sem(f"q{v}_done") for v in ("sq", "ss", "std", "r", "n"))
        qn_t, qd_hi_done, qd_lo_done = sem("qn_t"), sem("qd_hi_done"), sem("qd_lo_done")
        qi_hi_done, qi_lo_done, ki_lo_done = sem("qi_hi_done"), sem("qi_lo_done"), sem("ki_lo_done")
        idx_mm, relu_done, score_add = sem("idx_mm"), sem("relu_done"), sem("score_add")
        causal = sem("causal")
        top = sem("top")
        r_step, r_done = sem("r_step"), sem("r_done")
        sbp_done = sem("sbp_done")
        vsb_done = sem("vsb_done")
        z_done, ln_step, sp_done, suf_done, a_done, pv_done = (
            sem(v) for v in ("z_done", "ln_step", "sp_done", "suf_done", "a_done", "pv_done"))
        round_done, sp_hi_done, sp_lo_done = sem("round_done"), sem("sp_hi_done"), sem("sp_lo_done")
        ysb_hi_done, ysb_lo_done = sem("ysb_hi_done"), sem("ysb_lo_done")
        gate_done = sem("gate_done")
        lg_done, ttr_done, p_done, p_t, pT_done, pvd_done = (
            sem(v) for v in ("lg_done", "ttr_done", "p_done", "p_t", "pT_done", "pvd_done"))
        pinv_done, ydn_done, yd_t, ydT_done = sem("pinv_done"), sem("ydn_done"), sem("yd_t"), sem("ydT_done")
        yd_hi_done, yd_lo_done = sem("yd_hi_done"), sem("yd_lo_done")
        sig_done = sem("sig_done")
        gy_done, gz_done, mg_done, mg_hi_done, mg_lo_done = (
            sem(v) for v in ("gy_done", "gz_done", "mg_done", "mg_hi_done", "mg_lo_done"))
        h_t, out_copy = sem("h_t"), sem("out_copy")
        out_in = [sem(f"out_in{i}") for i in range(4)]

        def cols_unit(w, c0, n=256):
            return w[:, c0:c0 + n].rearrange("(k p) n -> p k n", p=P)

        def rows_unit(w, r0, c0, n):
            k = 2048 // n
            return w[r0:r0 + k * P, c0:c0 + n].rearrange("(k p) n -> p k n", p=P)

        ffn_w = [(w1_ffn1[0], w3_ffn1[0], w2_ffn1[0]), (w1_ffn2[0], w3_ffn2[0], w2_ffn2[0])]
        win, wg = w_in[0], w_gate[0]
        out_view = out[0].rearrange("(j p) (m q) -> m p j q", p=P, q=P)

        def middle_unit(u):
            if u < U_QI:
                return rows_unit(win, 4 * P * (u - U_QD), Q_D, 512)
            if u < U_QSB:
                return cols_unit(win, Q_I + 256 * (u - U_QI))
            if u < U_KSB:
                return cols_unit(win, Q_SB + 256 * (u - U_QSB))
            if u < U_VSB:
                return cols_unit(win, K_SB + 256 * (u - U_KSB))
            if u < U_GATE:
                return rows_unit(win, 4 * P * (u - U_VSB), V_SB, 512)
            if u < U_PROJ:
                return cols_unit(wg, 256 * (u - U_GATE))
            if u < U_OUT:
                w = (w_proj_sb, w_proj_dsa)[(u - U_PROJ) % 2][0]
                return rows_unit(w, 0, 512 * ((u - U_PROJ) // 2), 512)
            return cols_unit(w_out[0], 256 * (u - U_OUT))

        def qi_parts(t):
            return [(2 * t + n, own, other) for n, (own, other) in enumerate(HALVES)]

        def qd2_heads(j, half, n):
            return qd2[j][half].rearrange("p (t two) q -> p two t q", two=2)[:, n]

        def raw_as(u, n):
            return raw[u % 2][:, 0:2048].rearrange("p (k n) -> p k n", n=n)

        def size(u):
            return KD * XC if u == U_X else 2048

        def in_parts(u):
            return 16 * 4 if u == U_X else 16

        def arrived(u):
            extra = in_parts(U_X) - 16 if u % 2 == U_X % 2 and u >= U_X else 0
            return 16 * (u // 2 + 1) + extra

        block = ctx.enter_context(nc.Block())

        @block.sync
        def _(sp):
            def load(u, src, n):
                if u >= 2:
                    sp.wait_ge(lo_done, u - 1)
                sp.dma_start(raw_as(u, n), src).then_inc(raw_in[u % 2], 16)

            sp.dma_start(rows[C_C:C_C + 8, :], c[0].rearrange("(r q) -> r q", q=P)).then_inc(rows_in, 16)
            sp.dma_start(rows[C_BADA:C_BADA + 72, :], b_ada[0].rearrange("(r q) -> r q", q=P)).then_inc(rows_in, 16)
            for j in range(NB):
                sp.dma_start(xin[:, j, :], x[0, j * P:(j + 1) * P, :]).then_inc(x_in[j], 16)
            for c0, arrive in ((D, scale_in), (0, shift_in)):
                for k in range(KD):
                    sp.dma_start(slab[:, k, c0:c0 + D], w_ada[0, k * P:(k + 1) * P, c0:c0 + D]).then_inc(arrive[k], 16)

            def ffn(f):
                w1, w3, w2 = ffn_w[f]
                u0 = (0, U_FFN2)[f]
                if f == 0:
                    halves = cols_unit(w1, 0)
                    sp.dma_start(raw_as(0, 256)[:, 0:KD // 2], halves[:, 0:KD // 2]).then_inc(first_in, 16)
                    sp.dma_start(raw_as(0, 256)[:, KD // 2:KD], halves[:, KD // 2:KD]).then_inc(raw_in[0], 16)
                else:
                    load(u0, cols_unit(w1, 0), 256)
                load(u0 + 1, cols_unit(w3, 0), 256)
                w1v = w1.rearrange("(k p) (c n) -> c p k n", p=P, n=256)
                w3v = w3.rearrange("(k p) (c n) -> c p k n", p=P, n=256)
                with sp.Fori(1, UP_PAIRS) as i:
                    sp.wait_ge(lo_done, i * 2 + (u0 - 1))
                    sp.dma_start(raw_as(u0, 256), w1v[bass.ds(i, 1)].rearrange("a p k n -> (a p) k n")
                                 ).then_inc(raw_in[u0 % 2], 16)
                    sp.wait_ge(lo_done, i * 2 + u0)
                    sp.dma_start(raw_as(u0 + 1, 256), w3v[bass.ds(i, 1)].rearrange("a p k n -> (a p) k n")
                                 ).then_inc(raw_in[(u0 + 1) % 2], 16)
                w2v = w2.rearrange("(t k p) n -> t p k n", p=P, k=2)
                u1 = u0 + 2 * UP_PAIRS
                load(u1, w2v[0], 1024)
                with sp.Fori(0, (UP_PAIRS - 1) // 2) as i:
                    for r in range(2):
                        sp.wait_ge(lo_done, i * 2 + (u1 + r))
                        sp.dma_start(raw_as(u1 + 1 + r, 1024),
                                     w2v[bass.ds(i * 2 + (1 + r), 1)].rearrange("a p k n -> (a p) k n")
                                     ).then_inc(raw_in[(u1 + 1 + r) % 2], 16)

            ffn(0)
            sp.wait_ge(lo_done, U_X - 1)
            xr = raw[U_X % 2][:, 0:KD * XC].rearrange("p (k n) -> p k n", n=XC)
            for at, c0, c1 in ((0, K_D, K_D + HD), (HD, V_D, V_D + HD), (2 * HD, W_I, W_END),
                               (2 * HD + NH, K_I, K_I + HD)):
                sp.dma_start(xr[:, :, at:at + c1 - c0], cols_unit(win, c0, c1 - c0)).then_inc(raw_in[U_X % 2], 16)
            for u in range(U_QD, U_FFN2):
                load(u, middle_unit(u), 512 if u in range(U_QD, U_QI) or u in range(U_VSB, U_GATE)
                     or u in range(U_PROJ, U_OUT) else 256)
            ffn(1)
            for o, m in enumerate(W2_ORDER):
                sp.wait_ge(out_copy, o + 1)
                sp.dma_start(out_view[m], outb[:, o % 4]).then_inc(out_in[o % 4], 16)
            for i in range(4):
                sp.wait_ge(out_in[i], 16 * KD // 4)

        @block.gpsimd
        def _(pool):
            g = nc.gpsimd
            g.memset(ident[:], 0.0).then_inc(consts, 1)
            pool.wait_ge(consts, 1)
            g.affine_select(out=ident[:], in_=ident[:], compare_op=ALU.not_equal, fill=1.0, base=0,
                            pattern=[[-1, P]], channel_multiplier=1).then_inc(consts, 1)
            g.memset(ones[:], 1.0).then_inc(consts, 1)
            g.memset(neg_ones[:], -1.0).then_inc(consts, 1)
            g.memset(eps[:], EPS).then_inc(consts, 1)
            g.memset(share[:], 1.0 / D).then_inc(consts, 1)
            g.memset(pick[:], 0.0).then_inc(consts, 1)
            g.memset(zeros[:], 0.0).then_inc(consts, 1)
            pool.wait_ge(consts, 8)
            g.memset(pick[:, REST - 1:REST], 1.0).then_inc(consts, 1)
            g.iota(turns[:], pattern=[[1, LOOP_GROUPS]], base=0, channel_multiplier=0,
                   allow_small_or_imprecise_dtypes=True).then_inc(consts, 1)
            g.tensor_copy(ident_bf[:], ident[:]).then_inc(consts, 1)
            g.affine_select(out=neg_tri[:], in_=neg_ones[:], compare_op=ALU.is_ge, fill=0.0, base=0,
                            pattern=[[-1, P]], channel_multiplier=1).then_inc(consts, 1)
            g.memset(strict_bf[:], 0.0).then_inc(consts, 1)
            pool.wait_ge(consts, 13)
            g.affine_select(out=strict_bf[:], in_=strict_bf[:], compare_op=ALU.is_gt, fill=NEG, base=0,
                            pattern=[[1, P]], channel_multiplier=-1).then_inc(consts, 1)

            ada_v = w_ada[0].rearrange("(s k p) n -> s p k n", p=P, k=2)

            def ada_load(gr, n, wait):
                if wait is not None:
                    pool.wait_ge(ada_mac, wait)
                src = (ada_v[n, :, :, HEAD_COLS + 512 * gr:HEAD_COLS + 512 * gr + 512] if isinstance(gr, int)
                       else ada_v[n, :, :, bass.ds(gr * 512 + HEAD_COLS, 512)])
                pool.dma_start(ada_ring[:, n % 2, :].rearrange("p (k n) -> p k n", n=512), src).then_inc(ada_in[n % 2], 16)

            pool.wait_ge(rstd_done, 1)
            for m in range(KD):
                pool.wait_ge(xg_done, m + 1)
                g.tensor_tensor(nx[:, m, :], nx[:, m, :], ssq[:], ALU.mult).then_inc(nx_done, 1)
            pool.wait_ge(shift_in[KD - 1], 16)
            for n in range(4):
                ada_load(0, n, 2 * n - 2 if n >= 2 else None)
            with pool.Fori(1, LOOP_GROUPS) as i:
                for n in range(4):
                    ada_load(i, n, i * 8 + (2 * n - 2))
            def add_squares(q):
                for o in range(1, KD - 2):
                    pool.wait_ge(sq_done, KD * q + o + 1)
                    if o >= 2:
                        pool.wait_ge(ssq_done, (KD - 3) * (q - 1) + o - 1)
                    g.tensor_tensor(ssq[:], ssq[:], nt[:, o % 2, :], ALU.add).then_inc(ssq_done, 1)

            add_squares(1)
            pool.wait_ge(hi_done, U_QD + 1)
            pool.wait_ge(lo_done, U_QD)
            g.tensor_tensor(w_lo[U_QD % 2][:, 0:2048], raw[U_QD % 2][:, 0:2048], w_hi[U_QD % 2][:, 0:2048].bitcast(F32),
                            ALU.subtract).then_inc(lo_done, 1)
            pool.wait_ge(n_lo_done, 2 * KD)
            g.iota(dist[:], pattern=[[1, S]], base=0, channel_multiplier=-1,
                   allow_small_or_imprecise_dtypes=True).then_inc(consts, 1)
            pool.wait_ge(consts, 15)
            g.affine_select(out=R[:, 0:P], in_=dist[:, 0:P], compare_op=ALU.is_ge, fill=NEG, base=0,
                            pattern=[[-1, P]], channel_multiplier=1).then_inc(consts, 1)
            for gr in range(LOOP_GROUPS, GROUPS):
                for n in range(4):
                    ada_load(gr, n, 8 * gr + 2 * n - 2)
            for n, i in enumerate((1, 2, 3)):
                pool.wait_ge(score_add, NH * (n + 1))
                d = score[:, S_OFF[i] + i * P:S_OFF[i] + (i + 1) * P]
                g.affine_select(out=d, in_=d, compare_op=ALU.is_ge, fill=NOT_CAUSAL, base=0,
                                pattern=[[-1, P]], channel_multiplier=1).then_inc(causal, 1)
            add_squares(2)

        @block.scalar
        def _(act):
            a = nc.scalar
            a.preload_act_table(ACT.Silu)
            dma_rows = [(C_G, 8, g_ffn1[0].rearrange("(r q) -> r q", q=P)),
                        (C_G + 8, 8, g_mix[0].rearrange("(r q) -> r q", q=P)),
                        (C_G + 16, 8, g_ffn2[0].rearrange("(r q) -> r q", q=P)),
                        (C_BGATE, 16, b_gate[0].rearrange("(r q) -> r q", q=P))]
            for r0, n, src in dma_rows:
                act.dma_start(rows[r0:r0 + n, :], src).then_inc(rows_in, 16)
            for r0, src in ((C_GQ, g_q_dsa), (C_GK, g_k_dsa)):
                act.dma_start(rows[r0:r0 + 1, :].rearrange("p (a n) -> p a n", n=HD),
                              src.unsqueeze(1).to_broadcast([1, 2, HD])).then_inc(rows_in, 16)

            def hi(u):
                act.wait_ge(raw_in[u % 2], arrived(u))
                if u >= 2:
                    act.wait_ge(tiles, before(u - 1))
                n = size(u)
                a.activation(w_hi[u % 2][:, 0:n], raw[u % 2][:, 0:n], ACT.Copy).then_inc(hi_done, 1)

            def hi_in_loop(i, u, signals):
                act.wait_ge(raw_in[u % 2], i * 16 + arrived(u))
                act.wait_ge(tiles, i * signals + before(u - 1))
                a.activation(w_hi[u % 2][:, 0:2048], raw[u % 2][:, 0:2048], ACT.Copy).then_inc(hi_done, 1)

            def squares(q, o):
                act.wait_ge(h_done, KD * q + o + 1)
                if o >= 3:
                    act.wait_ge(ssq_done, (KD - 3) * (q - 1) + o - 2)
                a.activation(ssq[:] if o == 0 else nt[:, o % 2, :], h[:, ORDERS[q][o], :], ACT.Square).then_inc(sq_done, 1)

            def norm_std(q):
                act.wait_ge(sum_done, q + 1)
                a.activation(ssq[:], ps[:, 4, :], ACT.Sqrt, bias=eps[:]).then_inc(std_done, 1)

            def norm_apply(q):
                act.wait_ge(mod_done, q + 2)
                for m in range(KD):
                    act.wait_ge(nx_done, KD * q + m + 1)
                    a.activation(n_hi[:, m, :], nx[:, m, :], ACT.Identity,
                                 bias=mod[:, 24 * q + m:24 * q + m + 1]).then_inc(n_hi_done, 1)

            def ffn(f):
                u0 = (0, U_FFN2)[f]
                j0 = KF * f
                with act.Fori(0, UP_PAIRS) as i:
                    hi_in_loop(i, u0 + 1, 4)
                    for t in range(2):
                        act.wait_ge(tiles, i * 4 + tile_at(u0, t))
                        act.wait_ge(mid_lo_done, i * 2 + (j0 + t + 1))
                        a.activation(nt[:, t, :], ps[:, t, :], ACT.Silu).then_inc(silu_done, 1)
                        if t == 0:
                            hi_in_loop(i, u0 + 2, 4)
                    if f == 0:
                        act.wait_ge(ada_mac, i * 8 + 8)
                        a.activation(acc_hi[:], ada_acc[:], ACT.Copy).then_inc(acc_hi_done, 1)
                    for t in range(2):
                        act.wait_ge(mul_done, i * 2 + (j0 + t + 3))
                        a.activation(mid_hi[:, bass.ds(i * 2 + t, 1), :], nt[:, t:t + 1, :], ACT.Copy).then_inc(mid_hi_done, 1)
                with act.Fori(0, (UP_PAIRS - 1) // 2) as i:
                    hi_in_loop(i, u0 + 2 * UP_PAIRS + 1, 2)
                    hi_in_loop(i, u0 + 2 * UP_PAIRS + 2, 2)

            act.wait_ge(consts, 5)
            act.wait_ge(cols_done, 1)
            a.activation(sc[:], cols[:, C_C:C_C + KD], ACT.Silu).then_inc(silu_c, 1)
            a.preload_act_table(ACT.Sqrt)
            for m in range(KD):
                act.wait_ge(x_t, m + 1)
                a.activation(h[:, m, :], ps[:, X_BANKS[m % 4], :], ACT.Copy).then_inc(h_done, 1)
                if m >= 2:
                    act.wait_ge(sq_used, m - 1)
                a.activation(nt[:, m % 2, :], ps[:, X_BANKS[m % 4], :], ACT.Square).then_inc(sq_done, 1)
            norm_std(0)
            a.preload_act_table(ACT.Silu)
            act.wait_ge(coef, 1)
            for m in range(KD):
                a.activation(nx[:, m, :], h[:, m, :], ACT.Copy, scale=nscale[:, 0, m:m + 1]).then_inc(xg_done, 1)
            act.wait_ge(first_in, 16)
            a.activation(w_hi[0][:, 0:1024], raw[0][:, 0:1024], ACT.Copy).then_inc(first_hi, 1)
            act.wait_ge(raw_in[0], 16)
            a.activation(w_hi[0][:, 1024:2048], raw[0][:, 1024:2048], ACT.Copy).then_inc(hi_done, 1)
            norm_apply(0)
            ffn(0)
            hi(U_X)
            a.preload_act_table(ACT.Sqrt)
            for o in range(KD):
                squares(1, o)
            norm_std(1)
            hi(U_QD)
            norm_apply(1)

            for y in range(2):
                act.wait_ge(tiles, tile_at(U_X, y))
                src = ps[:, 1 + y, 0:2 * XC].rearrange("p (b n) -> p b n", n=XC)[:, :, 0:HD]
                a.activation(sqt[:, y * P:(y + 1) * P].rearrange("p (b n) -> p b n", n=HD), src,
                             ACT.Square).then_inc(ksq_done, 1)
            hi(U_QD + 1)
            act.wait_ge(kss_done, 1)
            a.activation(kr[:], kr[:], ACT.Sqrt, bias=eps[:], scale=1.0 / HD).then_inc(kstd_done, 1)
            hi(U_QI)
            for j in range(NB):
                act.wait_ge(tiles, tile_at(U_QD + 1, j))
                if j == 0:
                    act.wait_ge(kss_done, 1)
                else:
                    act.wait_ge(qss_done, j)
                a.activation(sqt[:], ps[:, 4 + j, :], ACT.Square).then_inc(qsq_done, 1)
            act.wait_ge(kn_t, 1)
            a.activation(kd_hi[:], ps[:, 3, :], ACT.Copy, scale=cols[:, C_GK:C_GK + 1]).then_inc(kd_hi_done, 1)
            act.wait_ge(ki_t, 1)
            a.activation(ki_hi[:], ps[:, 2, :], ACT.Copy).then_inc(ki_done, 1)
            act.wait_ge(qss_done, NB)
            a.activation(qr[:], qr[:], ACT.Sqrt, bias=eps[:], scale=1.0 / HD).then_inc(qstd_done, 1)
            hi(U_QI + 1)
            for t in range(4):
                if t == 2:
                    hi(U_QSB)
                act.wait_ge(tiles, tile_at(U_QI, t))
                for hd, own, _ in qi_parts(t):
                    a.activation(qi2[hd // 4][own, hd % 4, :], ps[own, t % 2, :], ACT.Copy).then_inc(qi_hi_done, 1)
                if t % 2:
                    for j in (t - 1, t):
                        act.wait_ge(qn_t, j + 1)
                        for n, (own, _) in enumerate(HALVES):
                            a.activation(qd2_heads(j, own, n), ps[own, 2 + j % 2, :].rearrange("p (t q) -> p t q", q=P),
                                         ACT.Copy, scale=cols[own, C_GQ:C_GQ + 1]).then_inc(qd_hi_done, 1)
            for t in range(8):
                if t % 2 == 0:
                    hi(U_QSB + 1 + t // 2)
                act.wait_ge(tiles, tile_at(U_QSB, t))
                dst = (qsbT if t < 4 else ksbT)[:, t % 4, :]
                a.activation(dst, ps[:, t % 4, :], ACT.Copy, scale=HD ** -0.5 if t < 4 else 1.0).then_inc(sbp_done, 1)
                for s in range(3 * t, 3 * t + 3):
                    n = (IDX[s][0] + 1) * P
                    act.wait_ge(idx_mm, s + 1)
                    if s >= 2:
                        act.wait_ge(score_add, s - 1)
                    a.activation(relu[:, s % 2, 0:n], ps[:, 4 + s % 4, 0:n], ACT.Relu).then_inc(relu_done, 1)
            hi(U_VSB + 1)
            hi(U_GATE)
            for j in range(NB):
                act.wait_ge(tiles, tile_at(U_VSB + 1, j))
                a.activation(vsb[:, j, :], ps[:, 4 + j, :], ACT.Copy).then_inc(vsb_done, 1)

            def soft(s):
                i = s // NH
                n = (i + 1) * P
                act.wait_ge(ttr_done, s + 1)
                a.activation(lgb[:, s % 2, 0:n], lgb[:, s % 2, 0:n], ACT.Exp, bias=negmax[:, s:s + 1], scale=-1.0,
                             accum_out=psum_p[:, s:s + 1]).then_inc(p_done, 1)

            def ydT_copy(i):
                act.wait_ge(yd_t, i + 1)
                a.activation(ydT[:, :, i * P:(i + 1) * P], ps[:, B_F, :].rearrange("p (t q) -> p t q", q=P),
                             ACT.Copy).then_inc(ydT_done, 1)

            a.preload_act_table_set("natural_log_exp_and_others")
            a.activation(neg_tri_r[:], neg_tri[:], ACT.Copy).then_inc(round_done, 1)
            a.activation(neg_ones_r[:], neg_ones[:], ACT.Copy).then_inc(round_done, 1)
            for hd in range(NH):
                act.wait_ge(z_done, hd + 1)
                if hd:
                    act.wait_ge(pv_done, hd)
                a.activation(sp_a[:], psf[:, 0:ZW], ACT.Abs).then_inc(ln_step, 1)
                act.wait_ge(ln_step, 3 * hd + 1)
                a.activation(sp_a[:], sp_a[:], ACT.Exp, scale=-1.0).then_inc(ln_step, 1)
                act.wait_ge(ln_step, 3 * hd + 2)
                a.activation(sp_a[:], sp_a[:], ACT.Ln, bias=1.0).then_inc(ln_step, 1)
                soft(4 * hd)
                act.wait_ge(sp_done, 2 * hd + 1)
                if hd:
                    act.wait_ge(suf_done, hd)
                a.activation(sp_hi1[:], sp_a[:, S:ZW], ACT.Copy).then_inc(sp_hi_done, 1)
                act.wait_ge(sp_done, 2 * hd + 2)
                a.activation(sp_hi0[:], sp_a[:, 0:S], ACT.Copy).then_inc(sp_hi_done, 1)
                hi(U_GATE + 1 + hd)
                soft(4 * hd + 1)
                act.wait_ge(suf_done, hd + 1)
                a.activation(sp_a[:], psf[:, 0:ZW], ACT.Exp).then_inc(a_done, 1)
                if hd in (2, 4, 6):
                    ydT_copy(hd // 2 - 1)
                soft(4 * hd + 2)
                soft(4 * hd + 3)
                if hd % 2:
                    act.wait_ge(pv_done, hd + 1)
                    a.activation(ysb_hi[:, hd // 2, :], ps[:, B_Y, :], ACT.Copy).then_inc(ysb_hi_done, 1)
            hi(U_PROJ + 1)
            a.preload_act_table(ACT.Sigmoid)
            act.wait_ge(gate_done, 16)

            def sigmoids(m0):
                for m in range(m0, m0 + 4):
                    a.activation(gates[:, m, :], gates[:, m, :], ACT.Sigmoid).then_inc(sig_done, 1)

            sigmoids(0)
            ydT_copy(3)
            act.wait_ge(ydT_done, 4)
            a.activation(yd_hi[:], ydT[:], ACT.Copy).then_inc(yd_hi_done, 1)
            sigmoids(8)
            sigmoids(4)
            sigmoids(12)
            hi(U_PROJ + 2)
            for m in range(KD):
                if m == 4:
                    hi(U_PROJ + 3)
                    hi(U_OUT)
                act.wait_ge(mg_done, m + 1)
                a.activation(n_hi[:, m, :], gates[:, 8 + m, :], ACT.Copy).then_inc(mg_hi_done, 1)
            a.preload_act_table(ACT.Sqrt)
            hi(U_OUT + 1)
            for o in range(KD):
                if o == 2:
                    hi(U_OUT + 2)
                if o == 4:
                    hi(U_OUT + 3)
                if o == 6:
                    hi(U_FFN2)
                squares(2, o)
            norm_std(2)
            a.preload_act_table(ACT.Silu)
            norm_apply(2)
            ffn(1)
            for o, m in enumerate(W2_ORDER):
                act.wait_ge(h_t, o + 1)
                if o >= 4:
                    act.wait_ge(out_in[o % 4], 16)
                a.activation(outb[:, o % 4], ps[:, m, :].rearrange("p (j q) -> p j q", q=P), ACT.Copy).then_inc(out_copy, 1)

        @block.vector
        def _(dve):
            v = nc.vector

            def lo(u):
                dve.wait_ge(hi_done, u + 1)
                n = size(u)
                v.tensor_tensor(w_lo[u % 2][:, 0:n], raw[u % 2][:, 0:n], w_hi[u % 2][:, 0:n].bitcast(F32),
                                ALU.subtract).then_inc(lo_done, 1)

            def lo_in_loop(i, u):
                dve.wait_ge(hi_done, i * 2 + (u + 1))
                v.tensor_tensor(w_lo[u % 2][:, 0:2048], raw[u % 2][:, 0:2048], w_hi[u % 2][:, 0:2048].bitcast(F32),
                                ALU.subtract).then_inc(lo_done, 1)

            def norm_rstd(q):
                dve.wait_ge(std_done, q + 1)
                v.reciprocal(ssq[:], ssq[:]).then_inc(rstd_done, 1)

            def norm_x(q, m):
                if m == 0:
                    dve.wait_ge(rstd_done, q + 1)
                    dve.wait_ge(coef, (1, 3, 5)[q])
                v.scalar_tensor_tensor(out=nx[:, m, :], in0=h[:, m, :], scalar=nscale[:, q, m:m + 1], in1=ssq[:],
                                       op0=ALU.mult, op1=ALU.mult).then_inc(nx_done, 1)

            def norm_lo(q, m):
                dve.wait_ge(n_hi_done, KD * q + m + 1)
                v.scalar_tensor_tensor(out=n_lo[:, m, :], in0=nx[:, m, :], scalar=mod[:, 24 * q + m:24 * q + m + 1],
                                       in1=n_hi[:, m, :].bitcast(F32), op0=ALU.add, op1=ALU.subtract).then_inc(n_lo_done, 1)

            def norm_apply(q):
                norm_x(q, 0)
                norm_x(q, 1)
                norm_lo(q, 0)
                norm_x(q, 2)
                for m in range(1, KD):
                    if m + 2 < KD:
                        norm_x(q, m + 2)
                    norm_lo(q, m)

            def scale_of(q):
                v.scalar_tensor_tensor(out=nscale[:, q, :], in0=mod[:, 24 * q + 8:24 * q + 16], scalar=1.0,
                                       in1=cols[:, C_G + 8 * q:C_G + 8 * q + 8], op0=ALU.add, op1=ALU.mult).then_inc(coef, 1)

            def ada_group(acc, arrive, mac_at, ks=range(KD)):
                for k in ks:
                    if k % 2 == 0:
                        dve.wait_ge(ada_in[k // 2 % 2], arrive + 16 * (k // 4))
                    w = ada_ring[:, k // 2 % 2, 512 * (k % 2):512 * (k % 2) + 512]
                    if k == 0:
                        v.tensor_scalar(acc, w, sc[:, 0:1], None, ALU.mult).then_inc(ada_mac, 1)
                    else:
                        dve.wait_ge(ada_mac, mac_at + k)
                        v.scalar_tensor_tensor(out=acc, in0=w, scalar=sc[:, k:k + 1], in1=acc,
                                               op0=ALU.mult, op1=ALU.add).then_inc(ada_mac, 1)

            def ada_copy(bank, n, mm):
                dve.wait_ge(ada_mm, mm)
                v.tensor_copy(mod_rows[0:n, :], ps[0:n, bank, :]).then_inc(ada_rows, 1)

            def ada_columns(bank, n, m0, count):
                dve.wait_ge(ada_t, count)
                v.tensor_tensor(mod[:, m0:m0 + 4 * n].rearrange("p (g t) -> p t g", t=4),
                                ps[:, bank, 0:4 * n].rearrange("p (t g) -> p t g", g=n),
                                cols[:, m0:m0 + 4 * n].rearrange("p (g t) -> p t g", t=4), ALU.add).then_inc(mod_done, 1)

            def residual(q, o, bank, gate):
                m = ORDERS[q][o]
                dve.wait_ge(tiles, tile_at((U_X - 1, U_OUT, U_END - 1)[q - 1], o))
                v.scalar_tensor_tensor(out=h[:, m, :], in0=ps[:, bank, :], scalar=gate[:, m:m + 1], in1=h[:, m, :],
                                       op0=ALU.mult, op1=ALU.add).then_inc(h_done, 1)

            def ffn(f):
                u0 = (0, U_FFN2)[f]
                j0 = KF * f
                if f == 0:
                    dve.wait_ge(consts, 14)
                with dve.Fori(0, UP_PAIRS) as i:
                    lo_in_loop(i, u0 + 1)
                    if f == 0:
                        dve.wait_ge(ada_mm, i + 1)
                        dve.wait_ge(now_done, i * 2 + 1)
                        v.tensor_scalar(now[:], turns[:], 0.0, None, ALU.is_equal).then_inc(now_done, 1)
                        ada_group(ada_acc[:], i * 32 + 16, i * 8, range(KD // 2))
                        dve.wait_ge(now_done, i * 2 + 2)
                        v.tensor_scalar(turns[:], turns[:], -1.0, None, ALU.add).then_inc(now_done, 1)
                    lo_in_loop(i, u0 + 2)
                    if f == 0:
                        ada_group(ada_acc[:], i * 32 + 16, i * 8, range(KD // 2, KD))
                        dve.wait_ge(acc_hi_done, i + 1)
                        v.tensor_tensor(acc_lo[:], ada_acc[:], acc_hi[:].bitcast(F32), ALU.subtract).then_inc(acc_lo_done, 1)
                    for t in range(2):
                        dve.wait_ge(tiles, i * 4 + tile_at(u0 + 1, t))
                        dve.wait_ge(silu_done, i * 2 + (j0 + t + 3))
                        v.tensor_tensor(nt[:, t, :], nt[:, t, :], ps[:, 2 + t, :], ALU.mult).then_inc(mul_done, 1)
                    for t in range(2):
                        dve.wait_ge(mid_hi_done, i * 2 + (j0 + t + 1))
                        v.tensor_tensor(mid_lo[:, bass.ds(i * 2 + t, 1), :], nt[:, t:t + 1, :],
                                        mid_hi[:, bass.ds(i * 2 + t, 1), :].bitcast(F32), ALU.subtract).then_inc(mid_lo_done, 1)
                if f == 0:
                    ada_copy(7, LOOP_GROUPS, LOOP_GROUPS + 1)
                    ada_columns(7, LOOP_GROUPS, 16, 1)
                    dve.wait_ge(mod_done, 3)
                    v.tensor_scalar(half_gate[:, 0, :], mod[:, 16:24], 0.5, None, ALU.mult).then_inc(coef, 1)
                    scale_of(1)
                with dve.Fori(0, (UP_PAIRS - 1) // 2) as i:
                    lo_in_loop(i, u0 + 2 * UP_PAIRS + 1)
                    lo_in_loop(i, u0 + 2 * UP_PAIRS + 2)

            v.memset(best[:, 0:1], 0.0).then_inc(tiles, 1)
            v.memset(best[:, 1:2], 0.0).then_inc(silu_done, 2)
            v.memset(best[:, 2:3], 0.0).then_inc(mul_done, 2)
            v.memset(best[:, 3:4], 0.0).then_inc(mid_lo_done, 2)
            v.memset(best[:, 4:5], 0.0).then_inc(ada_mm, 1)
            v.memset(best[:, 5:6], 0.0).then_inc(now_done, 1)
            for hd in range(NH):
                ins = v.memset(slope_inv[:, hd:hd + 1], 2.0 ** (hd + 1) * HD ** -0.5)
            ins.then_inc(coef_q, 1)
            dve.wait_ge(rows_t, 1)
            v.tensor_copy(cols[:], ps[:, 0, 0:C_END]).then_inc(cols_done, 1)
            dve.wait_ge(cols_done, 1)
            def head_macs(c0, arrive, ks, n):
                for k in ks:
                    dve.wait_ge(arrive[k], 16)
                    w, acc = slab[:, k, c0:c0 + D], head_acc[:, c0:c0 + D]
                    if k == 0:
                        v.tensor_scalar(acc, w, sc[:, 0:1], None, ALU.mult).then_inc(head_mac, 1)
                    else:
                        dve.wait_ge(head_mac, n + k)
                        v.scalar_tensor_tensor(out=acc, in0=w, scalar=sc[:, k:k + 1], in1=acc,
                                               op0=ALU.mult, op1=ALU.add).then_inc(head_mac, 1)

            dve.wait_ge(silu_c, 1)
            head_macs(D, scale_in, range(KD), 0)
            norm_rstd(0)
            dve.wait_ge(head_mm, 1)
            v.tensor_tensor(mod[:, 8:16], ps[:, 1, 8:16], cols[:, 8:16], ALU.add).then_inc(mod_done, 1)
            dve.wait_ge(mod_done, 1)
            scale_of(0)
            head_macs(0, shift_in, range(SHIFT_MACS), KD)
            dve.wait_ge(first_hi, 1)
            v.tensor_tensor(w_lo[0][:, 0:1024], raw[0][:, 0:1024], w_hi[0][:, 0:1024].bitcast(F32),
                            ALU.subtract).then_inc(first_lo, 1)
            dve.wait_ge(hi_done, 1)
            v.tensor_tensor(w_lo[0][:, 1024:2048], raw[0][:, 1024:2048], w_hi[0][:, 1024:2048].bitcast(F32),
                            ALU.subtract).then_inc(lo_done, 1)
            dve.wait_ge(head_mm, 2)
            v.tensor_tensor(mod[:, 0:8], ps[:, 0, 0:8], cols[:, 0:8], ALU.add).then_inc(mod_done, 1)
            dve.wait_ge(mod_done, 2)
            for m in range(KD):
                norm_lo(0, m)
            ffn(0)
            dve.wait_ge(coef, 2)
            for o in range(KD):
                residual(1, o, W2_ORDER[o], half_gate[:, 0, :])
            lo(U_X)
            norm_rstd(1)
            norm_apply(1)

            def rest_group(g, ks=range(KD)):
                gr = LOOP_GROUPS + g
                ada_group(ada_rest[:, g, :], 32 * gr + 16, 8 * gr, ks)

            for y in range(2):
                dve.wait_ge(tiles, tile_at(U_X, y))
                dve.wait_ge(ksq_done, 1 + y)
                both = ps[:, 1 + y, 0:2 * XC].rearrange("p (b n) -> p b n", n=XC)
                for dup in range(2):
                    v.tensor_copy(ki[:, 2 * y:2 * y + 2, dup, :], both[:, :, 2 * HD + NH:XC]).then_inc(ki_tok, 1)
                v.tensor_copy(vd[:, 2 * y:2 * y + 2, :], both[:, :, HD:2 * HD]).then_inc(vw_done, 1)
                v.tensor_scalar(wi[:, 2 * y:2 * y + 2, :], both[:, :, 2 * HD:2 * HD + NH],
                                HD ** -0.5 * NH ** -0.5, None, ALU.mult).then_inc(vw_done, 1)
            v.tensor_reduce(kr[:], sqt[:, 0:NB * HD].rearrange("p (b n) -> p b n", n=HD), AX.X, ALU.add).then_inc(kss_done, 1)
            dve.wait_ge(kstd_done, 1)
            v.reciprocal(kr[:], kr[:]).then_inc(kr_done, 1)
            dve.wait_ge(kr_done, 1)
            for y in range(2):
                both = ps[:, 1 + y, 0:2 * XC].rearrange("p (b n) -> p b n", n=XC)
                for dup in range(2):
                    v.tensor_tensor(kn[:, 2 * y:2 * y + 2, dup, :], both[:, :, 0:HD],
                                    kr[:, 2 * y:2 * y + 2].unsqueeze(2).to_broadcast([P, 2, HD]), ALU.mult).then_inc(kn_done, 1)
            dve.wait_ge(lo_done, U_QD + 1)
            lo(U_QD + 1)
            rest_group(0)
            lo(U_QI)
            for j in range(NB):
                dve.wait_ge(qsq_done, j + 1)
                v.tensor_reduce(qr[:, j * NH:(j + 1) * NH], sqt[:].rearrange("p (b n) -> p b n", n=HD),
                                AX.X, ALU.add).then_inc(qss_done, 1)
            dve.wait_ge(kn_t, 1)
            dve.wait_ge(kd_hi_done, 1)
            v.scalar_tensor_tensor(out=kd_lo[:], in0=ps[:, 3, :], scalar=cols[:, C_GK:C_GK + 1], in1=kd_hi[:].bitcast(F32),
                                   op0=ALU.mult, op1=ALU.subtract).then_inc(kd_lo_done, 1)
            dve.wait_ge(qstd_done, 1)
            v.reciprocal(qr[:], qr[:]).then_inc(qr_done, 1)
            dve.wait_ge(qr_done, 1)
            dve.wait_ge(coef_q, 1)
            by_block = qr[:].rearrange("p (b n) -> p b n", n=NH)
            v.tensor_tensor(by_block, by_block, slope_inv[:].unsqueeze(1).to_broadcast([P, NB, NH]), ALU.mult).then_inc(qr_done, 1)
            dve.wait_ge(qr_done, 2)

            def qi_low(t):
                for hd, own, other in qi_parts(t):
                    dve.wait_ge(qi_hi_done, hd + 1)
                    v.tensor_tensor(qi2[hd // 4][other, hd % 4, :], ps[own, t % 2, :],
                                    qi2[hd // 4][own, hd % 4, :].bitcast(F32), ALU.subtract).then_inc(qi_lo_done, 1)

            def q_norm(j):
                if j >= 2:
                    dve.wait_ge(qn_t, j - 1)
                v.tensor_tensor(qn[:, j % 2, :].rearrange("p (b n) -> p b n", n=HD),
                                ps[:, 4 + j, :].rearrange("p (b n) -> p b n", n=HD),
                                qr[:, j * NH:(j + 1) * NH].unsqueeze(2).to_broadcast([P, NH, HD]), ALU.mult).then_inc(qn_done, 1)

            def q_store(j):
                for n, (own, other) in enumerate(HALVES):
                    dve.wait_ge(qd_hi_done, 2 * j + n + 1)
                    v.scalar_tensor_tensor(out=qd2_heads(j, other, n), in0=ps[own, 2 + j % 2, :].rearrange("p (t q) -> p t q", q=P),
                                           scalar=cols[own, C_GQ:C_GQ + 1], in1=qd2_heads(j, own, n).bitcast(F32),
                                           op0=ALU.mult, op1=ALU.subtract).then_inc(qd_lo_done, 1)

            q_norm(0)
            q_norm(1)
            dve.wait_ge(ki_done, 1)
            v.tensor_tensor(ki_lo[:], ps[:, 2, :], ki_hi[:].bitcast(F32), ALU.subtract).then_inc(ki_lo_done, 1)
            qi_low(0)
            lo(U_QI + 1)
            qi_low(1)
            q_store(0)
            q_norm(2)
            q_store(1)
            q_norm(3)
            lo(U_QSB)
            qi_low(2)
            qi_low(3)
            q_store(2)
            q_store(3)
            def add_score(s):
                i, hd = IDX[s]
                n = (i + 1) * P
                acc = score[:, S_OFF[i]:S_OFF[i] + n]
                dve.wait_ge(relu_done, s + 1)
                w = wi[:, i, hd:hd + 1]
                if hd == 0:
                    v.tensor_scalar(acc, relu[:, s % 2, 0:n], w, 0.0, ALU.mult, ALU.add).then_inc(score_add, 1)
                else:
                    dve.wait_ge(score_add, s)
                    v.scalar_tensor_tensor(out=acc, in0=relu[:, s % 2, 0:n], scalar=w, in1=acc,
                                           op0=ALU.mult, op1=ALU.add).then_inc(score_add, 1)

            top_count = [0]

            def take(i):
                n = (i + 1) * P
                acc = score[:, S_OFF[i]:S_OFF[i] + n]
                if top_count[0] % (2 * ROUNDS) == 0:
                    dve.wait_ge(causal, i)
                    dve.wait_ge(consts, 16)
                if top_count[0]:
                    dve.wait_ge(top, top_count[0])
                v.max(best[:], acc).then_inc(top, 1)
                dve.wait_ge(top, top_count[0] + 1)
                v.match_replace(acc, best[:], acc, TAKEN).then_inc(top, 1)
                top_count[0] += 2
                if top_count[0] % (2 * ROUNDS) == 0:
                    r = R[:, R_OFF[i]:R_OFF[i] + n]
                    dve.wait_ge(top, top_count[0])
                    v.tensor_scalar(r, acc, (TAKEN + NOT_CAUSAL) / 2, NEG, ALU.is_gt, ALU.mult).then_inc(r_step, 1)
                    dve.wait_ge(r_step, i)
                    v.scalar_tensor_tensor(out=r, in0=dist[:, 0:n], scalar=float(-P * i), in1=r,
                                           op0=ALU.add, op1=ALU.add).then_inc(r_done, 1)

            rounds = [1] * ROUNDS + [2] * ROUNDS + [3] * ROUNDS
            taken = [0]

            def takes(n):
                for i in rounds[taken[0]:taken[0] + n]:
                    take(i)
                taken[0] += n

            for t in range(8):
                if t % 2 == 0:
                    lo(U_QSB + 1 + t // 2)
                for s in range(3 * t, 3 * t + 3):
                    add_score(s)
                if t < 4:
                    rest_group(1 + t // 2, range(KD // 2 * (t % 2), KD // 2 * (t % 2 + 1)))
                if t >= 3:
                    takes(3 if t > 3 else 2)
            lo(U_VSB + 1)
            ada_copy(3, REST, LOOP_GROUPS + 2)
            ada_columns(3, REST, 16 + 4 * LOOP_GROUPS, 2)
            dve.wait_ge(mod_done, 4)
            scale_of(2)
            v.tensor_scalar(half_gate[:, 1, :], mod[:, 64:72], 0.5, None, ALU.mult).then_inc(coef, 1)
            takes(10)
            lo(U_GATE)

            def logits_max(s):
                i, hd = divmod(s, NH)
                n = (i + 1) * P
                dve.wait_ge(lg_done, s + 1)
                if s == 0:
                    dve.wait_ge(consts, 16)
                if hd == 0 and i:
                    dve.wait_ge(r_done, i)
                if s >= 2:
                    dve.wait_ge(p_t, s - 1)
                v.tensor_tensor_reduce(lgb[:, s % 2, 0:n], ps[:, B_LG, 0:n], R[:, R_OFF[i]:R_OFF[i] + n],
                                       -(2.0 ** -(hd + 1)), 3e38, ALU.add, ALU.min, negmax[:, s:s + 1]).then_inc(ttr_done, 1)

            def pT_copy(s):
                n = (s // NH + 1) * P
                dve.wait_ge(p_t, s + 1)
                if s >= 2:
                    dve.wait_ge(pvd_done, s - 1)
                v.tensor_copy(pT[:, s % 2, 0:n], ps[:, B_PT, 0:n]).then_inc(pT_done, 1)

            def gate_store(m):
                dve.wait_ge(tiles, tile_at(U_GATE, m))
                v.tensor_scalar(gates[:, m, :], ps[:, B_F, :], cols[:, C_BGATE + m:C_BGATE + m + 1], None,
                                ALU.add).then_inc(gate_done, 1)

            def yd_norm(i):
                dve.wait_ge(pvd_done, NH * (i + 1))
                v.reciprocal(pinv[:, NH * i:NH * (i + 1)], psum_p[:, NH * i:NH * (i + 1)]).then_inc(pinv_done, 1)
                dve.wait_ge(pinv_done, i + 1)
                if i:
                    dve.wait_ge(yd_t, i)
                v.tensor_tensor(ydtok[:].rearrange("p (b n) -> p b n", n=HD), ps[:, B_O, :].rearrange("p (b n) -> p b n", n=HD),
                                pinv[:, NH * i:NH * (i + 1)].unsqueeze(2).to_broadcast([P, NH, HD]), ALU.mult).then_inc(ydn_done, 1)

            for hd in range(NH):
                if hd:
                    pT_copy(4 * hd - 1)
                logits_max(4 * hd)
                dve.wait_ge(ln_step, 3 * hd + 3)
                for c in (slice(S, ZW), slice(0, S)):
                    v.scalar_tensor_tensor(out=sp_a[:, c], in0=psf[:, c], scalar=0.0, in1=sp_a[:, c], op0=ALU.max,
                                           op1=ALU.add).then_inc(sp_done, 1)
                dve.wait_ge(sp_hi_done, 2 * hd + 1)
                v.tensor_tensor(sp_lo[:, S:ZW], sp_a[:, S:ZW], sp_hi1[:].bitcast(F32), ALU.subtract).then_inc(sp_lo_done, 1)
                dve.wait_ge(sp_hi_done, 2 * hd + 2)
                v.tensor_tensor(sp_lo[:, 0:S], sp_a[:, 0:S], sp_hi0[:].bitcast(F32), ALU.subtract).then_inc(sp_lo_done, 1)
                gate_store(2 * hd)
                pT_copy(4 * hd)
                logits_max(4 * hd + 1)
                if hd in (2, 4, 6):
                    yd_norm(hd // 2 - 1)
                lo(U_GATE + 1 + hd)
                pT_copy(4 * hd + 1)
                logits_max(4 * hd + 2)
                if hd < 6:
                    takes(2)
                gate_store(2 * hd + 1)
                pT_copy(4 * hd + 2)
                logits_max(4 * hd + 3)
                if hd < 6:
                    takes(2 if taken[0] < len(rounds) - 1 else 0)
                if hd % 2:
                    dve.wait_ge(ysb_hi_done, hd // 2 + 1)
                    v.tensor_tensor(ysb_lo[:, hd // 2, :], ps[:, B_Y, :], ysb_hi[:, hd // 2, :].bitcast(F32),
                                    ALU.subtract).then_inc(ysb_lo_done, 1)
            assert taken[0] == len(rounds)
            pT_copy(31)
            lo(U_PROJ + 1)
            yd_norm(3)

            def gated_sb(m):
                dve.wait_ge(tiles, tile_at(U_PROJ + 2 * (m // 4), m % 4))
                dve.wait_ge(sig_done, m + 1 if m < 4 else m + 5)
                v.tensor_tensor(gates[:, m, :], gates[:, m, :], ps[:, m % 4, :], ALU.mult).then_inc(gy_done, 1)

            def merged(m):
                dve.wait_ge(tiles, tile_at(U_PROJ + 2 * (m // 4) + 1, m % 4))
                dve.wait_ge(sig_done, m + 5 if m < 4 else m + 9)
                g = gates[:, 8 + m, :]
                v.tensor_tensor(g, g, ps[:, 4 + m % 4, :], ALU.mult).then_inc(gz_done, 1)
                dve.wait_ge(gz_done, m + 1)
                dve.wait_ge(gy_done, m + 1)
                v.tensor_tensor(g, g, gates[:, m, :], ALU.add).then_inc(mg_done, 1)

            def merged_lo(m):
                dve.wait_ge(mg_hi_done, m + 1)
                v.tensor_tensor(n_lo[:, m, :], gates[:, 8 + m, :], n_hi[:, m, :].bitcast(F32), ALU.subtract).then_inc(mg_lo_done, 1)

            for half in range(2):
                for m in range(4 * half, 4 * half + 4):
                    gated_sb(m)
                    if m == 1:
                        dve.wait_ge(yd_hi_done, 1)
                        v.tensor_tensor(yd_lo[:], ydT[:], yd_hi[:].bitcast(F32), ALU.subtract).then_inc(yd_lo_done, 1)
                    if m == 4 * half + 3:
                        lo(U_PROJ + 2 if half == 0 else U_OUT)
                for m in range(4 * half, 4 * half + 4):
                    merged(m)
                    if m > 4 * half:
                        merged_lo(m - 1)
                merged_lo(4 * half + 3)
                lo(U_PROJ + 3 if half == 0 else U_OUT + 1)
            for o in range(KD):
                if o == 2:
                    lo(U_OUT + 2)
                if o == 4:
                    lo(U_OUT + 3)
                if o == 6:
                    lo(U_FFN2)
                residual(2, o, o, mod[:, 40:48])
            norm_rstd(2)
            norm_apply(2)
            ffn(1)
            for o in range(KD):
                residual(3, o, W2_ORDER[o], half_gate[:, 1, :])

        @block.tensor
        def _(pe):
            def mm3(dst, whi, wlo, xhi, xlo, first, last):
                pe.matmul(dst, whi, xhi, start=first, stop=False, skip_group_check=True)
                pe.matmul(dst, whi, xlo, start=False, stop=False, skip_group_check=True)
                return pe.matmul(dst, wlo, xhi, start=False, stop=last, skip_group_check=True)

            def column_tile(u, bank, t, act_hi, act_lo, width=256, nk=KD, step=None):
                for k in range(nk):
                    if step is not None:
                        pe.wait_ge(step[0], step[1] + k)
                    w = slice(k * width + t * P, k * width + (t + 1) * P)
                    ins = mm3(ps[:, bank, :], w_hi[u % 2][:, w], w_lo[u % 2][:, w], act_hi[:, k, :], act_lo[:, k, :],
                              k == 0, k == nk - 1)
                return ins

            def token_tile(u, dst, j, w0, n, width, ks, k0, first, last):
                for k in ks:
                    w = slice((k - k0) * width + w0, (k - k0) * width + w0 + n)
                    tok = slice(j * P, (j + 1) * P)
                    f, l = first and k == ks[0], last and k == ks[-1]
                    pe.matmul(dst, n_hi[:, k, tok], w_hi[u % 2][:, w], start=f, stop=False, skip_group_check=True)
                    pe.matmul(dst, n_hi[:, k, tok], w_lo[u % 2][:, w], start=False, stop=False, skip_group_check=True)
                    ins = pe.matmul(dst, n_lo[:, k, tok], w_hi[u % 2][:, w], start=False, stop=l, skip_group_check=True)
                return ins

            def norm_sum(q):
                pe.wait_ge(ssq_done, (KD - 3) * q)
                pe.wait_ge(h_done, KD * q + ORDERS[q].index(4) + 1)
                pe.matmul(ps[:, 4, :], share[:], ssq[:], start=True, stop=False)
                pe.wait_ge(sq_done, KD * (q + 1) - 1)
                pe.matmul(ps[:, 4, :], share[:], nt[:, KD % 2, :], start=False, stop=False)
                pe.wait_ge(sq_done, KD * (q + 1))
                pe.matmul(ps[:, 4, :], share[:], nt[:, (KD - 1) % 2, :], start=False, stop=True).then_inc(sum_done, 1)

            def ada_turn(bank, n, count):
                pe.wait_ge(ada_rows, count)
                for t in range(4):
                    ins = pe.transpose(ps[:, bank, t * n:(t + 1) * n], mod_rows[0:n, t * P:(t + 1) * P], ident[0:n, 0:n])
                ins.then_inc(ada_t, 1)

            def ffn(f):
                u0 = (0, U_FFN2)[f]
                j0 = KF * f
                with pe.Fori(0, UP_PAIRS) as i:
                    for r in range(2):
                        u = u0 + r
                        pe.wait_ge(lo_done, i * 2 + (u + 1))
                        pe.wait_ge((silu_done, mul_done)[r], i * 2 + (j0 + 2))
                        if r == 0:
                            for k in range(KD):
                                pe.wait_ge(n_lo_done, KD * 2 * f + k + 1)
                                for t in range(2):
                                    w = slice(k * 256 + t * P, k * 256 + (t + 1) * P)
                                    ins = mm3(ps[:, t, :], w_hi[u % 2][:, w], w_lo[u % 2][:, w], n_hi[:, k, :],
                                              n_lo[:, k, :], k == 0, k == KD - 1)
                                    if k == KD - 1:
                                        ins.then_inc(tiles, 1)
                        else:
                            for t in range(2):
                                column_tile(u, 2 + t, t, n_hi, n_lo).then_inc(tiles, 1)
                    if f == 0:
                        pe.wait_ge(acc_lo_done, i + 1)
                        pe.wait_ge(now_done, i * 2 + 2)
                        pe.matmul(ps[0:LOOP_GROUPS, 7, :], now[:], acc_hi[:], start=False, stop=False,
                                  skip_group_check=True)
                        pe.matmul(ps[0:LOOP_GROUPS, 7, :], now[:], acc_lo[:], start=False, stop=False,
                                  skip_group_check=True).then_inc(ada_mm, 1)
                u1 = u0 + 2 * UP_PAIRS

                def down(u, k_at, first=False, last=False):
                    for o, m in enumerate(W2_ORDER):
                        if first and m == 0 and f == 0:
                            ada_turn(7, LOOP_GROUPS, 1)
                        if first and m == 7 and f == 0:
                            pe.wait_ge(mod_done, 3)
                        if first and m == 0:
                            pe.wait_ge(silu_done, j0 + KF + 2)
                        if first and m == 2:
                            pe.wait_ge(mul_done, j0 + KF + 2)
                        for k in range(2):
                            w = slice(k * D + m * P, k * D + (m + 1) * P)
                            ins = mm3(ps[:, m, :], w_hi[u % 2][:, w], w_lo[u % 2][:, w], mid_hi[:, k_at(k), :],
                                      mid_lo[:, k_at(k), :], first and k == 0, last and k == 1)
                        if last or m == W2_ORDER[-1]:
                            ins.then_inc(tiles, 1)
                        if last and f == 1 and o >= 2:
                            out_tile(o - 2)

                def out_tile(o):
                    m = W2_ORDER[o]
                    pe.wait_ge(h_done, KD * 3 + o + 1)
                    for j in range(NB):
                        ins = pe.transpose(ps[:, m, j * P:(j + 1) * P], h[:, m, j * P:(j + 1) * P], ident[:])
                    ins.then_inc(h_t, 1)

                pe.wait_ge(lo_done, u1 + 1)
                pe.wait_ge(mid_lo_done, j0 + 2 + 2)
                down(u1, lambda k: slice(k, k + 1), first=True)
                pe.wait_ge(mid_lo_done, j0 + KF + 2)
                with pe.Fori(0, (UP_PAIRS - 3) // 2) as i:
                    for r in range(2):
                        pe.wait_ge(lo_done, i * 2 + (u1 + 2 + r))
                        down(u1 + 1 + r, lambda k: bass.ds(i * 4 + (2 + 2 * r + k), 1))
                for n in (UP_PAIRS - 2, UP_PAIRS - 1):
                    pe.wait_ge(lo_done, u1 + n + 1)
                    down(u1 + n, lambda k: slice(2 * n + k, 2 * n + k + 1), last=n == UP_PAIRS - 1)
                if f == 0:
                    norm_sum(1)
                else:
                    out_tile(KD - 2)
                    out_tile(KD - 1)

            pe.wait_ge(rows_in, 16 * 8)
            pe.wait_ge(consts, 14)
            pe.transpose(ps[:, 0, 0:C_END], rows[:], ident[0:C_END, 0:C_END]).then_inc(rows_t, 1)
            for j in range(NB):
                pe.wait_ge(x_in[j], 16)

            def add_x_square(m):
                pe.wait_ge(sq_done, m + 1)
                pe.matmul(ps[:, 4, :], share[:], nt[:, m % 2, :], start=m == 0, stop=m == KD - 1,
                          skip_group_check=True).then_inc(sum_done if m == KD - 1 else sq_used, 1)

            for m in range(KD):
                if m >= 4:
                    pe.wait_ge(h_done, m - 3)
                    pe.wait_ge(sq_done, m - 3)
                for j in range(NB):
                    ins = pe.transpose(ps[:, X_BANKS[m % 4], j * P:(j + 1) * P], xin[:, j, m * P:(m + 1) * P], ident[:])
                ins.then_inc(x_t, 1)
                if m >= 2:
                    add_x_square(m - 2)
            add_x_square(KD - 2)
            add_x_square(KD - 1)
            for t in range(4):
                pe.matmul(ps[0:LOOP_GROUPS, 7, t * P:(t + 1) * P], zeros[:], ones[:], start=t == 0, stop=False,
                          skip_group_check=True)
            pe.wait_ge(head_mac, KD)
            for t in range(KD):
                ins = pe.matmul(ps[:, 1, 8 + t:9 + t], head_acc[:, D + t * P:D + (t + 1) * P], ones[:, 0:1],
                                start=t == 0, stop=t == KD - 1, skip_group_check=True)
            ins.then_inc(head_mm, 1)
            pe.wait_ge(silu_c, 1)
            for k in list(range(SHIFT_MACS, KD)) + [None]:
                if k is None:
                    pe.wait_ge(head_mac, KD + SHIFT_MACS)
                else:
                    pe.wait_ge(shift_in[k], 16)
                for t in range(KD):
                    w, r = ((head_acc[:, t * P:(t + 1) * P], ones[:, 0:1]) if k is None else
                            (slab[:, k, t * P:(t + 1) * P], sc[:, k:k + 1]))
                    ins = pe.matmul(ps[:, 0, t:t + 1], w, r, start=k == SHIFT_MACS and t == 0,
                                    stop=k is None and t == KD - 1, skip_group_check=True)
            ins.then_inc(head_mm, 1)
            ffn(0)

            u = U_X
            pe.wait_ge(lo_done, u + 1)
            for k in range(KD):
                pe.wait_ge(n_lo_done, KD + k + 1)
                for j in range(NB):
                    ins = token_tile(u, ps[:, 1 + j // 2, (j % 2) * XC:(j % 2 + 1) * XC], j, 0, XC, XC, [k], 0,
                                     k == 0 and j % 2 == 0, k == KD - 1)
                    if k == KD - 1 and j % 2:
                        ins.then_inc(tiles, 1)
            for half in range(2):
                u = U_QD + half
                pe.wait_ge(lo_done, u + 1)
                for j in range(NB):
                    ins = token_tile(u, ps[:, 4 + j, :], j, 0, 512, 512, range(4 * half, 4 * half + 4), 4 * half,
                                     half == 0, half == 1)
                    if half or j == NB - 1:
                        ins.then_inc(tiles, 1)
            pe.wait_ge(kn_done, NB)
            for j in range(NB):
                ins = pe.transpose(ps[:, 3, j * P:(j + 1) * P], kn[:, j].rearrange("p a n -> p (a n)"), ident[:])
            ins.then_inc(kn_t, 1)
            pe.wait_ge(ki_tok, NB)
            for j in range(NB):
                ins = pe.transpose(ps[:, 2, j * P:(j + 1) * P], ki[:, j].rearrange("p a n -> p (a n)"), ident[:])
            ins.then_inc(ki_t, 1)

            def q_turn(j):
                pe.wait_ge(qn_done, j + 1)
                if j == 0:
                    pe.wait_ge(ki_lo_done, 1)
                if j == 1:
                    pe.wait_ge(kd_lo_done, 1)
                if j >= 2:
                    pe.wait_ge(qd_lo_done, 2 * (j - 1))
                for t in range(4):
                    ins = pe.transpose(ps[:, 2 + j % 2, t * P:(t + 1) * P], qn[:, j % 2, t * P:(t + 1) * P], ident[:])
                ins.then_inc(qn_t, 1)

            def qi_tile(t):
                u = U_QI + t // 2
                pe.wait_ge(lo_done, u + 1)
                if t >= 2:
                    pe.wait_ge(qi_lo_done, 2 * (t - 1))
                column_tile(u, t % 2, t % 2, n_hi, n_lo).then_inc(tiles, 1)

            qi_tile(0)
            qi_tile(1)
            q_turn(0)
            q_turn(1)
            qi_tile(2)
            qi_tile(3)
            q_turn(2)
            q_turn(3)

            pe.wait_ge(qi_lo_done, 8)
            for t in range(8):
                u = U_QSB + t // 2
                pe.wait_ge(lo_done, u + 1)
                if t == 2:
                    pe.wait_ge(qd_lo_done, 2 * NB)
                if t >= 4:
                    pe.wait_ge(sbp_done, t - 3)
                column_tile(u, t % 4, t % 2, n_hi, n_lo).then_inc(tiles, 1)
                for s in range(3 * t, 3 * t + 3):
                    i, hd = IDX[s]
                    n = (i + 1) * P
                    if s >= 4:
                        pe.wait_ge(relu_done, s - 3)
                    q = qi2[hd // 4][:, hd % 4, i * P:n]
                    pe.matmul(ps[:, 4 + s % 4, 0:n], q, ki_hi[:, 0:n], start=True, stop=False)
                    pe.matmul(ps[:, 4 + s % 4, 0:n], q, ki_lo[:, 0:n], start=False, stop=True).then_inc(idx_mm, 1)
            pe.wait_ge(ada_mac, 8 * GROUPS)
            pe.wait_ge(sbp_done, 8)
            for gr in range(REST):
                ins = pe.matmul(ps[0:REST, 3, :], pick[:, REST - 1 - gr:2 * REST - 1 - gr], ada_rest[:, gr, :],
                                start=gr == 0, stop=gr == REST - 1, skip_group_check=True)
            ins.then_inc(ada_mm, 1)
            pe.wait_ge(relu_done, len(IDX))
            for half in range(2):
                u = U_VSB + half
                pe.wait_ge(lo_done, u + 1)
                for j in range(NB):
                    ins = token_tile(u, ps[:, 4 + j, :], j, 0, 512, 512, range(4 * half, 4 * half + 4), 4 * half,
                                     half == 0, half == 1)
                    if half or j == NB - 1:
                        ins.then_inc(tiles, 1)
                if half == 0:
                    ada_turn(3, REST, 2)

            def logits(s):
                i, hd = divmod(s, NH)
                n = (i + 1) * P
                if s:
                    pe.wait_ge(ttr_done, s)
                pe.matmul(ps[:, B_LG, 0:n], qd2[i][:, hd, :], kd_hi[:, 0:n], start=True, stop=False)
                pe.matmul(ps[:, B_LG, 0:n], qd2[i][:, hd, :], kd_lo[:, 0:n], start=False, stop=True).then_inc(lg_done, 1)

            def turn(s):
                pe.wait_ge(p_done, s + 1)
                if s:
                    pe.wait_ge(pT_done, s)
                for b in range(s // NH + 1):
                    ins = pe.transpose(ps[:, B_PT, b * P:(b + 1) * P], lgb[:, s % 2, b * P:(b + 1) * P], ident[:])
                ins.then_inc(p_t, 1)

            def values(s):
                i, hd = divmod(s, NH)
                pe.wait_ge(pT_done, s + 1)
                if hd == 0 and i:
                    pe.wait_ge(ydn_done, i)
                for b in range(i + 1):
                    ins = pe.matmul(ps[:, B_O, hd * HD:(hd + 1) * HD], pT[:, s % 2, b * P:(b + 1) * P], vd[:, b, :],
                                    start=b == 0, stop=b == i, skip_group_check=True)
                ins.then_inc(pvd_done, 1)

            def sparse(s):
                if s >= 2:
                    values(s - 2)
                if 1 <= s <= NB * NH:
                    turn(s - 1)
                if s < NB * NH:
                    logits(s)

            def yd_turn(i, gate_tiles):
                pe.wait_ge(ydn_done, i + 1)
                pe.wait_ge(gate_done, gate_tiles)
                for t in range(4):
                    ins = pe.transpose(ps[:, B_F, t * P:(t + 1) * P], ydtok[:, t * P:(t + 1) * P], ident[:])
                ins.then_inc(yd_t, 1)

            def z_block(b, q0=0):
                return psf[:, BLK[b] + q0 * P:BLK[b] + S - b * P]

            pe.wait_ge(sbp_done, 8)
            pe.wait_ge(vsb_done, NB)
            for hd in range(NH):
                t, half = hd // 2, slice((hd % 2) * HD, (hd % 2 + 1) * HD)
                if hd:
                    pe.wait_ge(a_done, hd)
                for b in (0, 1, 3, 2):
                    pe.matmul(z_block(b), ksbT[half, t, b * P:(b + 1) * P], qsbT[half, t, b * P:S],
                              start=b != 3, stop=False, skip_group_check=True)
                for b in range(NB):
                    ins = pe.matmul(psf[:, BLK[b]:BLK[b] + P], ident_bf[:], strict_bf[:], start=False, stop=False,
                                    skip_group_check=True)
                ins.then_inc(z_done, 1)
                sparse(4 * hd)
                u = U_GATE + hd
                pe.wait_ge(lo_done, u + 1)
                if hd:
                    pe.wait_ge(gate_done, 2 * hd)
                column_tile(u, B_F, 0, n_hi, n_lo).then_inc(tiles, 1)
                sparse(4 * hd + 1)
                if hd == 0:
                    pe.wait_ge(round_done, 2)
                for b2 in (1, 3, 2, 0):
                    pe.wait_ge(sp_lo_done, 2 * hd + (2 if b2 == 0 else 1))
                    n = S - b2 * P
                    high = sp_hi0[:] if b2 == 0 else sp_hi1[:, BLK[b2] - S:BLK[b2] - S + n]
                    for b in range(b2 + 1):
                        w = (neg_tri_r if b2 == b else neg_ones_r)[:]
                        pe.matmul(z_block(b, b2 - b), w, high, start=False, stop=False, skip_group_check=True)
                        ins = pe.matmul(z_block(b, b2 - b), w, sp_lo[:, BLK[b2]:BLK[b2] + n], start=False,
                                        stop=b2 == 0, skip_group_check=True)
                ins.then_inc(suf_done, 1)
                if hd in (2, 4, 6):
                    yd_turn(hd // 2 - 1, 2 * hd + 1)
                sparse(4 * hd + 2)
                pe.wait_ge(gate_done, 2 * hd + 1)
                if hd in (2, 4, 6):
                    pe.wait_ge(ydT_done, hd // 2)
                column_tile(u, B_F, 1, n_hi, n_lo).then_inc(tiles, 1)
                sparse(4 * hd + 3)
                pe.wait_ge(a_done, hd + 1)
                if hd and hd % 2 == 0:
                    pe.wait_ge(ysb_lo_done, hd // 2)
                for b in range(NB):
                    ins = pe.matmul(ps[half, B_Y, b * P:S], vsb[:, b, hd * HD:(hd + 1) * HD],
                                    sp_a[:, BLK[b]:BLK[b] + S - b * P], start=b == 0, stop=b == NB - 1,
                                    skip_group_check=True)
                ins.then_inc(pv_done, 1)
            sparse(32)

            for n in range(4):
                u = U_PROJ + n
                if n == 1:
                    pe.wait_ge(yd_lo_done, 1)
                pe.wait_ge(lo_done, u + 1)
                for t in range(4):
                    if n >= 2:
                        pe.wait_ge((gy_done, gz_done)[n % 2], t + 1)
                    column_tile(u, 4 * (n % 2) + t, t, *((ysb_hi, ysb_lo), (yd_hi, yd_lo))[n % 2], width=512,
                                nk=4, step=(ysb_lo_done, 1) if n == 0 else None).then_inc(tiles, 1)
                    if n == 0 and t == 0:
                        sparse(33)
                    if n == 0 and t == 1:
                        yd_turn(3, 16)
            for m in range(KD):
                u = U_OUT + m // 2
                pe.wait_ge(lo_done, u + 1)
                if m == 0:
                    pe.wait_ge(mg_done, KD)
                column_tile(u, m, m % 2, n_hi, n_lo, step=(mg_lo_done, 1) if m == 0 else None).then_inc(tiles, 1)
            norm_sum(2)
            ffn(1)


_INS = ["x", "c", "w_ada", "b_ada", "g_ffn1", "w1_ffn1", "w3_ffn1", "w2_ffn1", "g_mix", "w_in", "g_q_dsa", "g_k_dsa",
        "w_proj_sb", "w_proj_dsa", "w_gate", "b_gate", "w_out", "g_ffn2", "w1_ffn2", "w3_ffn2", "w2_ffn2"]


def kernel(**inputs):
    import numpy as np
    import concourse.bacc as bacc
    from concourse.bass_utils import run_bass_kernel_spmd

    nc = bacc.Bacc("TRN2", target_bir_lowering=False, num_devices=1)
    arrays, args = {}, []
    for name in _INS:
        a = np.ascontiguousarray(inputs[name])
        arrays[f"in_{name}"] = a
        args.append(nc.dram_tensor(f"in_{name}", a.shape, mybir.dt.from_np(a.dtype), kind="ExternalInput").ap())
    args.append(nc.dram_tensor("out", (1, S, D), F32, kind="ExternalOutput").ap())
    layer_kernel(nc, *args)
    r = run_bass_kernel_spmd(nc, [arrays], core_ids=[0])
    return r.results[0]["out"]
```

```python
from contextlib import ExitStack

import concourse.bass as bass
from concourse import mybir

F32 = mybir.dt.float32
F32R = mybir.dt.float32r
BF16 = mybir.dt.bfloat16
ACT = mybir.ActivationFunctionType
ALU = mybir.AluOpType
AX = mybir.AxisListType

P = 128
D = 1024
S = 512
KD = D // P
NB = S // P
F = 2816
KF = F // P
HD = 64
NH = 8
TOPK = 128
EPS = 1e-6
UP_PAIRS = KF // 2
FFN_UNITS = 3 * UP_PAIRS
SLOT = 2048
NEG = -(2.0 ** 100)
NOT_CAUSAL = -1e38
TAKEN = -3e38

Q_SB, K_SB, V_SB, Q_D, K_D, V_D, Q_I, K_I, W_I, W_END = 0, 512, 1024, 1536, 2048, 2112, 2176, 2688, 2752, 2760
XC = HD + HD + HD + NH

U_X = FFN_UNITS
U_QD = U_X + 1
U_QI = U_QD + 2
U_QSB = U_QI + 2
U_KSB = U_QSB + 2
U_VSB = U_KSB + 2
U_GATE = U_VSB + 2
U_PROJ = U_GATE + 8
U_OUT = U_PROJ + 4
U_FFN2 = U_OUT + 4
U_END = U_FFN2 + FFN_UNITS

C_BADA, C_G, C_BGATE, C_C, C_GQ, C_GK, C_END = 0, 72, 96, 112, 120, 121, 122
HEAD_COLS = 2 * D
GROUPS = (9 * D - HEAD_COLS) // 512
LOOP_GROUPS = UP_PAIRS
REST = GROUPS - LOOP_GROUPS
SHIFT_MACS = 7

B_Y, B_F, B_LG, B_PT, B_O = 3, 4, 5, 6, 7
SHIFT_BANKS = [0, 2]
X_BANKS = [2, 3, 5, 6]
W2_ORDER = [4, 5, 6, 0, 1, 2, 3, 7]
HALF = S // 2
H_BASE = [0, KD, 3 * KD, 5 * KD]
N_BASE = [0, KD, 3 * KD]
ADDED = KD - 3

BLK = {0: 0, 1: 512, 3: 896, 2: 1024}
ZW = 1280
IDX = [(i, h) for i in (1, 2, 3) for h in range(NH)]
S_OFF = {1: 0, 2: 256, 3: 640}
R_OFF = {0: 0, 1: 128, 2: 384, 3: 768}
ROUNDS = TOPK // 8
HALVES = ((slice(0, HD), slice(HD, P)), (slice(HD, P), slice(0, HD)))


def tiles_of(u):
    if u < U_X or u >= U_FFN2:
        n = u if u < U_X else u - U_FFN2
        return 2 if n < 2 * UP_PAIRS else 1 if n < FFN_UNITS - 1 else 2 * KD if u < U_X else KD
    if U_OUT <= u:
        return 2 * KD if u == U_FFN2 - 1 else 1
    return {U_X: 2, U_QD: 1, U_QD + 1: NB, U_VSB: 1, U_VSB + 1: NB}.get(u, 4 if U_PROJ <= u < U_OUT else 2)


def before(u):
    return 1 + sum(tiles_of(v) for v in range(u))


def tile_at(u, t):
    return before(u) + t + 1


def layer_kernel(nc, x, c, w_ada, b_ada, g_ffn1, w1_ffn1, w3_ffn1, w2_ffn1, g_mix, w_in, g_q_dsa, g_k_dsa,
                 w_proj_sb, w_proj_dsa, w_gate, b_gate, w_out, g_ffn2, w1_ffn2, w3_ffn2, w2_ffn2, out):
    ctx = ExitStack()
    with ctx:
        place = [16640]

        def sb(name, shape, dt=F32, at=None):
            n = 1
            for v in shape[1:]:
                n *= v
            n *= 2 if dt == BF16 else 4
            off = place[0] if at is None else at
            if at is None:
                place[0] += -(-n // 32) * 32
                assert place[0] <= 229344, (name, place[0])
            return nc.alloc_sbuf_tensor_at(name, shape, dt, offset=off)

        def sem(name):
            return ctx.enter_context(nc.semaphore(name))

        h = sb("h", [P, KD, S])
        n_hi = sb("n_hi", [P, KD, S], F32R)
        n_at = place[0]
        n_lo = sb("n_lo", [P, KD, S], F32R)
        nx = sb("nx", [P, KD, S], at=n_at)
        raw = [sb(f"raw{i}", [P, SLOT]) for i in range(2)]
        w_hi = [sb(f"w_hi{i}", [P, SLOT], F32R) for i in range(2)]
        w_lo = [sb(f"w_lo{i}", [P, SLOT], F32R) for i in range(2)]
        ident = sb("ident", [P, P])
        ident_bf = sb("ident_bf", [P, P], BF16)
        strict_bf = sb("strict_bf", [P, P], BF16)
        neg_tri = sb("neg_tri", [P, P])
        neg_ones = sb("neg_ones", [P, P])
        neg_tri_r = sb("neg_tri_r", [P, P], F32R, at=place[0] - 1024)
        neg_ones_r = sb("neg_ones_r", [P, P], F32R, at=place[0] - 512)
        ones = sb("ones", [P, P])
        share = sb("share", [P, P])
        rows = sb("rows", [C_END, P])
        cols = sb("cols", [P, C_END])
        mod = sb("mod", [P, 9 * KD])
        nscale = sb("nscale", [P, 3, KD])
        half_gate = sb("half_gate", [P, 2, KD])
        sc = sb("sc", [P, KD])
        eps = sb("eps", [P, 1])
        zeros = sb("zeros", [P, LOOP_GROUPS])
        pick = sb("pick", [P, 2 * REST - 1])
        turns = sb("turns", [P, LOOP_GROUPS])
        now = sb("now", [P, LOOP_GROUPS], F32R)
        slope_inv = sb("slope_inv", [P, NH])
        wi = sb("wi", [P, NB, NH])
        kr = sb("kr", [P, NB])
        qr = sb("qr", [P, NB * NH])
        best = sb("best", [P, 8])
        negmax = sb("negmax", [P, NB * NH])
        psum_p = sb("psum_p", [P, NB * NH])
        pinv = sb("pinv", [P, NB * NH])
        tmp_at = place[0]
        nt = sb("nt", [P, 2, S])
        ssq = sb("ssq", [P, S])
        outb = sb("outb", [P, 4, NB, P], at=tmp_at)
        lgb = sb("lgb", [P, 2, S], at=tmp_at)
        arena = place[0]
        mid_hi = sb("mid_hi", [P, KF, S], F32R)
        mid_lo = sb("mid_lo", [P, KF, S], F32R)
        ada_ring = sb("ada_ring", [P, 2, 2 * 512])
        mod_rows = sb("mod_rows", [LOOP_GROUPS, 512], at=place[0])
        acc_lo = sb("acc_lo", [P, 512], F32R, at=place[0])
        acc_hi = sb("acc_hi", [P, 512], F32R, at=arena - 2048)
        ada_acc = sb("ada_acc", [P, 512])
        ada_rest = sb("ada_rest", [P, REST, 512], at=arena + 49152)
        slab = sb("slab", [P, KD, HEAD_COLS], at=arena)
        head_acc = sb("head_acc", [P, HEAD_COLS], at=arena + 65536)
        xin = sb("xin", [P, NB, D], at=arena + 73728)
        gates = sb("gates", [P, 16, S], at=arena)
        qi2 = [sb(f"qi2_{v}", [P, 4, S], F32R, at=arena + (0, 78848)[v]) for v in range(2)]
        ki_hi = sb("ki_hi", [P, S], F32R, at=arena + 8192)
        ki_lo = sb("ki_lo", [P, S], F32R, at=arena + 14336)
        relu = sb("relu", [P, 2, S], at=arena + 10240)
        qn = sb("qn", [P, 2, S], at=arena + 69120)
        kn = sb("kn", [P, NB, 2, HD], at=arena + 20480)
        ki = sb("ki", [P, NB, 2, HD], at=arena + 22528)
        dist = sb("dist", [P, S], at=arena + 26112)
        score = sb("score", [P, 1152], at=arena + 28160)
        qsbT = sb("qsbT", [P, 4, S], at=arena + 32768)
        ksbT = sb("ksbT", [P, 4, S], at=arena + 40960)
        ysb_hi = sb("ysb_hi", [P, 4, S], F32R, at=arena + 32768)
        ysb_lo = sb("ysb_lo", [P, 4, S], F32R, at=arena + 40960)
        vsb = sb("vsb", [P, NB, S], at=arena + 49152)
        qd2 = [sb(f"qd2_{i}", [P, NH, P], F32R, at=arena + (20480, 16384, 57344, 61440)[i]) for i in range(NB)]
        yd_hi = sb("yd_hi", [P, 4, S], F32R, at=arena + 49152)
        yd_lo = sb("yd_lo", [P, 4, S], F32R, at=arena + 57344)
        kd_hi = sb("kd_hi", [P, S], F32R, at=arena + 65536)
        kd_lo = sb("kd_lo", [P, S], F32R, at=arena + 87040)
        vd = sb("vd", [P, NB, HD], at=arena + 67584)
        R = sb("R", [P, ZW], at=arena + 68608)
        sp_a = sb("sp_a", [P, ZW], at=arena + 73728)
        sp_lo = sb("sp_lo", [P, ZW], F32R, at=arena + 73728)
        sqt = sb("sqt", [P, S], at=arena + 73728)
        ydT = sb("ydT", [P, 4, S], at=arena + 78848)
        pT = sb("pT", [P, 2, S], at=arena + 93184)
        ydtok = sb("ydtok", [P, S], at=arena + 91136)
        assert arena + 93184 <= place[0] - 2048 - 4096
        sp_hi0 = sb("sp_hi0", [P, S], F32R, at=arena - 2048)
        sp_hi1 = sb("sp_hi1", [P, ZW - S], F32R, at=arena + 97280)
        assert arena + 97280 + 4 * (ZW - S) <= place[0]

        ps = ctx.enter_context(nc.psum_tensor("ps", [P, 8, S], F32))
        psf = ps[:, :, :].rearrange("p b n -> p (b n)")

        rows_in, rows_t, cols_done, silu_c = sem("rows_in"), sem("rows_t"), sem("cols_done"), sem("silu_c")
        coef_q = sem("coef_q")
        consts = sem("consts")
        scale_in = [sem(f"scale_in{k}") for k in range(KD)]
        shift_in = [sem(f"shift_in{k}") for k in range(KD)]
        x_in = [sem(f"x_in{j}") for j in range(NB)]
        x_t = sem("x_t")
        head_mac, head_mm = sem("head_mac"), sem("head_mm")
        shift_half = sem("shift_half")
        xg_done = sem("xg_done")
        sq_used = sem("sq_used")
        first_in, first_hi, first_lo = sem("first_in"), sem("first_hi"), sem("first_lo")
        now_done = sem("now_done")
        ada_in = [sem(f"ada_in{r}") for r in range(2)]
        acc_hi_done, acc_lo_done = sem("acc_hi_done"), sem("acc_lo_done")
        ada_mac = sem("ada_mac")
        ada_mm = sem("ada_mm")
        ada_rows, ada_t = sem("ada_rows"), sem("ada_t")
        mod_done = sem("mod_done")
        coef = sem("coef")
        raw_in = [sem(f"raw_in{i}") for i in range(2)]
        hi_done, lo_done = sem("hi_done"), sem("lo_done")
        tiles = sem("tiles")
        silu_done, mul_done = sem("silu_done"), sem("mul_done")
        mid_hi_done, mid_lo_done = sem("mid_hi_done"), sem("mid_lo_done")
        h_done = sem("h_done")
        sq_done, ssq_done = sem("sq_done"), sem("ssq_done")
        sum_done, std_done, rstd_done = sem("sum_done"), sem("std_done"), sem("rstd_done")
        nx_done, n_hi_done, n_lo_done = sem("nx_done"), sem("n_hi_done"), sem("n_lo_done")
        ki_tok, ki_t, ki_done, vw_done = sem("ki_tok"), sem("ki_t"), sem("ki_done"), sem("vw_done")
        ksq_done, kss_done, kstd_done, kr_done, kn_done = (sem(f"k{v}_done") for v in ("sq", "ss", "std", "r", "n"))
        kn_t, kd_hi_done, kd_lo_done = sem("kn_t"), sem("kd_hi_done"), sem("kd_lo_done")
        qsq_done, qss_done, qstd_done, qr_done, qn_done = (sem(f"q{v}_done") for v in ("sq", "ss", "std", "r", "n"))
        qn_t, qd_hi_done, qd_lo_done = sem("qn_t"), sem("qd_hi_done"), sem("qd_lo_done")
        qi_hi_done, qi_lo_done, ki_lo_done = sem("qi_hi_done"), sem("qi_lo_done"), sem("ki_lo_done")
        idx_mm, relu_done, score_add = sem("idx_mm"), sem("relu_done"), sem("score_add")
        causal = sem("causal")
        top = sem("top")
        r_step, r_done = sem("r_step"), sem("r_done")
        sbp_done = sem("sbp_done")
        vsb_done = sem("vsb_done")
        z_done, ln_step, sp_done, suf_done, a_done, pv_done = (
            sem(v) for v in ("z_done", "ln_step", "sp_done", "suf_done", "a_done", "pv_done"))
        round_done, sp_hi_done, sp_lo_done = sem("round_done"), sem("sp_hi_done"), sem("sp_lo_done")
        ysb_hi_done, ysb_lo_done = sem("ysb_hi_done"), sem("ysb_lo_done")
        gate_done = sem("gate_done")
        lg_done, ttr_done, p_done, p_t, pT_done, pvd_done = (
            sem(v) for v in ("lg_done", "ttr_done", "p_done", "p_t", "pT_done", "pvd_done"))
        pinv_done, ydn_done, yd_t, ydT_done = sem("pinv_done"), sem("ydn_done"), sem("yd_t"), sem("ydT_done")
        yd_hi_done, yd_lo_done = sem("yd_hi_done"), sem("yd_lo_done")
        sig_done = sem("sig_done")
        gy_done, gz_done, mg_done, mg_hi_done, mg_lo_done = (
            sem(v) for v in ("gy_done", "gz_done", "mg_done", "mg_hi_done", "mg_lo_done"))
        h_t, out_copy = sem("h_t"), sem("out_copy")
        out_in = [sem(f"out_in{i}") for i in range(4)]

        def cols_unit(w, c0, n=256):
            return w[:, c0:c0 + n].rearrange("(k p) n -> p k n", p=P)

        def rows_unit(w, r0, c0, n):
            k = 2048 // n
            return w[r0:r0 + k * P, c0:c0 + n].rearrange("(k p) n -> p k n", p=P)

        ffn_w = [(w1_ffn1[0], w3_ffn1[0], w2_ffn1[0]), (w1_ffn2[0], w3_ffn2[0], w2_ffn2[0])]
        win, wg = w_in[0], w_gate[0]
        out_view = out[0].rearrange("(j p) (m q) -> m p j q", p=P, q=P)

        def middle_unit(u):
            if u < U_QI:
                return rows_unit(win, 4 * P * (u - U_QD), Q_D, 512)
            if u < U_QSB:
                return cols_unit(win, Q_I + 256 * (u - U_QI))
            if u < U_KSB:
                return cols_unit(win, Q_SB + 256 * (u - U_QSB))
            if u < U_VSB:
                return cols_unit(win, K_SB + 256 * (u - U_KSB))
            if u < U_GATE:
                return rows_unit(win, 4 * P * (u - U_VSB), V_SB, 512)
            if u < U_PROJ:
                return cols_unit(wg, 256 * (u - U_GATE))
            if u < U_OUT:
                w = (w_proj_sb, w_proj_dsa)[(u - U_PROJ) % 2][0]
                return rows_unit(w, 0, 512 * ((u - U_PROJ) // 2), 512)
            return rows_unit(w_out[0], 2 * P * (u - U_OUT), 0, D)

        def qi_parts(t):
            return [(2 * t + n, own, other) for n, (own, other) in enumerate(HALVES)]

        def qd2_heads(j, half, n):
            return qd2[j][half].rearrange("p (t two) q -> p two t q", two=2)[:, n]

        def half_tokens(th):
            return slice(th * HALF, (th + 1) * HALF)

        def raw_as(u, n):
            return raw[u % 2][:, 0:2048].rearrange("p (k n) -> p k n", n=n)

        def size(u):
            return KD * XC if u == U_X else 2048

        def in_parts(u):
            return 16 * 4 if u == U_X else 16

        def arrived(u):
            extra = in_parts(U_X) - 16 if u % 2 == U_X % 2 and u >= U_X else 0
            return 16 * (u // 2 + 1) + extra

        block = ctx.enter_context(nc.Block())

        @block.sync
        def _(sp):
            def load(u, src, n):
                if u >= 2:
                    sp.wait_ge(lo_done, u - 1)
                sp.dma_start(raw_as(u, n), src).then_inc(raw_in[u % 2], 16)

            sp.dma_start(rows[C_C:C_C + 8, :], c[0].rearrange("(r q) -> r q", q=P)).then_inc(rows_in, 16)
            sp.dma_start(rows[C_BADA:C_BADA + 72, :], b_ada[0].rearrange("(r q) -> r q", q=P)).then_inc(rows_in, 16)
            for j in range(NB):
                sp.dma_start(xin[:, j, :], x[0, j * P:(j + 1) * P, :]).then_inc(x_in[j], 16)
            for c0, arrive in ((D, scale_in), (0, shift_in)):
                for k in range(KD):
                    sp.dma_start(slab[:, k, c0:c0 + D], w_ada[0, k * P:(k + 1) * P, c0:c0 + D]).then_inc(arrive[k], 16)

            def ffn(f):
                w1, w3, w2 = ffn_w[f]
                u0 = (0, U_FFN2)[f]
                if f == 0:
                    halves = cols_unit(w1, 0)
                    sp.dma_start(raw_as(0, 256)[:, 0:KD // 2], halves[:, 0:KD // 2]).then_inc(first_in, 16)
                    sp.dma_start(raw_as(0, 256)[:, KD // 2:KD], halves[:, KD // 2:KD]).then_inc(raw_in[0], 16)
                else:
                    load(u0, cols_unit(w1, 0), 256)
                load(u0 + 1, cols_unit(w3, 0), 256)
                w1v = w1.rearrange("(k p) (c n) -> c p k n", p=P, n=256)
                w3v = w3.rearrange("(k p) (c n) -> c p k n", p=P, n=256)
                with sp.Fori(1, UP_PAIRS) as i:
                    sp.wait_ge(lo_done, i * 2 + (u0 - 1))
                    sp.dma_start(raw_as(u0, 256), w1v[bass.ds(i, 1)].rearrange("a p k n -> (a p) k n")
                                 ).then_inc(raw_in[u0 % 2], 16)
                    sp.wait_ge(lo_done, i * 2 + u0)
                    sp.dma_start(raw_as(u0 + 1, 256), w3v[bass.ds(i, 1)].rearrange("a p k n -> (a p) k n")
                                 ).then_inc(raw_in[(u0 + 1) % 2], 16)
                w2v = w2.rearrange("(t k p) n -> t p k n", p=P, k=2)
                u1 = u0 + 2 * UP_PAIRS
                load(u1, w2v[0], 1024)
                with sp.Fori(0, (UP_PAIRS - 1) // 2) as i:
                    for r in range(2):
                        sp.wait_ge(lo_done, i * 2 + (u1 + r))
                        sp.dma_start(raw_as(u1 + 1 + r, 1024),
                                     w2v[bass.ds(i * 2 + (1 + r), 1)].rearrange("a p k n -> (a p) k n")
                                     ).then_inc(raw_in[(u1 + 1 + r) % 2], 16)

            ffn(0)
            sp.wait_ge(lo_done, U_X - 1)
            xr = raw[U_X % 2][:, 0:KD * XC].rearrange("p (k n) -> p k n", n=XC)
            for at, c0, c1 in ((0, K_D, K_D + HD), (HD, V_D, V_D + HD), (2 * HD, W_I, W_END),
                               (2 * HD + NH, K_I, K_I + HD)):
                sp.dma_start(xr[:, :, at:at + c1 - c0], cols_unit(win, c0, c1 - c0)).then_inc(raw_in[U_X % 2], 16)
            for u in range(U_QD, U_FFN2):
                load(u, middle_unit(u), 512 if u in range(U_QD, U_QI) or u in range(U_VSB, U_GATE)
                     or u in range(U_PROJ, U_OUT) else D if u >= U_OUT else 256)
            ffn(1)
            for o, m in enumerate(W2_ORDER):
                sp.wait_ge(out_copy, o + 1)
                sp.dma_start(out_view[m], outb[:, o % 4]).then_inc(out_in[o % 4], 16)
            for i in range(4):
                sp.wait_ge(out_in[i], 16 * KD // 4)

        @block.gpsimd
        def _(pool):
            g = nc.gpsimd
            g.memset(ident[:], 0.0).then_inc(consts, 1)
            pool.wait_ge(consts, 1)
            g.affine_select(out=ident[:], in_=ident[:], compare_op=ALU.not_equal, fill=1.0, base=0,
                            pattern=[[-1, P]], channel_multiplier=1).then_inc(consts, 1)
            g.memset(ones[:], 1.0).then_inc(consts, 1)
            g.memset(neg_ones[:], -1.0).then_inc(consts, 1)
            g.memset(eps[:], EPS).then_inc(consts, 1)
            g.memset(share[:], 1.0 / D).then_inc(consts, 1)
            g.memset(pick[:], 0.0).then_inc(consts, 1)
            g.memset(zeros[:], 0.0).then_inc(consts, 1)
            pool.wait_ge(consts, 8)
            g.memset(pick[:, REST - 1:REST], 1.0).then_inc(consts, 1)
            g.iota(turns[:], pattern=[[1, LOOP_GROUPS]], base=0, channel_multiplier=0,
                   allow_small_or_imprecise_dtypes=True).then_inc(consts, 1)
            g.tensor_copy(ident_bf[:], ident[:]).then_inc(consts, 1)
            g.affine_select(out=neg_tri[:], in_=neg_ones[:], compare_op=ALU.is_ge, fill=0.0, base=0,
                            pattern=[[-1, P]], channel_multiplier=1).then_inc(consts, 1)
            g.memset(strict_bf[:], 0.0).then_inc(consts, 1)
            pool.wait_ge(consts, 13)
            g.affine_select(out=strict_bf[:], in_=strict_bf[:], compare_op=ALU.is_gt, fill=NEG, base=0,
                            pattern=[[1, P]], channel_multiplier=-1).then_inc(consts, 1)

            ada_v = w_ada[0].rearrange("(s k p) n -> s p k n", p=P, k=2)

            def ada_load(gr, n, wait):
                if wait is not None:
                    pool.wait_ge(ada_mac, wait)
                src = (ada_v[n, :, :, HEAD_COLS + 512 * gr:HEAD_COLS + 512 * gr + 512] if isinstance(gr, int)
                       else ada_v[n, :, :, bass.ds(gr * 512 + HEAD_COLS, 512)])
                pool.dma_start(ada_ring[:, n % 2, :].rearrange("p (k n) -> p k n", n=512), src).then_inc(ada_in[n % 2], 16)

            pool.wait_ge(rstd_done, 1)
            for m in range(KD):
                pool.wait_ge(xg_done, m + 1)
                g.tensor_tensor(nx[:, m, :], nx[:, m, :], ssq[:], ALU.mult).then_inc(nx_done, 1)
            pool.wait_ge(shift_in[KD - 1], 16)
            for n in range(4):
                ada_load(0, n, 2 * n - 2 if n >= 2 else None)
            with pool.Fori(1, LOOP_GROUPS) as i:
                for n in range(4):
                    ada_load(i, n, i * 8 + (2 * n - 2))
            def add_squares(q, th):
                tok = half_tokens(th)
                for o in range(1, ADDED + 1):
                    pool.wait_ge(sq_done, N_BASE[q] + th * KD + o + 1)
                    if o >= 2:
                        pool.wait_ge(ssq_done, ADDED * (2 * (q - 1) + th) + o - 1)
                    g.tensor_tensor(ssq[:, tok], ssq[:, tok], nt[:, o % 2, tok], ALU.add).then_inc(ssq_done, 1)

            def pool_lo(u):
                pool.wait_ge(hi_done, u + 1)
                pool.wait_ge(lo_done, u)
                g.tensor_tensor(w_lo[u % 2][:, 0:2048], raw[u % 2][:, 0:2048], w_hi[u % 2][:, 0:2048].bitcast(F32),
                                ALU.subtract).then_inc(lo_done, 1)

            add_squares(1, 0)
            add_squares(1, 1)
            pool_lo(U_QD)
            pool.wait_ge(n_lo_done, 3 * KD)
            g.iota(dist[:], pattern=[[1, S]], base=0, channel_multiplier=-1,
                   allow_small_or_imprecise_dtypes=True).then_inc(consts, 1)
            pool.wait_ge(consts, 15)
            g.affine_select(out=R[:, 0:P], in_=dist[:, 0:P], compare_op=ALU.is_ge, fill=NEG, base=0,
                            pattern=[[-1, P]], channel_multiplier=1).then_inc(consts, 1)
            for gr in range(LOOP_GROUPS, GROUPS):
                for n in range(4):
                    ada_load(gr, n, 8 * gr + 2 * n - 2)
            for n, i in enumerate((1, 2, 3)):
                pool.wait_ge(score_add, NH * (n + 1))
                d = score[:, S_OFF[i] + i * P:S_OFF[i] + (i + 1) * P]
                g.affine_select(out=d, in_=d, compare_op=ALU.is_ge, fill=NOT_CAUSAL, base=0,
                                pattern=[[-1, P]], channel_multiplier=1).then_inc(causal, 1)
            add_squares(2, 0)
            add_squares(2, 1)
            pool_lo(U_FFN2 + 1)

        @block.scalar
        def _(act):
            a = nc.scalar
            a.preload_act_table(ACT.Silu)
            dma_rows = [(C_G, 8, g_ffn1[0].rearrange("(r q) -> r q", q=P)),
                        (C_G + 8, 8, g_mix[0].rearrange("(r q) -> r q", q=P)),
                        (C_G + 16, 8, g_ffn2[0].rearrange("(r q) -> r q", q=P)),
                        (C_BGATE, 16, b_gate[0].rearrange("(r q) -> r q", q=P))]
            for r0, n, src in dma_rows:
                act.dma_start(rows[r0:r0 + n, :], src).then_inc(rows_in, 16)
            for r0, src in ((C_GQ, g_q_dsa), (C_GK, g_k_dsa)):
                act.dma_start(rows[r0:r0 + 1, :].rearrange("p (a n) -> p a n", n=HD),
                              src.unsqueeze(1).to_broadcast([1, 2, HD])).then_inc(rows_in, 16)

            def hi(u):
                act.wait_ge(raw_in[u % 2], arrived(u))
                if u >= 2:
                    act.wait_ge(tiles, before(u - 1))
                n = size(u)
                a.activation(w_hi[u % 2][:, 0:n], raw[u % 2][:, 0:n], ACT.Copy).then_inc(hi_done, 1)

            def hi_in_loop(i, u, signals):
                act.wait_ge(raw_in[u % 2], i * 16 + arrived(u))
                act.wait_ge(tiles, i * signals + before(u - 1))
                a.activation(w_hi[u % 2][:, 0:2048], raw[u % 2][:, 0:2048], ACT.Copy).then_inc(hi_done, 1)

            def square(q, th, o):
                tok = half_tokens(th)
                act.wait_ge(h_done, H_BASE[q] + th * KD + o + 1)
                if o >= 3:
                    act.wait_ge(ssq_done, ADDED * (2 * (q - 1) + th) + o - 2)
                dst = ssq[:, tok] if o == 0 else nt[:, o % 2, tok]
                a.activation(dst, h[:, W2_ORDER[o], tok], ACT.Square).then_inc(sq_done, 1)

            def norm_std(count, tok=slice(0, S)):
                act.wait_ge(sum_done, count)
                a.activation(ssq[:, tok], ps[:, 4, tok], ACT.Sqrt, bias=eps[:]).then_inc(std_done, 1)

            def norm_hi(q, m, th=None):
                if q == 0 and m == 0:
                    act.wait_ge(shift_half, 1)
                elif m == (4 if q == 0 else 0) and not th:
                    act.wait_ge(mod_done, q + 2)
                act.wait_ge(nx_done, N_BASE[q] + KD * (th or 0) + m + 1)
                tok = slice(0, S) if th is None else half_tokens(th)
                a.activation(n_hi[:, m, tok], nx[:, m, tok], ACT.Identity,
                             bias=mod[:, 24 * q + m:24 * q + m + 1]).then_inc(n_hi_done, 1)

            def norm(q):
                for o in range(KD):
                    square(q, 0, o)
                for o in range(5):
                    square(q, 1, o)
                norm_std(2 * q, half_tokens(0))
                square(q, 1, 5)
                norm_hi(q, 0, 0)
                norm_hi(q, 1, 0)
                square(q, 1, 6)
                square(q, 1, 7)
                norm_hi(q, 2, 0)
                norm_hi(q, 3, 0)
                norm_std(2 * q + 1, half_tokens(1))
                hi((U_QD, U_FFN2 + 1)[q - 1])
                for m in range(4, KD):
                    norm_hi(q, m, 0)
                for m in range(KD):
                    norm_hi(q, m, 1)

            def ffn(f):
                u0 = (0, U_FFN2)[f]
                j0 = KF * f
                def up_round(i):
                    for t in range(2):
                        act.wait_ge(tiles, i * 4 + tile_at(u0, t))
                        act.wait_ge(mid_lo_done, i * 2 + (j0 + t + 1))
                        a.activation(nt[:, t, :], ps[:, t, :], ACT.Silu).then_inc(silu_done, 1)
                        if t == 0:
                            hi_in_loop(i, u0 + 2, 4)
                    if f == 0:
                        act.wait_ge(ada_mac, i * 8 + 8)
                        a.activation(acc_hi[:], ada_acc[:], ACT.Copy).then_inc(acc_hi_done, 1)
                    for t in range(2):
                        act.wait_ge(mul_done, i * 2 + (j0 + t + 3))
                        dst = mid_hi[:, bass.ds(i * 2 + t, 1), :]
                        a.activation(dst, nt[:, t:t + 1, :], ACT.Copy).then_inc(mid_hi_done, 1)

                if f == 0:
                    hi(u0 + 1)
                with act.Fori(0, UP_PAIRS - 1) as i:
                    up_round(i)
                    hi_in_loop(i, u0 + 3, 4)
                up_round(UP_PAIRS - 1)
                with act.Fori(0, (UP_PAIRS - 1) // 2) as i:
                    hi_in_loop(i, u0 + 2 * UP_PAIRS + 1, 2)
                    hi_in_loop(i, u0 + 2 * UP_PAIRS + 2, 2)

            act.wait_ge(consts, 5)
            act.wait_ge(cols_done, 1)
            a.activation(sc[:], cols[:, C_C:C_C + KD], ACT.Silu).then_inc(silu_c, 1)
            a.preload_act_table(ACT.Sqrt)
            for m in range(KD):
                act.wait_ge(x_t, m + 1)
                a.activation(h[:, m, :], ps[:, X_BANKS[m % 4], :], ACT.Copy).then_inc(h_done, 1)
                if m >= 2:
                    act.wait_ge(sq_used, m - 1)
                a.activation(nt[:, m % 2, :], ps[:, X_BANKS[m % 4], :], ACT.Square).then_inc(sq_done, 1)
            norm_std(1)
            a.preload_act_table(ACT.Silu)
            act.wait_ge(coef, 1)
            for m in range(KD):
                a.activation(nx[:, m, :], h[:, m, :], ACT.Copy, scale=nscale[:, 0, m:m + 1]).then_inc(xg_done, 1)
            act.wait_ge(first_in, 16)
            a.activation(w_hi[0][:, 0:1024], raw[0][:, 0:1024], ACT.Copy).then_inc(first_hi, 1)
            act.wait_ge(raw_in[0], 16)
            a.activation(w_hi[0][:, 1024:2048], raw[0][:, 1024:2048], ACT.Copy).then_inc(hi_done, 1)
            for m in range(KD):
                norm_hi(0, m)
            ffn(0)
            hi(U_X)
            a.preload_act_table(ACT.Sqrt)
            norm(1)

            for y in range(2):
                act.wait_ge(tiles, tile_at(U_X, y))
                src = ps[:, 1 + y, 0:2 * XC].rearrange("p (b n) -> p b n", n=XC)[:, :, 0:HD]
                a.activation(sqt[:, y * P:(y + 1) * P].rearrange("p (b n) -> p b n", n=HD), src,
                             ACT.Square).then_inc(ksq_done, 1)
            hi(U_QD + 1)
            act.wait_ge(kss_done, 1)
            a.activation(kr[:], kr[:], ACT.Sqrt, bias=eps[:], scale=1.0 / HD).then_inc(kstd_done, 1)
            hi(U_QI)
            for j in range(NB):
                act.wait_ge(tiles, tile_at(U_QD + 1, j))
                if j == 0:
                    act.wait_ge(kss_done, 1)
                else:
                    act.wait_ge(qss_done, j)
                a.activation(sqt[:], ps[:, 4 + j, :], ACT.Square).then_inc(qsq_done, 1)
            act.wait_ge(kn_t, 1)
            a.activation(kd_hi[:], ps[:, 3, :], ACT.Copy, scale=cols[:, C_GK:C_GK + 1]).then_inc(kd_hi_done, 1)
            act.wait_ge(ki_t, 1)
            a.activation(ki_hi[:], ps[:, 2, :], ACT.Copy).then_inc(ki_done, 1)
            act.wait_ge(qss_done, NB)
            a.activation(qr[:], qr[:], ACT.Sqrt, bias=eps[:], scale=1.0 / HD).then_inc(qstd_done, 1)
            hi(U_QI + 1)
            for t in range(4):
                if t == 2:
                    hi(U_QSB)
                act.wait_ge(tiles, tile_at(U_QI, t))
                for hd, own, _ in qi_parts(t):
                    a.activation(qi2[hd // 4][own, hd % 4, :], ps[own, t % 2, :], ACT.Copy).then_inc(qi_hi_done, 1)
                if t % 2:
                    for j in (t - 1, t):
                        act.wait_ge(qn_t, j + 1)
                        for n, (own, _) in enumerate(HALVES):
                            a.activation(qd2_heads(j, own, n), ps[own, 2 + j % 2, :].rearrange("p (t q) -> p t q", q=P),
                                         ACT.Copy, scale=cols[own, C_GQ:C_GQ + 1]).then_inc(qd_hi_done, 1)
            for t in range(8):
                if t % 2 == 0:
                    hi(U_QSB + 1 + t // 2)
                act.wait_ge(tiles, tile_at(U_QSB, t))
                dst = (qsbT if t < 4 else ksbT)[:, t % 4, :]
                a.activation(dst, ps[:, t % 4, :], ACT.Copy, scale=HD ** -0.5 if t < 4 else 1.0).then_inc(sbp_done, 1)
                for s in range(3 * t, 3 * t + 3):
                    n = (IDX[s][0] + 1) * P
                    act.wait_ge(idx_mm, s + 1)
                    if s >= 2:
                        act.wait_ge(score_add, s - 1)
                    a.activation(relu[:, s % 2, 0:n], ps[:, 4 + s % 4, 0:n], ACT.Relu).then_inc(relu_done, 1)
            hi(U_VSB + 1)
            hi(U_GATE)
            for j in range(NB):
                act.wait_ge(tiles, tile_at(U_VSB + 1, j))
                a.activation(vsb[:, j, :], ps[:, 4 + j, :], ACT.Copy).then_inc(vsb_done, 1)

            def soft(s):
                i = s // NH
                n = (i + 1) * P
                act.wait_ge(ttr_done, s + 1)
                a.activation(lgb[:, s % 2, 0:n], lgb[:, s % 2, 0:n], ACT.Exp, bias=negmax[:, s:s + 1], scale=-1.0,
                             accum_out=psum_p[:, s:s + 1]).then_inc(p_done, 1)

            def ydT_copy(i):
                act.wait_ge(yd_t, i + 1)
                a.activation(ydT[:, :, i * P:(i + 1) * P], ps[:, B_F, :].rearrange("p (t q) -> p t q", q=P),
                             ACT.Copy).then_inc(ydT_done, 1)

            a.preload_act_table_set("natural_log_exp_and_others")
            a.activation(neg_tri_r[:], neg_tri[:], ACT.Copy).then_inc(round_done, 1)
            a.activation(neg_ones_r[:], neg_ones[:], ACT.Copy).then_inc(round_done, 1)
            for hd in range(NH):
                act.wait_ge(z_done, hd + 1)
                if hd:
                    act.wait_ge(pv_done, hd)
                a.activation(sp_a[:], psf[:, 0:ZW], ACT.Abs).then_inc(ln_step, 1)
                act.wait_ge(ln_step, 3 * hd + 1)
                a.activation(sp_a[:], sp_a[:], ACT.Exp, scale=-1.0).then_inc(ln_step, 1)
                act.wait_ge(ln_step, 3 * hd + 2)
                a.activation(sp_a[:], sp_a[:], ACT.Ln, bias=1.0).then_inc(ln_step, 1)
                soft(4 * hd)
                act.wait_ge(sp_done, 2 * hd + 1)
                if hd:
                    act.wait_ge(suf_done, hd)
                a.activation(sp_hi1[:], sp_a[:, S:ZW], ACT.Copy).then_inc(sp_hi_done, 1)
                act.wait_ge(sp_done, 2 * hd + 2)
                a.activation(sp_hi0[:], sp_a[:, 0:S], ACT.Copy).then_inc(sp_hi_done, 1)
                hi(U_GATE + 1 + hd)
                soft(4 * hd + 1)
                act.wait_ge(suf_done, hd + 1)
                a.activation(sp_a[:], psf[:, 0:ZW], ACT.Exp).then_inc(a_done, 1)
                if hd in (2, 4, 6):
                    ydT_copy(hd // 2 - 1)
                soft(4 * hd + 2)
                soft(4 * hd + 3)
                if hd % 2:
                    act.wait_ge(pv_done, hd + 1)
                    a.activation(ysb_hi[:, hd // 2, :], ps[:, B_Y, :], ACT.Copy).then_inc(ysb_hi_done, 1)
            hi(U_PROJ + 1)
            a.preload_act_table(ACT.Sigmoid)
            act.wait_ge(gate_done, 16)

            def sigmoids(m0):
                for m in range(m0, m0 + 4):
                    a.activation(gates[:, m, :], gates[:, m, :], ACT.Sigmoid).then_inc(sig_done, 1)

            sigmoids(0)
            ydT_copy(3)
            act.wait_ge(ydT_done, 4)
            a.activation(yd_hi[:], ydT[:], ACT.Copy).then_inc(yd_hi_done, 1)
            sigmoids(8)
            sigmoids(4)
            sigmoids(12)
            hi(U_PROJ + 2)
            for m in range(KD):
                if m == 4:
                    hi(U_PROJ + 3)
                    hi(U_OUT)
                act.wait_ge(mg_done, m + 1)
                a.activation(n_hi[:, m, :], gates[:, 8 + m, :], ACT.Copy).then_inc(mg_hi_done, 1)
            a.preload_act_table(ACT.Sqrt)
            for n in range(1, 4):
                hi(U_OUT + n)
            hi(U_FFN2)
            norm(2)
            a.preload_act_table(ACT.Silu)
            ffn(1)
            for o, m in enumerate(W2_ORDER):
                act.wait_ge(h_t, o + 1)
                if o >= 4:
                    act.wait_ge(out_in[o % 4], 16)
                a.activation(outb[:, o % 4], ps[:, m, :].rearrange("p (j q) -> p j q", q=P), ACT.Copy).then_inc(out_copy, 1)

        @block.vector
        def _(dve):
            v = nc.vector

            def lo(u):
                dve.wait_ge(hi_done, u + 1)
                n = size(u)
                v.tensor_tensor(w_lo[u % 2][:, 0:n], raw[u % 2][:, 0:n], w_hi[u % 2][:, 0:n].bitcast(F32),
                                ALU.subtract).then_inc(lo_done, 1)

            def lo_in_loop(i, u):
                dve.wait_ge(hi_done, i * 2 + (u + 1))
                v.tensor_tensor(w_lo[u % 2][:, 0:2048], raw[u % 2][:, 0:2048], w_hi[u % 2][:, 0:2048].bitcast(F32),
                                ALU.subtract).then_inc(lo_done, 1)

            def norm_rstd(count, tok=slice(0, S)):
                dve.wait_ge(std_done, count)
                v.reciprocal(ssq[:, tok], ssq[:, tok]).then_inc(rstd_done, 1)

            def norm_x(q, m, th):
                tok = half_tokens(th)
                if m == 0:
                    dve.wait_ge(rstd_done, 2 * q + th)
                    dve.wait_ge(coef, (1, 3, 5)[q])
                v.scalar_tensor_tensor(out=nx[:, m, tok], in0=h[:, m, tok], scalar=nscale[:, q, m:m + 1], in1=ssq[:, tok],
                                       op0=ALU.mult, op1=ALU.mult).then_inc(nx_done, 1)

            def norm_lo(q, m, th=None):
                dve.wait_ge(n_hi_done, N_BASE[q] + KD * (th or 0) + m + 1)
                tok = slice(0, S) if th is None else half_tokens(th)
                v.scalar_tensor_tensor(out=n_lo[:, m, tok], in0=nx[:, m, tok], scalar=mod[:, 24 * q + m:24 * q + m + 1],
                                       in1=n_hi[:, m, tok].bitcast(F32), op0=ALU.add,
                                       op1=ALU.subtract).then_inc(n_lo_done, 1)

            def norm(q, gate):
                for o in range(KD):
                    if o == 2:
                        lo((U_X, U_FFN2)[q - 1])
                    residual(q, o, gate, 0)
                for o in range(6):
                    residual(q, o, gate, 1)
                norm_rstd(2 * q, half_tokens(0))
                norm_x(q, 0, 0)
                norm_x(q, 1, 0)
                residual(q, 6, gate, 1)
                residual(q, 7, gate, 1)
                norm_lo(q, 0, 0)
                for m in range(1, 4):
                    norm_x(q, m + 1, 0)
                    norm_lo(q, m, 0)
                norm_rstd(2 * q + 1, half_tokens(1))
                for m in range(4, KD):
                    if m + 1 < KD:
                        norm_x(q, m + 1, 0)
                    norm_lo(q, m, 0)
                norm_x(q, 0, 1)
                norm_x(q, 1, 1)
                for m in range(KD):
                    if m + 2 < KD:
                        norm_x(q, m + 2, 1)
                    norm_lo(q, m, 1)

            def scale_of(q):
                v.scalar_tensor_tensor(out=nscale[:, q, :], in0=mod[:, 24 * q + 8:24 * q + 16], scalar=1.0,
                                       in1=cols[:, C_G + 8 * q:C_G + 8 * q + 8], op0=ALU.add, op1=ALU.mult).then_inc(coef, 1)

            def ada_group(acc, arrive, mac_at, ks=range(KD)):
                for k in ks:
                    if k % 2 == 0:
                        dve.wait_ge(ada_in[k // 2 % 2], arrive + 16 * (k // 4))
                    w = ada_ring[:, k // 2 % 2, 512 * (k % 2):512 * (k % 2) + 512]
                    if k == 0:
                        v.tensor_scalar(acc, w, sc[:, 0:1], None, ALU.mult).then_inc(ada_mac, 1)
                    else:
                        dve.wait_ge(ada_mac, mac_at + k)
                        v.scalar_tensor_tensor(out=acc, in0=w, scalar=sc[:, k:k + 1], in1=acc,
                                               op0=ALU.mult, op1=ALU.add).then_inc(ada_mac, 1)

            def ada_copy(bank, n, mm):
                dve.wait_ge(ada_mm, mm)
                v.tensor_copy(mod_rows[0:n, :], ps[0:n, bank, :]).then_inc(ada_rows, 1)

            def ada_columns(bank, n, m0, count):
                dve.wait_ge(ada_t, count)
                v.tensor_tensor(mod[:, m0:m0 + 4 * n].rearrange("p (g t) -> p t g", t=4),
                                ps[:, bank, 0:4 * n].rearrange("p (t g) -> p t g", g=n),
                                cols[:, m0:m0 + 4 * n].rearrange("p (g t) -> p t g", t=4), ALU.add).then_inc(mod_done, 1)

            def residual(q, o, gate, th=None):
                m = W2_ORDER[o]
                tok = slice(0, S) if th is None else half_tokens(th)
                dve.wait_ge(tiles, tile_at((U_X - 1, U_FFN2 - 1, U_END - 1)[q - 1], KD * (th or 0) + o))
                v.scalar_tensor_tensor(out=h[:, m, tok], in0=ps[:, m, tok], scalar=gate[:, m:m + 1], in1=h[:, m, tok],
                                       op0=ALU.mult, op1=ALU.add).then_inc(h_done, 1)

            def ffn(f):
                u0 = (0, U_FFN2)[f]
                j0 = KF * f
                if f == 0:
                    dve.wait_ge(consts, 14)
                def up_round(i):
                    if f == 0:
                        dve.wait_ge(ada_mm, i + 1)
                        dve.wait_ge(now_done, i * 2 + 1)
                        v.tensor_scalar(now[:], turns[:], 0.0, None, ALU.is_equal).then_inc(now_done, 1)
                        ada_group(ada_acc[:], i * 32 + 16, i * 8, range(KD // 2))
                        dve.wait_ge(now_done, i * 2 + 2)
                        v.tensor_scalar(turns[:], turns[:], -1.0, None, ALU.add).then_inc(now_done, 1)
                    lo_in_loop(i, u0 + 2)
                    if f == 0:
                        ada_group(ada_acc[:], i * 32 + 16, i * 8, range(KD // 2, KD))
                        dve.wait_ge(acc_hi_done, i + 1)
                        v.tensor_tensor(acc_lo[:], ada_acc[:], acc_hi[:].bitcast(F32), ALU.subtract).then_inc(acc_lo_done, 1)
                    for t in range(2):
                        dve.wait_ge(tiles, i * 4 + tile_at(u0 + 1, t))
                        dve.wait_ge(silu_done, i * 2 + (j0 + t + 3))
                        v.tensor_tensor(nt[:, t, :], nt[:, t, :], ps[:, 2 + t, :], ALU.mult).then_inc(mul_done, 1)
                    for t in range(2):
                        dve.wait_ge(mid_hi_done, i * 2 + (j0 + t + 1))
                        at = bass.ds(i * 2 + t, 1)
                        v.tensor_tensor(mid_lo[:, at, :], nt[:, t:t + 1, :], mid_hi[:, at, :].bitcast(F32),
                                        ALU.subtract).then_inc(mid_lo_done, 1)

                if f == 0:
                    lo(u0 + 1)
                else:
                    dve.wait_ge(lo_done, u0 + 2)
                with dve.Fori(0, UP_PAIRS - 1) as i:
                    up_round(i)
                    lo_in_loop(i, u0 + 3)
                up_round(UP_PAIRS - 1)
                if f == 0:
                    ada_copy(7, LOOP_GROUPS, LOOP_GROUPS + 1)
                    ada_columns(7, LOOP_GROUPS, 16, 1)
                    dve.wait_ge(mod_done, 3)
                    v.tensor_scalar(half_gate[:, 0, :], mod[:, 16:24], 0.5, None, ALU.mult).then_inc(coef, 1)
                    scale_of(1)
                with dve.Fori(0, (UP_PAIRS - 1) // 2) as i:
                    lo_in_loop(i, u0 + 2 * UP_PAIRS + 1)
                    lo_in_loop(i, u0 + 2 * UP_PAIRS + 2)

            v.memset(best[:, 0:1], 0.0).then_inc(tiles, 1)
            v.memset(best[:, 1:2], 0.0).then_inc(silu_done, 2)
            v.memset(best[:, 2:3], 0.0).then_inc(mul_done, 2)
            v.memset(best[:, 3:4], 0.0).then_inc(mid_lo_done, 2)
            v.memset(best[:, 4:5], 0.0).then_inc(ada_mm, 1)
            v.memset(best[:, 5:6], 0.0).then_inc(now_done, 1)
            for hd in range(NH):
                ins = v.memset(slope_inv[:, hd:hd + 1], 2.0 ** (hd + 1) * HD ** -0.5)
            ins.then_inc(coef_q, 1)
            dve.wait_ge(rows_t, 1)
            v.tensor_copy(cols[:], ps[:, 0, 0:C_END]).then_inc(cols_done, 1)
            dve.wait_ge(cols_done, 1)
            def head_macs(c0, arrive, ks, n):
                for k in ks:
                    dve.wait_ge(arrive[k], 16)
                    w, acc = slab[:, k, c0:c0 + D], head_acc[:, c0:c0 + D]
                    if k == 0:
                        v.tensor_scalar(acc, w, sc[:, 0:1], None, ALU.mult).then_inc(head_mac, 1)
                    else:
                        dve.wait_ge(head_mac, n + k)
                        v.scalar_tensor_tensor(out=acc, in0=w, scalar=sc[:, k:k + 1], in1=acc,
                                               op0=ALU.mult, op1=ALU.add).then_inc(head_mac, 1)

            dve.wait_ge(silu_c, 1)
            head_macs(D, scale_in, range(KD), 0)
            norm_rstd(1)
            dve.wait_ge(head_mm, 1)
            v.tensor_tensor(mod[:, 8:16], ps[:, 1, 8:16], cols[:, 8:16], ALU.add).then_inc(mod_done, 1)
            dve.wait_ge(mod_done, 1)
            scale_of(0)
            head_macs(0, shift_in, range(SHIFT_MACS), KD)
            dve.wait_ge(first_hi, 1)
            v.tensor_tensor(w_lo[0][:, 0:1024], raw[0][:, 0:1024], w_hi[0][:, 0:1024].bitcast(F32),
                            ALU.subtract).then_inc(first_lo, 1)
            dve.wait_ge(hi_done, 1)
            v.tensor_tensor(w_lo[0][:, 1024:2048], raw[0][:, 1024:2048], w_hi[0][:, 1024:2048].bitcast(F32),
                            ALU.subtract).then_inc(lo_done, 1)
            for half, done in enumerate((shift_half, mod_done)):
                at = slice(4 * half, 4 * half + 4)
                dve.wait_ge(head_mm, 2 + half)
                v.tensor_tensor(mod[:, at], ps[:, SHIFT_BANKS[half], at], cols[:, at], ALU.add).then_inc(done, 1)
                dve.wait_ge(done, 1 + half)
                for m in ((0, 1), range(2, KD))[half]:
                    norm_lo(0, m)
            ffn(0)
            dve.wait_ge(coef, 2)
            norm(1, half_gate[:, 0, :])

            def rest_group(g, ks=range(KD)):
                gr = LOOP_GROUPS + g
                ada_group(ada_rest[:, g, :], 32 * gr + 16, 8 * gr, ks)

            for y in range(2):
                dve.wait_ge(tiles, tile_at(U_X, y))
                dve.wait_ge(ksq_done, 1 + y)
                both = ps[:, 1 + y, 0:2 * XC].rearrange("p (b n) -> p b n", n=XC)
                for dup in range(2):
                    v.tensor_copy(ki[:, 2 * y:2 * y + 2, dup, :], both[:, :, 2 * HD + NH:XC]).then_inc(ki_tok, 1)
                v.tensor_copy(vd[:, 2 * y:2 * y + 2, :], both[:, :, HD:2 * HD]).then_inc(vw_done, 1)
                v.tensor_scalar(wi[:, 2 * y:2 * y + 2, :], both[:, :, 2 * HD:2 * HD + NH],
                                HD ** -0.5 * NH ** -0.5, None, ALU.mult).then_inc(vw_done, 1)
            v.tensor_reduce(kr[:], sqt[:, 0:NB * HD].rearrange("p (b n) -> p b n", n=HD), AX.X, ALU.add).then_inc(kss_done, 1)
            dve.wait_ge(kstd_done, 1)
            v.reciprocal(kr[:], kr[:]).then_inc(kr_done, 1)
            dve.wait_ge(kr_done, 1)
            for y in range(2):
                both = ps[:, 1 + y, 0:2 * XC].rearrange("p (b n) -> p b n", n=XC)
                for dup in range(2):
                    v.tensor_tensor(kn[:, 2 * y:2 * y + 2, dup, :], both[:, :, 0:HD],
                                    kr[:, 2 * y:2 * y + 2].unsqueeze(2).to_broadcast([P, 2, HD]), ALU.mult).then_inc(kn_done, 1)
            dve.wait_ge(lo_done, U_QD + 1)
            lo(U_QD + 1)
            rest_group(0)
            lo(U_QI)
            for j in range(NB):
                dve.wait_ge(qsq_done, j + 1)
                v.tensor_reduce(qr[:, j * NH:(j + 1) * NH], sqt[:].rearrange("p (b n) -> p b n", n=HD),
                                AX.X, ALU.add).then_inc(qss_done, 1)
            dve.wait_ge(kn_t, 1)
            dve.wait_ge(kd_hi_done, 1)
            v.scalar_tensor_tensor(out=kd_lo[:], in0=ps[:, 3, :], scalar=cols[:, C_GK:C_GK + 1], in1=kd_hi[:].bitcast(F32),
                                   op0=ALU.mult, op1=ALU.subtract).then_inc(kd_lo_done, 1)
            dve.wait_ge(qstd_done, 1)
            v.reciprocal(qr[:], qr[:]).then_inc(qr_done, 1)
            dve.wait_ge(qr_done, 1)
            dve.wait_ge(coef_q, 1)
            by_block = qr[:].rearrange("p (b n) -> p b n", n=NH)
            v.tensor_tensor(by_block, by_block, slope_inv[:].unsqueeze(1).to_broadcast([P, NB, NH]),
                            ALU.mult).then_inc(qr_done, 1)
            dve.wait_ge(qr_done, 2)

            def qi_low(t):
                for hd, own, other in qi_parts(t):
                    dve.wait_ge(qi_hi_done, hd + 1)
                    v.tensor_tensor(qi2[hd // 4][other, hd % 4, :], ps[own, t % 2, :],
                                    qi2[hd // 4][own, hd % 4, :].bitcast(F32), ALU.subtract).then_inc(qi_lo_done, 1)

            def q_norm(j):
                if j >= 2:
                    dve.wait_ge(qn_t, j - 1)
                v.tensor_tensor(qn[:, j % 2, :].rearrange("p (b n) -> p b n", n=HD),
                                ps[:, 4 + j, :].rearrange("p (b n) -> p b n", n=HD),
                                qr[:, j * NH:(j + 1) * NH].unsqueeze(2).to_broadcast([P, NH, HD]), ALU.mult).then_inc(qn_done, 1)

            def q_store(j):
                for n, (own, other) in enumerate(HALVES):
                    dve.wait_ge(qd_hi_done, 2 * j + n + 1)
                    v.scalar_tensor_tensor(out=qd2_heads(j, other, n),
                                           in0=ps[own, 2 + j % 2, :].rearrange("p (t q) -> p t q", q=P),
                                           scalar=cols[own, C_GQ:C_GQ + 1], in1=qd2_heads(j, own, n).bitcast(F32),
                                           op0=ALU.mult, op1=ALU.subtract).then_inc(qd_lo_done, 1)

            q_norm(0)
            q_norm(1)
            dve.wait_ge(ki_done, 1)
            v.tensor_tensor(ki_lo[:], ps[:, 2, :], ki_hi[:].bitcast(F32), ALU.subtract).then_inc(ki_lo_done, 1)
            qi_low(0)
            lo(U_QI + 1)
            qi_low(1)
            q_store(0)
            q_norm(2)
            q_store(1)
            q_norm(3)
            lo(U_QSB)
            qi_low(2)
            qi_low(3)
            q_store(2)
            q_store(3)
            def add_score(s):
                i, hd = IDX[s]
                n = (i + 1) * P
                acc = score[:, S_OFF[i]:S_OFF[i] + n]
                dve.wait_ge(relu_done, s + 1)
                w = wi[:, i, hd:hd + 1]
                if hd == 0:
                    v.tensor_scalar(acc, relu[:, s % 2, 0:n], w, 0.0, ALU.mult, ALU.add).then_inc(score_add, 1)
                else:
                    dve.wait_ge(score_add, s)
                    v.scalar_tensor_tensor(out=acc, in0=relu[:, s % 2, 0:n], scalar=w, in1=acc,
                                           op0=ALU.mult, op1=ALU.add).then_inc(score_add, 1)

            top_count = [0]

            def take(i):
                n = (i + 1) * P
                acc = score[:, S_OFF[i]:S_OFF[i] + n]
                if top_count[0] % (2 * ROUNDS) == 0:
                    dve.wait_ge(causal, i)
                    dve.wait_ge(consts, 16)
                if top_count[0]:
                    dve.wait_ge(top, top_count[0])
                v.max(best[:], acc).then_inc(top, 1)
                dve.wait_ge(top, top_count[0] + 1)
                v.match_replace(acc, best[:], acc, TAKEN).then_inc(top, 1)
                top_count[0] += 2
                if top_count[0] % (2 * ROUNDS) == 0:
                    r = R[:, R_OFF[i]:R_OFF[i] + n]
                    dve.wait_ge(top, top_count[0])
                    v.tensor_scalar(r, acc, (TAKEN + NOT_CAUSAL) / 2, NEG, ALU.is_gt, ALU.mult).then_inc(r_step, 1)
                    dve.wait_ge(r_step, i)
                    v.scalar_tensor_tensor(out=r, in0=dist[:, 0:n], scalar=float(-P * i), in1=r,
                                           op0=ALU.add, op1=ALU.add).then_inc(r_done, 1)

            rounds = [1] * ROUNDS + [2] * ROUNDS + [3] * ROUNDS
            taken = [0]

            def takes(n):
                for i in rounds[taken[0]:taken[0] + n]:
                    take(i)
                taken[0] += n

            for t in range(8):
                if t % 2 == 0:
                    lo(U_QSB + 1 + t // 2)
                for s in range(3 * t, 3 * t + 3):
                    add_score(s)
                if t < 4:
                    rest_group(1 + t // 2, range(KD // 2 * (t % 2), KD // 2 * (t % 2 + 1)))
                if t >= 3:
                    takes(3 if t > 3 else 2)
            lo(U_VSB + 1)
            ada_copy(3, REST, LOOP_GROUPS + 2)
            ada_columns(3, REST, 16 + 4 * LOOP_GROUPS, 2)
            dve.wait_ge(mod_done, 4)
            scale_of(2)
            v.tensor_scalar(half_gate[:, 1, :], mod[:, 64:72], 0.5, None, ALU.mult).then_inc(coef, 1)
            takes(6)
            lo(U_GATE)
            takes(4)

            def logits_max(s):
                i, hd = divmod(s, NH)
                n = (i + 1) * P
                dve.wait_ge(lg_done, s + 1)
                if s == 0:
                    dve.wait_ge(consts, 16)
                if hd == 0 and i:
                    dve.wait_ge(r_done, i)
                if s >= 2:
                    dve.wait_ge(p_t, s - 1)
                v.tensor_tensor_reduce(lgb[:, s % 2, 0:n], ps[:, B_LG, 0:n], R[:, R_OFF[i]:R_OFF[i] + n],
                                       -(2.0 ** -(hd + 1)), 3e38, ALU.add, ALU.min, negmax[:, s:s + 1]).then_inc(ttr_done, 1)

            def pT_copy(s):
                n = (s // NH + 1) * P
                dve.wait_ge(p_t, s + 1)
                if s >= 2:
                    dve.wait_ge(pvd_done, s - 1)
                v.tensor_copy(pT[:, s % 2, 0:n], ps[:, B_PT, 0:n]).then_inc(pT_done, 1)

            def gate_store(m):
                dve.wait_ge(tiles, tile_at(U_GATE, m))
                v.tensor_scalar(gates[:, m, :], ps[:, B_F, :], cols[:, C_BGATE + m:C_BGATE + m + 1], None,
                                ALU.add).then_inc(gate_done, 1)

            def yd_norm(i):
                dve.wait_ge(pvd_done, NH * (i + 1))
                v.reciprocal(pinv[:, NH * i:NH * (i + 1)], psum_p[:, NH * i:NH * (i + 1)]).then_inc(pinv_done, 1)
                dve.wait_ge(pinv_done, i + 1)
                if i:
                    dve.wait_ge(yd_t, i)
                v.tensor_tensor(ydtok[:].rearrange("p (b n) -> p b n", n=HD), ps[:, B_O, :].rearrange("p (b n) -> p b n", n=HD),
                                pinv[:, NH * i:NH * (i + 1)].unsqueeze(2).to_broadcast([P, NH, HD]), ALU.mult).then_inc(ydn_done, 1)

            for hd in range(NH):
                if hd:
                    pT_copy(4 * hd - 1)
                logits_max(4 * hd)
                dve.wait_ge(ln_step, 3 * hd + 3)
                for c in (slice(S, ZW), slice(0, S)):
                    v.scalar_tensor_tensor(out=sp_a[:, c], in0=psf[:, c], scalar=0.0, in1=sp_a[:, c], op0=ALU.max,
                                           op1=ALU.add).then_inc(sp_done, 1)
                dve.wait_ge(sp_hi_done, 2 * hd + 1)
                v.tensor_tensor(sp_lo[:, S:ZW], sp_a[:, S:ZW], sp_hi1[:].bitcast(F32), ALU.subtract).then_inc(sp_lo_done, 1)
                dve.wait_ge(sp_hi_done, 2 * hd + 2)
                v.tensor_tensor(sp_lo[:, 0:S], sp_a[:, 0:S], sp_hi0[:].bitcast(F32), ALU.subtract).then_inc(sp_lo_done, 1)
                gate_store(2 * hd)
                pT_copy(4 * hd)
                logits_max(4 * hd + 1)
                if hd in (2, 4, 6):
                    yd_norm(hd // 2 - 1)
                lo(U_GATE + 1 + hd)
                pT_copy(4 * hd + 1)
                logits_max(4 * hd + 2)
                if hd < 6:
                    takes(2)
                gate_store(2 * hd + 1)
                pT_copy(4 * hd + 2)
                logits_max(4 * hd + 3)
                if hd < 6:
                    takes(2 if taken[0] < len(rounds) - 1 else 0)
                if hd % 2:
                    dve.wait_ge(ysb_hi_done, hd // 2 + 1)
                    v.tensor_tensor(ysb_lo[:, hd // 2, :], ps[:, B_Y, :], ysb_hi[:, hd // 2, :].bitcast(F32),
                                    ALU.subtract).then_inc(ysb_lo_done, 1)
            assert taken[0] == len(rounds)
            pT_copy(31)
            lo(U_PROJ + 1)
            yd_norm(3)

            def gated_sb(m):
                dve.wait_ge(tiles, tile_at(U_PROJ + 2 * (m // 4), m % 4))
                dve.wait_ge(sig_done, m + 1 if m < 4 else m + 5)
                v.tensor_tensor(gates[:, m, :], gates[:, m, :], ps[:, m % 4, :], ALU.mult).then_inc(gy_done, 1)

            def merged(m):
                dve.wait_ge(tiles, tile_at(U_PROJ + 2 * (m // 4) + 1, m % 4))
                dve.wait_ge(sig_done, m + 5 if m < 4 else m + 9)
                g = gates[:, 8 + m, :]
                v.tensor_tensor(g, g, ps[:, 4 + m % 4, :], ALU.mult).then_inc(gz_done, 1)
                dve.wait_ge(gz_done, m + 1)
                dve.wait_ge(gy_done, m + 1)
                v.tensor_tensor(g, g, gates[:, m, :], ALU.add).then_inc(mg_done, 1)

            def merged_lo(m):
                dve.wait_ge(mg_hi_done, m + 1)
                v.tensor_tensor(n_lo[:, m, :], gates[:, 8 + m, :], n_hi[:, m, :].bitcast(F32), ALU.subtract).then_inc(mg_lo_done, 1)

            for half in range(2):
                for m in range(4 * half, 4 * half + 4):
                    gated_sb(m)
                    if m == 1:
                        dve.wait_ge(yd_hi_done, 1)
                        v.tensor_tensor(yd_lo[:], ydT[:], yd_hi[:].bitcast(F32), ALU.subtract).then_inc(yd_lo_done, 1)
                    if m == 4 * half + 3:
                        lo(U_PROJ + 2 if half == 0 else U_OUT)
                for m in range(4 * half, 4 * half + 4):
                    merged(m)
                    if m > 4 * half:
                        merged_lo(m - 1)
                merged_lo(4 * half + 3)
                lo(U_PROJ + 3 if half == 0 else U_OUT + 1)
            lo(U_OUT + 2)
            lo(U_OUT + 3)
            norm(2, mod[:, 40:48])
            ffn(1)
            for o in range(KD):
                residual(3, o, half_gate[:, 1, :])

        @block.tensor
        def _(pe):
            ALL = [slice(0, S)]

            def mm3(dst, whi, wlo, xhi, xlo, first, last):
                pe.matmul(dst, whi, xhi, start=first, stop=False, skip_group_check=True)
                pe.matmul(dst, whi, xlo, start=False, stop=False, skip_group_check=True)
                return pe.matmul(dst, wlo, xhi, start=False, stop=last, skip_group_check=True)

            def column_tile(u, bank, t, act_hi, act_lo, width=256, nk=KD, step=None):
                for k in range(nk):
                    if step is not None:
                        pe.wait_ge(step[0], step[1] + k)
                    w = slice(k * width + t * P, k * width + (t + 1) * P)
                    ins = mm3(ps[:, bank, :], w_hi[u % 2][:, w], w_lo[u % 2][:, w], act_hi[:, k, :], act_lo[:, k, :],
                              k == 0, k == nk - 1)
                return ins

            def token_tile(u, dst, j, w0, n, width, ks, k0, first, last):
                for k in ks:
                    w = slice((k - k0) * width + w0, (k - k0) * width + w0 + n)
                    tok = slice(j * P, (j + 1) * P)
                    f, l = first and k == ks[0], last and k == ks[-1]
                    pe.matmul(dst, n_hi[:, k, tok], w_hi[u % 2][:, w], start=f, stop=False, skip_group_check=True)
                    pe.matmul(dst, n_hi[:, k, tok], w_lo[u % 2][:, w], start=False, stop=False, skip_group_check=True)
                    ins = pe.matmul(dst, n_lo[:, k, tok], w_hi[u % 2][:, w], start=False, stop=l, skip_group_check=True)
                return ins

            def norm_sum(q, th):
                tok = half_tokens(th)
                pe.wait_ge(ssq_done, ADDED * (2 * (q - 1) + th + 1))
                if th == 0:
                    pe.wait_ge(h_done, H_BASE[q] + KD + 1)
                else:
                    pe.wait_ge(std_done, 2 * q)
                pe.matmul(ps[:, 4, tok], share[:], ssq[:, tok], start=th == 0, stop=False, skip_group_check=True)
                pe.wait_ge(sq_done, N_BASE[q] + KD * (th + 1) - 1)
                pe.matmul(ps[:, 4, tok], share[:], nt[:, KD % 2, tok], start=False, stop=False, skip_group_check=True)
                pe.wait_ge(sq_done, N_BASE[q] + KD * (th + 1))
                pe.matmul(ps[:, 4, tok], share[:], nt[:, (KD - 1) % 2, tok], start=False, stop=True,
                          skip_group_check=True).then_inc(sum_done, 1)

            def row_tile(u, m, k, k_in, act_hi, act_lo, tok, first, last):
                w = slice(k * D + m * P, k * D + (m + 1) * P)
                return mm3(ps[:, m, tok], w_hi[u % 2][:, w], w_lo[u % 2][:, w], act_hi[:, k_in, tok], act_lo[:, k_in, tok],
                           first, last)

            def by_halves(u, q, k0, act_hi, act_lo):
                for th in range(2):
                    for o, m in enumerate(W2_ORDER):
                        if th:
                            pe.wait_ge(h_done, H_BASE[q] + o + 1)
                        for k in range(2):
                            ins = row_tile(u, m, k, k0 + k, act_hi, act_lo, half_tokens(th), False, k == 1)
                        ins.then_inc(tiles, 1)
                        if th == 1 and o == 3:
                            norm_sum(q, 0)
                norm_sum(q, 1)

            def ada_turn(bank, n, count):
                pe.wait_ge(ada_rows, count)
                for t in range(4):
                    ins = pe.transpose(ps[:, bank, t * n:(t + 1) * n], mod_rows[0:n, t * P:(t + 1) * P], ident[0:n, 0:n])
                ins.then_inc(ada_t, 1)

            def ffn(f):
                u0 = (0, U_FFN2)[f]
                j0 = KF * f

                def w1_unit(i, tokens):
                    pe.wait_ge(lo_done, i * 2 + (u0 + 1))
                    pe.wait_ge(silu_done, i * 2 + (j0 + 2))
                    for th, tok in enumerate(tokens):
                        for k in range(KD):
                            if tokens is not ALL or f == 0:
                                pe.wait_ge(n_lo_done, N_BASE[2 * f] + KD * th + k + 1)
                            for t in range(2):
                                w = slice(k * 256 + t * P, k * 256 + (t + 1) * P)
                                ins = mm3(ps[:, t, tok], w_hi[u0 % 2][:, w], w_lo[u0 % 2][:, w], n_hi[:, k, tok],
                                          n_lo[:, k, tok], k == 0 and th == 0, k == KD - 1)
                                if k == KD - 1 and th == len(tokens) - 1:
                                    ins.then_inc(tiles, 1)

                def w3_unit(i):
                    u = u0 + 1
                    pe.wait_ge(lo_done, i * 2 + (u + 1))
                    pe.wait_ge(mul_done, i * 2 + (j0 + 2))
                    for t in range(2):
                        column_tile(u, 2 + t, t, n_hi, n_lo).then_inc(tiles, 1)
                    if f == 0:
                        pe.wait_ge(acc_lo_done, i + 1)
                        pe.wait_ge(now_done, i * 2 + 2)
                        pe.matmul(ps[0:LOOP_GROUPS, 7, :], now[:], acc_hi[:], start=False, stop=False,
                                  skip_group_check=True)
                        pe.matmul(ps[0:LOOP_GROUPS, 7, :], now[:], acc_lo[:], start=False, stop=False,
                                  skip_group_check=True).then_inc(ada_mm, 1)

                w1_unit(0, ALL if f == 0 else [half_tokens(0), half_tokens(1)])
                with pe.Fori(0, UP_PAIRS - 1) as i:
                    w3_unit(i)
                    w1_unit(i + 1, ALL)
                w3_unit(UP_PAIRS - 1)
                u1 = u0 + 2 * UP_PAIRS

                def down(u, k_at, first=False, last=False):
                    for o, m in enumerate(W2_ORDER):
                        if first and m == 0 and f == 0:
                            ada_turn(7, LOOP_GROUPS, 1)
                        if first and m == 7 and f == 0:
                            pe.wait_ge(mod_done, 3)
                        if first and m == 0:
                            pe.wait_ge(silu_done, j0 + KF + 2)
                        if first and m == 2:
                            pe.wait_ge(mul_done, j0 + KF + 2)
                        for k in range(2):
                            ins = row_tile(u, m, k, k_at(k), mid_hi, mid_lo, slice(0, S), first and k == 0, last and k == 1)
                        if last or m == W2_ORDER[-1]:
                            ins.then_inc(tiles, 1)
                        if last and f == 1 and o >= 2:
                            out_tile(o - 2)

                def out_tile(o):
                    m = W2_ORDER[o]
                    pe.wait_ge(h_done, H_BASE[3] + o + 1)
                    for j in range(NB):
                        ins = pe.transpose(ps[:, m, j * P:(j + 1) * P], h[:, m, j * P:(j + 1) * P], ident[:])
                    ins.then_inc(h_t, 1)

                pe.wait_ge(lo_done, u1 + 1)
                pe.wait_ge(mid_lo_done, j0 + 2 + 2)
                down(u1, lambda k: k, first=True)
                pe.wait_ge(mid_lo_done, j0 + KF + 2)
                with pe.Fori(0, (UP_PAIRS - 3) // 2) as i:
                    for r in range(2):
                        pe.wait_ge(lo_done, i * 2 + (u1 + 2 + r))
                        down(u1 + 1 + r, lambda k: bass.ds(i * 4 + (2 + 2 * r + k), 1))
                pe.wait_ge(lo_done, u1 + UP_PAIRS - 1)
                down(u1 + UP_PAIRS - 2, lambda k: 2 * UP_PAIRS - 4 + k)
                pe.wait_ge(lo_done, u1 + UP_PAIRS)
                if f == 0:
                    by_halves(u1 + UP_PAIRS - 1, 1, KF - 2, mid_hi, mid_lo)
                else:
                    down(u1 + UP_PAIRS - 1, lambda k: KF - 2 + k, last=True)
                    out_tile(KD - 2)
                    out_tile(KD - 1)

            pe.wait_ge(rows_in, 16 * 8)
            pe.wait_ge(consts, 14)
            pe.transpose(ps[:, 0, 0:C_END], rows[:], ident[0:C_END, 0:C_END]).then_inc(rows_t, 1)
            for j in range(NB):
                pe.wait_ge(x_in[j], 16)

            def add_x_square(m):
                pe.wait_ge(sq_done, m + 1)
                pe.matmul(ps[:, 4, :], share[:], nt[:, m % 2, :], start=m == 0, stop=m == KD - 1,
                          skip_group_check=True).then_inc(sum_done if m == KD - 1 else sq_used, 1)

            for m in range(KD):
                if m >= 4:
                    pe.wait_ge(h_done, m - 3)
                    pe.wait_ge(sq_done, m - 3)
                for j in range(NB):
                    ins = pe.transpose(ps[:, X_BANKS[m % 4], j * P:(j + 1) * P], xin[:, j, m * P:(m + 1) * P], ident[:])
                ins.then_inc(x_t, 1)
                if m >= 2:
                    add_x_square(m - 2)
            add_x_square(KD - 2)
            add_x_square(KD - 1)
            for t in range(4):
                pe.matmul(ps[0:LOOP_GROUPS, 7, t * P:(t + 1) * P], zeros[:], ones[:], start=t == 0, stop=False,
                          skip_group_check=True)
            pe.wait_ge(head_mac, KD)
            for t in range(KD):
                ins = pe.matmul(ps[:, 1, 8 + t:9 + t], head_acc[:, D + t * P:D + (t + 1) * P], ones[:, 0:1],
                                start=t == 0, stop=t == KD - 1, skip_group_check=True)
            ins.then_inc(head_mm, 1)
            pe.wait_ge(silu_c, 1)
            for k in list(range(SHIFT_MACS, KD)) + [None]:
                if k is None:
                    pe.wait_ge(head_mac, KD + SHIFT_MACS)
                else:
                    pe.wait_ge(shift_in[k], 16)
                for t in range(KD):
                    w, r = ((head_acc[:, t * P:(t + 1) * P], ones[:, 0:1]) if k is None else
                            (slab[:, k, t * P:(t + 1) * P], sc[:, k:k + 1]))
                    ins = pe.matmul(ps[:, SHIFT_BANKS[t // 4], t:t + 1], w, r, start=k == SHIFT_MACS and t % 4 == 0,
                                    stop=k is None and t % 4 == 3, skip_group_check=True)
                    if k is None and t % 4 == 3:
                        ins.then_inc(head_mm, 1)
            ffn(0)

            u = U_X
            pe.wait_ge(lo_done, u + 1)
            for th in range(2):
                for k in range(KD):
                    pe.wait_ge(n_lo_done, N_BASE[1] + KD * th + k + 1)
                    for j in (2 * th, 2 * th + 1):
                        ins = token_tile(u, ps[:, 1 + th, (j % 2) * XC:(j % 2 + 1) * XC], j, 0, XC, XC, [k], 0,
                                         k == 0 and j % 2 == 0, k == KD - 1)
                ins.then_inc(tiles, 1)
            for half in range(2):
                u = U_QD + half
                pe.wait_ge(lo_done, u + 1)
                for j in range(NB):
                    ins = token_tile(u, ps[:, 4 + j, :], j, 0, 512, 512, range(4 * half, 4 * half + 4), 4 * half,
                                     half == 0, half == 1)
                    if half or j == NB - 1:
                        ins.then_inc(tiles, 1)
            pe.wait_ge(kn_done, NB)
            for j in range(NB):
                ins = pe.transpose(ps[:, 3, j * P:(j + 1) * P], kn[:, j].rearrange("p a n -> p (a n)"), ident[:])
            ins.then_inc(kn_t, 1)
            pe.wait_ge(ki_tok, NB)
            for j in range(NB):
                ins = pe.transpose(ps[:, 2, j * P:(j + 1) * P], ki[:, j].rearrange("p a n -> p (a n)"), ident[:])
            ins.then_inc(ki_t, 1)

            def q_turn(j):
                pe.wait_ge(qn_done, j + 1)
                if j == 0:
                    pe.wait_ge(ki_lo_done, 1)
                if j == 1:
                    pe.wait_ge(kd_lo_done, 1)
                if j >= 2:
                    pe.wait_ge(qd_lo_done, 2 * (j - 1))
                for t in range(4):
                    ins = pe.transpose(ps[:, 2 + j % 2, t * P:(t + 1) * P], qn[:, j % 2, t * P:(t + 1) * P], ident[:])
                ins.then_inc(qn_t, 1)

            def qi_tile(t):
                u = U_QI + t // 2
                pe.wait_ge(lo_done, u + 1)
                if t >= 2:
                    pe.wait_ge(qi_lo_done, 2 * (t - 1))
                column_tile(u, t % 2, t % 2, n_hi, n_lo).then_inc(tiles, 1)

            qi_tile(0)
            qi_tile(1)
            q_turn(0)
            q_turn(1)
            qi_tile(2)
            qi_tile(3)
            q_turn(2)
            q_turn(3)

            for t in range(8):
                u = U_QSB + t // 2
                pe.wait_ge(lo_done, u + 1)
                if t == 0:
                    pe.wait_ge(qi_lo_done, 6)
                if t == 2:
                    pe.wait_ge(qd_lo_done, 2 * NB)
                if t >= 4:
                    pe.wait_ge(sbp_done, t - 3)
                column_tile(u, t % 4, t % 2, n_hi, n_lo).then_inc(tiles, 1)
                if t == 0:
                    pe.wait_ge(qi_lo_done, 8)
                for s in range(3 * t, 3 * t + 3):
                    i, hd = IDX[s]
                    n = (i + 1) * P
                    if s >= 4:
                        pe.wait_ge(relu_done, s - 3)
                    q = qi2[hd // 4][:, hd % 4, i * P:n]
                    pe.matmul(ps[:, 4 + s % 4, 0:n], q, ki_hi[:, 0:n], start=True, stop=False)
                    pe.matmul(ps[:, 4 + s % 4, 0:n], q, ki_lo[:, 0:n], start=False, stop=True).then_inc(idx_mm, 1)
            pe.wait_ge(ada_mac, 8 * GROUPS)
            pe.wait_ge(sbp_done, 8)
            for gr in range(REST):
                ins = pe.matmul(ps[0:REST, 3, :], pick[:, REST - 1 - gr:2 * REST - 1 - gr], ada_rest[:, gr, :],
                                start=gr == 0, stop=gr == REST - 1, skip_group_check=True)
            ins.then_inc(ada_mm, 1)
            pe.wait_ge(relu_done, len(IDX))
            for half in range(2):
                u = U_VSB + half
                pe.wait_ge(lo_done, u + 1)
                for j in range(NB):
                    ins = token_tile(u, ps[:, 4 + j, :], j, 0, 512, 512, range(4 * half, 4 * half + 4), 4 * half,
                                     half == 0, half == 1)
                    if half or j == NB - 1:
                        ins.then_inc(tiles, 1)
                if half == 0:
                    ada_turn(3, REST, 2)

            def logits(s):
                i, hd = divmod(s, NH)
                n = (i + 1) * P
                if s:
                    pe.wait_ge(ttr_done, s)
                pe.matmul(ps[:, B_LG, 0:n], qd2[i][:, hd, :], kd_hi[:, 0:n], start=True, stop=False)
                pe.matmul(ps[:, B_LG, 0:n], qd2[i][:, hd, :], kd_lo[:, 0:n], start=False, stop=True).then_inc(lg_done, 1)

            def turn(s):
                pe.wait_ge(p_done, s + 1)
                if s:
                    pe.wait_ge(pT_done, s)
                for b in range(s // NH + 1):
                    ins = pe.transpose(ps[:, B_PT, b * P:(b + 1) * P], lgb[:, s % 2, b * P:(b + 1) * P], ident[:])
                ins.then_inc(p_t, 1)

            def values(s):
                i, hd = divmod(s, NH)
                pe.wait_ge(pT_done, s + 1)
                if hd == 0 and i:
                    pe.wait_ge(ydn_done, i)
                for b in range(i + 1):
                    ins = pe.matmul(ps[:, B_O, hd * HD:(hd + 1) * HD], pT[:, s % 2, b * P:(b + 1) * P], vd[:, b, :],
                                    start=b == 0, stop=b == i, skip_group_check=True)
                ins.then_inc(pvd_done, 1)

            def sparse(s):
                if s >= 2:
                    values(s - 2)
                if 1 <= s <= NB * NH:
                    turn(s - 1)
                if s < NB * NH:
                    logits(s)

            def yd_turn(i, gate_tiles):
                pe.wait_ge(ydn_done, i + 1)
                pe.wait_ge(gate_done, gate_tiles)
                for t in range(4):
                    ins = pe.transpose(ps[:, B_F, t * P:(t + 1) * P], ydtok[:, t * P:(t + 1) * P], ident[:])
                ins.then_inc(yd_t, 1)

            def z_block(b, q0=0):
                return psf[:, BLK[b] + q0 * P:BLK[b] + S - b * P]

            pe.wait_ge(sbp_done, 8)
            for hd in range(NH):
                t, half = hd // 2, slice((hd % 2) * HD, (hd % 2 + 1) * HD)
                if hd:
                    pe.wait_ge(a_done, hd)
                for b in (0, 1, 3, 2):
                    pe.matmul(z_block(b), ksbT[half, t, b * P:(b + 1) * P], qsbT[half, t, b * P:S],
                              start=b != 3, stop=False, skip_group_check=True)
                for b in range(NB):
                    ins = pe.matmul(psf[:, BLK[b]:BLK[b] + P], ident_bf[:], strict_bf[:], start=False, stop=False,
                                    skip_group_check=True)
                ins.then_inc(z_done, 1)
                if hd == 0:
                    pe.wait_ge(vsb_done, NB)
                sparse(4 * hd)
                u = U_GATE + hd
                pe.wait_ge(lo_done, u + 1)
                if hd:
                    pe.wait_ge(gate_done, 2 * hd)
                column_tile(u, B_F, 0, n_hi, n_lo).then_inc(tiles, 1)
                sparse(4 * hd + 1)
                if hd == 0:
                    pe.wait_ge(round_done, 2)
                for b2 in (1, 3, 2, 0):
                    pe.wait_ge(sp_lo_done, 2 * hd + (2 if b2 == 0 else 1))
                    n = S - b2 * P
                    high = sp_hi0[:] if b2 == 0 else sp_hi1[:, BLK[b2] - S:BLK[b2] - S + n]
                    for b in range(b2 + 1):
                        w = (neg_tri_r if b2 == b else neg_ones_r)[:]
                        pe.matmul(z_block(b, b2 - b), w, high, start=False, stop=False, skip_group_check=True)
                        ins = pe.matmul(z_block(b, b2 - b), w, sp_lo[:, BLK[b2]:BLK[b2] + n], start=False,
                                        stop=b2 == 0, skip_group_check=True)
                ins.then_inc(suf_done, 1)
                if hd in (2, 4, 6):
                    yd_turn(hd // 2 - 1, 2 * hd + 1)
                sparse(4 * hd + 2)
                pe.wait_ge(gate_done, 2 * hd + 1)
                if hd in (2, 4, 6):
                    pe.wait_ge(ydT_done, hd // 2)
                column_tile(u, B_F, 1, n_hi, n_lo).then_inc(tiles, 1)
                sparse(4 * hd + 3)
                pe.wait_ge(a_done, hd + 1)
                if hd and hd % 2 == 0:
                    pe.wait_ge(ysb_lo_done, hd // 2)
                for b in range(NB):
                    ins = pe.matmul(ps[half, B_Y, b * P:S], vsb[:, b, hd * HD:(hd + 1) * HD],
                                    sp_a[:, BLK[b]:BLK[b] + S - b * P], start=b == 0, stop=b == NB - 1,
                                    skip_group_check=True)
                ins.then_inc(pv_done, 1)
            sparse(32)

            for n in range(4):
                u = U_PROJ + n
                if n == 1:
                    pe.wait_ge(yd_lo_done, 1)
                pe.wait_ge(lo_done, u + 1)
                for t in range(4):
                    if n >= 2:
                        pe.wait_ge((gy_done, gz_done)[n % 2], t + 1)
                    column_tile(u, 4 * (n % 2) + t, t, *((ysb_hi, ysb_lo), (yd_hi, yd_lo))[n % 2], width=512,
                                nk=4, step=(ysb_lo_done, 1) if n == 0 else None).then_inc(tiles, 1)
                    if n == 0 and t == 0:
                        sparse(33)
                    if n == 0 and t == 1:
                        yd_turn(3, 16)
            for n in range(3):
                u = U_OUT + n
                pe.wait_ge(lo_done, u + 1)
                for m in range(KD):
                    if n == 0:
                        pe.wait_ge(gy_done if m < 4 else gz_done, m + 5 if m < 4 else m + 1)
                    for k in range(2):
                        if m == 0:
                            pe.wait_ge(mg_lo_done, 2 * n + k + 1)
                        ins = row_tile(u, m, k, 2 * n + k, n_hi, n_lo, slice(0, S), n == 0 and k == 0, False)
                ins.then_inc(tiles, 1)
            pe.wait_ge(lo_done, U_FFN2)
            pe.wait_ge(mg_lo_done, KD)
            by_halves(U_FFN2 - 1, 2, KD - 2, n_hi, n_lo)
            ffn(1)


_INS = ["x", "c", "w_ada", "b_ada", "g_ffn1", "w1_ffn1", "w3_ffn1", "w2_ffn1", "g_mix", "w_in", "g_q_dsa", "g_k_dsa",
        "w_proj_sb", "w_proj_dsa", "w_gate", "b_gate", "w_out", "g_ffn2", "w1_ffn2", "w3_ffn2", "w2_ffn2"]


def kernel(**inputs):
    import numpy as np
    import concourse.bacc as bacc
    from concourse.bass_utils import run_bass_kernel_spmd

    nc = bacc.Bacc("TRN2", target_bir_lowering=False, num_devices=1)
    arrays, args = {}, []
    for name in _INS:
        a = np.ascontiguousarray(inputs[name])
        arrays[f"in_{name}"] = a
        args.append(nc.dram_tensor(f"in_{name}", a.shape, mybir.dt.from_np(a.dtype), kind="ExternalInput").ap())
    args.append(nc.dram_tensor("out", (1, S, D), F32, kind="ExternalOutput").ap())
    layer_kernel(nc, *args)
    r = run_bass_kernel_spmd(nc, [arrays], core_ids=[0])
    return r.results[0]["out"]
```
